# Optimizing a Trainium2 kernel written in Bass

```python
import jax
import jax.numpy as jnp
from jax import lax
import numpy as np
import math
import jax, jax.numpy as jnp

D_MODEL = 1024
BATCH = 1
SEQ = 256
DEPTH = 2

N_A_LAYERS = DEPTH // 2
N_B_LAYERS = DEPTH - N_A_LAYERS
HEAD_DIM = 64
N_HEADS_A = D_MODEL // HEAD_DIM
WIDTH_A = N_HEADS_A * HEAD_DIM
DECAY_LORA = 64
ICLR_LORA = 64
N_HEADS_B = D_MODEL // HEAD_DIM
WIDTH_B = N_HEADS_B * HEAD_DIM
MOBA_BLOCK = 256
MOBA_TOPK = 3
QUERY_CHUNK = 16
ROPE_THETA = 500000.0
ROPE_DIM = HEAD_DIM // 4
RMS_EPS = 1e-6
GN_EPS = 64e-5
NEG = -1e30


def rms_norm(x, g):
    xf = x.astype(jnp.float32)
    y = xf * lax.rsqrt(jnp.mean(xf * xf, axis=-1, keepdims=True) + RMS_EPS)
    return (y * g.astype(jnp.float32)).astype(x.dtype)

def rope_tables(T):
    inv_freq = jnp.power(jnp.float32(ROPE_THETA), -jnp.arange(0, ROPE_DIM, 2, dtype=jnp.float32) / ROPE_DIM)
    ang = jnp.arange(T, dtype=jnp.float32)[:, None] * inv_freq[None, :]
    return jnp.cos(ang), jnp.sin(ang)

def partial_rope(x, cos, sin):
    half = ROPE_DIM // 2
    xr = x[..., :ROPE_DIM].astype(jnp.float32)
    x1, x2 = xr[..., :half], xr[..., half:]
    rot = jnp.concatenate([x1 * cos - x2 * sin, x2 * cos + x1 * sin], axis=-1)
    return jnp.concatenate([rot.astype(x.dtype), x[..., ROPE_DIM:]], axis=-1)

def rwkv7_time_mix(h, mu, w_in, w0, w2, a0, a2, k_k, k_a, r_k, gn_w, gn_b, w_out):
    B, T, D = h.shape
    H, N = N_HEADS_A, HEAD_DIM
    xx = jnp.pad(h, ((0, 0), (1, 0), (0, 0)))[:, :-1] - h
    widths = (WIDTH_A, DECAY_LORA, WIDTH_A, WIDTH_A, ICLR_LORA, WIDTH_A)
    outs = []
    off = 0
    for i, wd in enumerate(widths):
        outs.append((h + xx * mu[i]) @ w_in[:, off:off + wd])
        off += wd
    r, wdn, k, v, adn, gp = [o.astype(jnp.float32) for o in outs]
    w = -jax.nn.softplus(-(w0 + jnp.tanh(wdn) @ w2)) - 0.5
    decay = jnp.exp(-jnp.exp(w))
    a = jax.nn.sigmoid(a0 + adn @ a2)
    kk = (k * k_k).reshape(B, T, H, N)
    kk = kk / jnp.maximum(jnp.linalg.norm(kk, axis=-1, keepdims=True), 1e-12)
    k = k * (1.0 + (a - 1.0) * k_a)

    def heads_tm(z):
        return z.reshape(B, T, H, N).transpose(1, 0, 2, 3)

    r4, d4, k4, v4 = heads_tm(r), heads_tm(decay), heads_tm(k), heads_tm(v)
    kk4 = heads_tm(kk)
    b4 = kk4 * heads_tm(a)

    def step(S, inp):
        r_t, d_t, k_t, v_t, kk_t, b_t = inp
        sa = jnp.einsum('bhvk,bhk->bhv', S, kk_t)
        S = S * d_t[:, :, None, :] - sa[..., None] * b_t[:, :, None, :] + v_t[..., None] * k_t[:, :, None, :]
        y = jnp.einsum('bhvk,bhk->bhv', S, r_t)
        return S, y

    S0 = jnp.zeros((B, H, N, N), jnp.float32)
    _, y = lax.scan(step, S0, (r4, d4, k4, v4, kk4, b4))
    y = y.transpose(1, 0, 2, 3)
    mean = jnp.mean(y, axis=-1, keepdims=True)
    var = jnp.mean(jnp.square(y - mean), axis=-1, keepdims=True)
    y = ((y - mean) * lax.rsqrt(var + GN_EPS)).reshape(B, T, D) * gn_w + gn_b
    bonus = jnp.sum(r.reshape(B, T, H, N) * k.reshape(B, T, H, N) * r_k, axis=-1, keepdims=True) * v.reshape(B, T, H, N)
    y = (y + bonus.reshape(B, T, D)) * jax.nn.silu(gp)
    return y.astype(h.dtype) @ w_out

def shared_kv(x, norm_kv, w_kv, k_norm, cos, sin):
    B, T, D = x.shape
    kv = rms_norm(x, norm_kv) @ w_kv
    k = kv[..., :WIDTH_B].reshape(B, T, N_HEADS_B, HEAD_DIM).transpose(0, 2, 1, 3)
    v = kv[..., WIDTH_B:].reshape(B, T, N_HEADS_B, HEAD_DIM).transpose(0, 2, 1, 3)
    k = partial_rope(rms_norm(k, k_norm), cos, sin)
    nb = -(-T // MOBA_BLOCK)
    pad = nb * MOBA_BLOCK - T
    k = jnp.pad(k, ((0, 0), (0, 0), (0, pad), (0, 0)))
    v = jnp.pad(v, ((0, 0), (0, 0), (0, pad), (0, 0)))
    kb = k.reshape(B, N_HEADS_B, nb, MOBA_BLOCK, HEAD_DIM)
    vb = v.reshape(B, N_HEADS_B, nb, MOBA_BLOCK, HEAD_DIM)
    kmean = jnp.mean(kb.astype(jnp.float32), axis=3)
    return kb, vb, kmean

def moba_attention(h, w_in, q_norm, w_out, kb, vb, kmean, cos, sin):
    B, T, D = h.shape
    H, hd, C, BS = N_HEADS_B, HEAD_DIM, QUERY_CHUNK, MOBA_BLOCK
    nb = kb.shape[2]
    topk = min(MOBA_TOPK, nb)
    scale = 1.0 / float(np.sqrt(hd))
    proj = h @ w_in
    q = proj[..., :WIDTH_B].reshape(B, T, H, hd).transpose(0, 2, 1, 3)
    gate = proj[..., WIDTH_B:]
    q = partial_rope(rms_norm(q, q_norm), cos, sin)
    nc = T // C
    qch = q.reshape(B, H, nc, C, hd).transpose(2, 0, 1, 3, 4)
    bi = jnp.arange(B)[:, None, None, None]
    hi = jnp.arange(H)[None, :, None, None]

    def chunk_fn(args):
        qc, ci = args
        cb = (ci * C) // BS
        qpos = ci * C + jnp.arange(C)
        gs = jnp.einsum('bhcd,bhnd->bhcn', qc.astype(jnp.float32), kmean)
        gs = jnp.where(jnp.arange(nb) < cb, gs, NEG)
        _, idx = lax.top_k(gs, topk)
        valid = idx < cb
        ksel = kb[bi, hi, idx]
        vsel = vb[bi, hi, idx]
        s_sel = jnp.einsum('bhcd,bhcjsd->bhcjs', qc, ksel).astype(jnp.float32) * scale
        s_sel = jnp.where(valid[..., None], s_sel, NEG).reshape(B, H, C, topk * BS)
        kown = lax.dynamic_index_in_dim(kb, cb, axis=2, keepdims=False)
        vown = lax.dynamic_index_in_dim(vb, cb, axis=2, keepdims=False)
        s_own = jnp.einsum('bhcd,bhsd->bhcs', qc, kown).astype(jnp.float32) * scale
        kpos = cb * BS + jnp.arange(BS)
        s_own = jnp.where(kpos[None, :] <= qpos[:, None], s_own, NEG)
        p = jax.nn.softmax(jnp.concatenate([s_sel, s_own], axis=-1), axis=-1)
        p_sel = p[..., :topk * BS].reshape(B, H, C, topk, BS).astype(vb.dtype)
        p_own = p[..., topk * BS:].astype(vb.dtype)
        return jnp.einsum('bhcjs,bhcjsd->bhcd', p_sel, vsel) + jnp.einsum('bhcs,bhsd->bhcd', p_own, vown)

    o = lax.map(chunk_fn, (qch, jnp.arange(nc)))
    o = o.transpose(1, 0, 3, 2, 4).reshape(B, T, WIDTH_B)
    return (o * jax.nn.silu(gate)) @ w_out

def first_inputs(seed: int = 0) -> dict:
    key = jax.random.key(seed)
    ks = jax.random.split(key, 24)
    D, NA, NB_ = D_MODEL, N_A_LAYERS, N_B_LAYERS
    in_a = 4 * WIDTH_A + DECAY_LORA + ICLR_LORA
    nrm = jax.random.normal
    return {
        "x": nrm(ks[0], (BATCH, SEQ, D), jnp.float32),
        "norm_a": 1.0 + 0.02 * nrm(ks[1], (NA, D), jnp.float32),
        "mu_a": jax.random.uniform(ks[2], (NA, 6, D), jnp.float32),
        "w_in_a": nrm(ks[3], (NA, D, in_a), jnp.float32) * D ** -0.5,
        "w0_a": jax.random.uniform(ks[4], (NA, D), jnp.float32, -5.0, 0.0),
        "w2_a": nrm(ks[5], (NA, DECAY_LORA, D), jnp.float32) * 0.5 * DECAY_LORA ** -0.5,
        "a0_a": 0.1 * nrm(ks[6], (NA, D), jnp.float32),
        "a2_a": nrm(ks[7], (NA, ICLR_LORA, D), jnp.float32) * 0.5 * ICLR_LORA ** -0.5,
        "kk_a": 0.85 + 0.05 * nrm(ks[8], (NA, D), jnp.float32),
        "ka_a": 1.0 + 0.05 * nrm(ks[9], (NA, D), jnp.float32),
        "rk_a": 0.1 * nrm(ks[10], (NA, N_HEADS_A, HEAD_DIM), jnp.float32),
        "gn_w_a": 1.0 + 0.02 * nrm(ks[11], (NA, D), jnp.float32),
        "gn_b_a": 0.02 * nrm(ks[12], (NA, D), jnp.float32),
        "w_out_a": nrm(ks[13], (NA, WIDTH_A, D), jnp.float32) * WIDTH_A ** -0.5,
        "norm_kv": 1.0 + 0.02 * nrm(ks[14], (D,), jnp.float32),
        "w_kv": nrm(ks[15], (D, 2 * WIDTH_B), jnp.float32) * D ** -0.5,
        "k_norm": 1.0 + 0.02 * nrm(ks[16], (HEAD_DIM,), jnp.float32),
        "norm_b": 1.0 + 0.02 * nrm(ks[17], (NB_, D), jnp.float32),
        "w_in_b": nrm(ks[18], (NB_, D, 2 * WIDTH_B), jnp.float32) * D ** -0.5,
        "q_norm_b": 1.0 + 0.02 * nrm(ks[19], (NB_, HEAD_DIM), jnp.float32),
        "w_out_b": nrm(ks[20], (NB_, WIDTH_B, D), jnp.float32) * WIDTH_B ** -0.5,
    }

def first_block(x, norm_a, mu_a, w_in_a, w0_a, w2_a, a0_a, a2_a, kk_a, ka_a, rk_a, gn_w_a, gn_b_a, w_out_a,
              norm_kv, w_kv, k_norm, norm_b, w_in_b, q_norm_b, w_out_b):
    T = x.shape[1]
    cos, sin = rope_tables(T)
    kb = vb = kmean = None
    for layer in range(DEPTH):
        if layer < N_A_LAYERS:
            i = layer
            x = x + rwkv7_time_mix(rms_norm(x, norm_a[i]), mu_a[i], w_in_a[i], w0_a[i], w2_a[i], a0_a[i], a2_a[i],
                                   kk_a[i], ka_a[i], rk_a[i], gn_w_a[i], gn_b_a[i], w_out_a[i])
        else:
            if layer == N_A_LAYERS:
                kb, vb, kmean = shared_kv(x, norm_kv, w_kv, k_norm, cos, sin)
            j = layer - N_A_LAYERS
            x = x + moba_attention(rms_norm(x, norm_b[j]), w_in_b[j], q_norm_b[j], w_out_b[j], kb, vb, kmean, cos, sin)
    return x


N_A = DEPTH // 2
N_B = DEPTH - N_A

A_HEADS = 8
A_QK_DIM = D_MODEL // 2 // A_HEADS
A_V_DIM = D_MODEL // A_HEADS
A_QK_W = A_HEADS * A_QK_DIM
A_V_W = A_HEADS * A_V_DIM
A_IN_WIDTH = 2 * A_QK_W + A_V_W + 2 * A_HEADS + A_V_W
A_CHUNK = 128

B_HEADS = 8
B_Q_LORA = 384
B_KV_LORA = 256
B_NOPE = 128
B_ROPE = 64
B_V = 128
B_QBLOCK = 128
ROPE_THETA_2 = 10000.0

D_FF = 4 * D_MODEL
EPS = 1e-6


def rmsnorm(x, g):
    xf = x.astype(jnp.float32)
    y = xf * lax.rsqrt(jnp.mean(xf * xf, axis=-1, keepdims=True) + EPS)
    return (y * g.astype(jnp.float32)).astype(x.dtype)

def modulate(h, shift, scale):
    return h * (1 + scale[:, None, :]) + shift[:, None, :]

def rope_tables_2(positions):
    half = B_ROPE // 2
    inv = ROPE_THETA_2 ** (-jnp.arange(half, dtype=jnp.float32) / half)
    ang = positions.astype(jnp.float32)[..., None] * inv
    return jnp.cos(ang), jnp.sin(ang)

def apply_rope(x, cos, sin):
    xf = x.astype(jnp.float32)
    x1, x2 = jnp.split(xf, 2, axis=-1)
    out = jnp.concatenate([x1 * cos - x2 * sin, x2 * cos + x1 * sin], axis=-1)
    return out.astype(x.dtype)

def mlstm_chunkwise(q, k, v, i_pre, f_pre):
    B_, H, S, dk = q.shape
    dv = v.shape[-1]
    L = A_CHUNK
    nc = S // L
    f32 = jnp.float32
    qf = q.astype(f32)
    kf = k.astype(f32) * (dk ** -0.5)
    vf = v.astype(f32)
    lf = jax.nn.log_sigmoid(f_pre.astype(f32))
    ig = i_pre.astype(f32)

    def chunks(a):
        return jnp.moveaxis(a.reshape(B_, H, nc, L, *a.shape[3:]), 2, 0)

    qc, kc, vc, ic = chunks(qf), chunks(kf), chunks(vf), chunks(ig)
    bc = jnp.cumsum(chunks(lf), axis=-1)
    tri = jnp.tril(jnp.ones((L, L), dtype=bool))

    def step(carry, xs):
        C, n, m = carry
        qb, kb, vb, ib, bb = xs
        log_d = bb[..., :, None] - bb[..., None, :] + ib[..., None, :]
        log_d = jnp.where(tri, log_d, -jnp.inf)
        log_inter = bb + m[..., None]
        m_t = jnp.maximum(log_inter, jnp.max(log_d, axis=-1))
        w_intra = jnp.exp(log_d - m_t[..., None])
        w_inter = jnp.exp(log_inter - m_t)
        s = jnp.einsum('bhtd,bhsd->bhts', qb, kb) * w_intra
        num = (w_inter[..., None] * jnp.einsum('bhtd,bhde->bhte', qb, C)
               + jnp.einsum('bhts,bhse->bhte', s, vb))
        den = w_inter * jnp.einsum('bhtd,bhd->bht', qb, n) + jnp.sum(s, axis=-1)
        h = num / jnp.maximum(jnp.abs(den), jnp.exp(-m_t))[..., None]
        b_last = bb[..., -1]
        log_w = b_last[..., None] - bb + ib
        m_new = jnp.maximum(b_last + m, jnp.max(log_w, axis=-1))
        w = jnp.exp(log_w - m_new[..., None])
        decay = jnp.exp(b_last + m - m_new)
        C_new = decay[..., None, None] * C + jnp.einsum('bhs,bhsd,bhse->bhde', w, kb, vb)
        n_new = decay[..., None] * n + jnp.einsum('bhs,bhsd->bhd', w, kb)
        return (C_new, n_new, m_new), h

    init = (jnp.zeros((B_, H, dk, dv), f32), jnp.zeros((B_, H, dk), f32), jnp.zeros((B_, H), f32))
    _, hc = lax.scan(step, init, (qc, kc, vc, ic, bc))
    return jnp.moveaxis(hc, 0, 2).reshape(B_, H, S, dv).astype(q.dtype)

def mlstm_mixer(h, w_in, gate_b, head_g, w_out):
    B_, S, _ = h.shape
    proj = h @ w_in
    splits = [A_QK_W, 2 * A_QK_W, 2 * A_QK_W + A_V_W, 2 * A_QK_W + A_V_W + A_HEADS,
              2 * A_QK_W + A_V_W + 2 * A_HEADS]
    q, k, v, ig, fg, og = jnp.split(proj, splits, axis=-1)
    heads = lambda a, d: a.reshape(B_, S, A_HEADS, d).transpose(0, 2, 1, 3)
    i_pre = (ig + gate_b[0]).transpose(0, 2, 1)
    f_pre = (fg + gate_b[1]).transpose(0, 2, 1)
    hh = mlstm_chunkwise(heads(q, A_QK_DIM), heads(k, A_QK_DIM), heads(v, A_V_DIM), i_pre, f_pre)
    hh = rmsnorm(hh.transpose(0, 2, 1, 3), head_g).reshape(B_, S, A_V_W)
    return (hh * jax.nn.sigmoid(og)) @ w_out

def mla_shared_kv(x, shift, scale, g_in, w_a, g_latent, w_b, cos, sin):
    B_, S, _ = x.shape
    h = modulate(rmsnorm(x, g_in), shift, scale)
    kv = h @ w_a
    c_kv, k_rope = jnp.split(kv, [B_KV_LORA], axis=-1)
    c_kv = rmsnorm(c_kv, g_latent)
    kvb = (c_kv @ w_b).reshape(B_, S, B_HEADS, B_NOPE + B_V)
    k_nope, v = jnp.split(kvb, [B_NOPE], axis=-1)
    k_rope = apply_rope(k_rope, cos, sin)
    return k_nope, k_rope, v

def causal_mla_attention(q_nope, q_rope, k_nope, k_rope, v):
    B_, S, H, _ = q_nope.shape
    nb = S // B_QBLOCK
    scale = (B_NOPE + B_ROPE) ** -0.5
    qn = jnp.moveaxis(q_nope.reshape(B_, nb, B_QBLOCK, H, B_NOPE), 1, 0)
    qr = jnp.moveaxis(q_rope.reshape(B_, nb, B_QBLOCK, H, B_ROPE), 1, 0)
    kpos = jnp.arange(S, dtype=jnp.int32)
    starts = jnp.arange(nb, dtype=jnp.int32) * B_QBLOCK

    def block(args):
        qn_b, qr_b, start = args
        s = (jnp.einsum('bqhd,bkhd->bhqk', qn_b, k_nope)
             + jnp.einsum('bqhd,bkd->bhqk', qr_b, k_rope)).astype(jnp.float32) * scale
        qpos = start + jnp.arange(B_QBLOCK, dtype=jnp.int32)
        s = jnp.where(kpos[None, :] <= qpos[:, None], s, -jnp.inf)
        p = jax.nn.softmax(s, axis=-1)
        return jnp.einsum('bhqk,bkhd->bqhd', p.astype(v.dtype), v)

    o = lax.map(block, (qn, qr, starts))
    return jnp.moveaxis(o, 0, 1).reshape(B_, S, H, B_V)

def mla_mixer(h, w_q_a, g_q_latent, w_q_b, w_out, k_nope, k_rope, v, cos, sin):
    B_, S, _ = h.shape
    cq = rmsnorm(h @ w_q_a, g_q_latent)
    q = (cq @ w_q_b).reshape(B_, S, B_HEADS, B_NOPE + B_ROPE)
    q_nope, q_rope = jnp.split(q, [B_NOPE], axis=-1)
    q_rope = apply_rope(q_rope, cos[:, :, None, :], sin[:, :, None, :])
    o = causal_mla_attention(q_nope, q_rope, k_nope, k_rope, v)
    return o.reshape(B_, S, B_HEADS * B_V) @ w_out

def sqrelu_mlp(h, w1, w2):
    return jnp.square(jax.nn.relu(h @ w1)) @ w2

def second_inputs(seed: int = 0) -> dict:
    key = jax.random.key(seed)
    ks = jax.random.split(key, 24)
    f32 = jnp.float32

    def nrm(k, shape, fan_in, s=1.0):
        return s * (fan_in ** -0.5) * jax.random.normal(k, shape, f32)

    def gain(k, shape):
        return 1.0 + 0.02 * jax.random.normal(k, shape, f32)

    x = jax.random.normal(ks[0], (BATCH, SEQ, D_MODEL), f32)
    c = jax.random.normal(ks[1], (BATCH, D_MODEL), f32)
    positions = (jax.random.randint(ks[2], (BATCH, 1), 0, 4096, dtype=jnp.int32)
                 + jnp.arange(SEQ, dtype=jnp.int32)[None, :])
    ada_w = nrm(ks[3], (DEPTH, D_MODEL, 6 * D_MODEL), D_MODEL, 0.5)
    ada_b = 0.02 * jax.random.normal(ks[4], (DEPTH, 6 * D_MODEL), f32)
    norm_g = gain(ks[5], (DEPTH, 4, D_MODEL))
    a_w_in = nrm(ks[6], (N_A, D_MODEL, A_IN_WIDTH), D_MODEL)
    kg1, kg2 = jax.random.split(ks[7])
    i_bias = 0.1 * jax.random.normal(kg1, (N_A, A_HEADS), f32)
    f_bias = jnp.linspace(3.0, 6.0, A_HEADS, dtype=f32)[None, :] + 0.1 * jax.random.normal(kg2, (N_A, A_HEADS), f32)
    a_gate_b = jnp.stack([i_bias, f_bias], axis=1)
    a_head_g = gain(ks[8], (N_A, A_HEADS, A_V_DIM))
    a_w_out = nrm(ks[9], (N_A, A_V_W, D_MODEL), A_V_W)
    kv_ada_w = nrm(ks[10], (D_MODEL, 2 * D_MODEL), D_MODEL, 0.5)
    kv_ada_b = 0.02 * jax.random.normal(ks[11], (2 * D_MODEL,), f32)
    kv_norm_g = gain(ks[12], (D_MODEL,))
    kv_w_a = nrm(ks[13], (D_MODEL, B_KV_LORA + B_ROPE), D_MODEL)
    kv_latent_g = gain(ks[14], (B_KV_LORA,))
    kv_w_b = nrm(ks[15], (B_KV_LORA, B_HEADS * (B_NOPE + B_V)), B_KV_LORA)
    b_w_q_a = nrm(ks[16], (N_B, D_MODEL, B_Q_LORA), D_MODEL)
    b_q_latent_g = gain(ks[17], (N_B, B_Q_LORA))
    b_w_q_b = nrm(ks[18], (N_B, B_Q_LORA, B_HEADS * (B_NOPE + B_ROPE)), B_Q_LORA)
    b_w_out = nrm(ks[19], (N_B, B_HEADS * B_V, D_MODEL), B_HEADS * B_V)
    mlp_w1 = nrm(ks[20], (DEPTH, D_MODEL, D_FF), D_MODEL)
    mlp_w2 = nrm(ks[21], (DEPTH, D_FF, D_MODEL), D_FF)
    return {"x": x, "c": c, "positions": positions, "ada_w": ada_w, "ada_b": ada_b,
            "norm_g": norm_g, "a_w_in": a_w_in, "a_gate_b": a_gate_b, "a_head_g": a_head_g,
            "a_w_out": a_w_out, "kv_ada_w": kv_ada_w, "kv_ada_b": kv_ada_b, "kv_norm_g": kv_norm_g,
            "kv_w_a": kv_w_a, "kv_latent_g": kv_latent_g, "kv_w_b": kv_w_b, "b_w_q_a": b_w_q_a,
            "b_q_latent_g": b_q_latent_g, "b_w_q_b": b_w_q_b, "b_w_out": b_w_out,
            "mlp_w1": mlp_w1, "mlp_w2": mlp_w2}

def second_block(x, c, positions, ada_w, ada_b, norm_g, a_w_in, a_gate_b, a_head_g, a_w_out,
              kv_ada_w, kv_ada_b, kv_norm_g, kv_w_a, kv_latent_g, kv_w_b, b_w_q_a, b_q_latent_g,
              b_w_q_b, b_w_out, mlp_w1, mlp_w2):
    cond = jax.nn.silu(c)
    cos, sin = rope_tables_2(positions)
    shared_kv = None
    for l in range(DEPTH):
        ada = cond @ ada_w[l] + ada_b[l]
        sh1, sc1, g1, sh2, sc2, g2 = jnp.split(ada, 6, axis=-1)
        h = modulate(rmsnorm(x, norm_g[l, 0]), sh1, sc1)
        if l < N_A:
            y = mlstm_mixer(h, a_w_in[l], a_gate_b[l], a_head_g[l], a_w_out[l])
        else:
            if shared_kv is None:
                kv_shift, kv_scale = jnp.split(cond @ kv_ada_w + kv_ada_b, 2, axis=-1)
                shared_kv = mla_shared_kv(x, kv_shift, kv_scale, kv_norm_g, kv_w_a, kv_latent_g,
                                          kv_w_b, cos, sin)
            k_nope, k_rope, v = shared_kv
            j = l - N_A
            y = mla_mixer(h, b_w_q_a[j], b_q_latent_g[j], b_w_q_b[j], b_w_out[j],
                          k_nope, k_rope, v, cos, sin)
        x = x + g1[:, None, :] * rmsnorm(y, norm_g[l, 1])
        h = modulate(rmsnorm(x, norm_g[l, 2]), sh2, sc2)
        y = sqrelu_mlp(h, mlp_w1[l], mlp_w2[l])
        x = x + g2[:, None, :] * rmsnorm(y, norm_g[l, 3])
    return x


def setup_inputs(seed=0):
    out = dict(first_inputs(seed))
    for name, value in second_inputs(seed + 1).items():
        if name != "x":
            out[name + "_2"] = value
    return out


def reference(
    x, norm_a, mu_a, w_in_a, w0_a, w2_a, a0_a, a2_a, kk_a, ka_a, rk_a, gn_w_a, gn_b_a, w_out_a,
    norm_kv, w_kv, k_norm, norm_b, w_in_b, q_norm_b, w_out_b, c_2, positions_2, ada_w_2,
    ada_b_2, norm_g_2, a_w_in_2, a_gate_b_2, a_head_g_2, a_w_out_2, kv_ada_w_2, kv_ada_b_2,
    kv_norm_g_2, kv_w_a_2, kv_latent_g_2, kv_w_b_2, b_w_q_a_2, b_q_latent_g_2, b_w_q_b_2,
    b_w_out_2, mlp_w1_2, mlp_w2_2,
):
    x = first_block(
        x, norm_a, mu_a, w_in_a, w0_a, w2_a, a0_a, a2_a, kk_a, ka_a, rk_a, gn_w_a, gn_b_a,
        w_out_a, norm_kv, w_kv, k_norm, norm_b, w_in_b, q_norm_b, w_out_b,
    )
    return second_block(
        x, c_2, positions_2, ada_w_2, ada_b_2, norm_g_2, a_w_in_2, a_gate_b_2, a_head_g_2,
        a_w_out_2, kv_ada_w_2, kv_ada_b_2, kv_norm_g_2, kv_w_a_2, kv_latent_g_2, kv_w_b_2,
        b_w_q_a_2, b_q_latent_g_2, b_w_q_b_2, b_w_out_2, mlp_w1_2, mlp_w2_2,
    )


_drawn_inputs = setup_inputs


def setup_inputs(seed=0):
    import zlib

    import numpy as np

    out = dict(_drawn_inputs(seed))
    spreads = {}
    factors = {'w2_a': 3.931,
     'kk_a': 4.043,
     'gn_w_a': 5.966,
     'gn_b_a': 5.769,
     'norm_kv': 8.0,
     'k_norm': 8.0,
     'norm_b': 8.0,
     'q_norm_b': 8.0,
     'norm_g_2': 26.536,
     'a_head_g_2': 64.0,
     'kv_ada_b_2': 29.715,
     'kv_norm_g_2': 64.0,
     'kv_latent_g_2': 64.0,
     'b_q_latent_g_2': 64.0,
     'ada_b_2': 8.0,
     'a_gate_b_2': 3.774,
     'kv_ada_w_2': 3.49}
    for name, (base, spread) in spreads.items():
        noise = np.random.default_rng([zlib.crc32(name.encode()), seed]).standard_normal(out[name].shape)
        drawn = base * np.exp(spread * noise) if base else spread * noise
        out[name] = jnp.asarray(drawn.astype(out[name].dtype))
    for name, factor in factors.items():
        out[name] = (out[name] * factor).astype(out[name].dtype)
    return out
```

```python
from contextlib import ExitStack

import concourse.bass as bass
import numpy as np
from concourse import mybir

F32 = mybir.dt.float32
I32 = mybir.dt.int32
ALU = mybir.AluOpType
ACT = mybir.ActivationFunctionType
AX = mybir.AxisListType

P = 128
D = 1024
KT = D // P
T = 256
TB = T // P
HD = 64
NH = D // HD
LC = 64
NC_ = T // LC
EPS = 1e-6
GN_EPS = 64e-5
KAPPA = float(np.exp(-0.5))
NEG = -1e30
MH = 8
DKM = 64
DV = 128
KVL = 256
QL = 384
RD = 64
FF = 4 * D
SLOT = 4096
SLOTS = 4
ADA_PANELS = 28
MLA_SCALE = float((DV + RD) ** -0.5)
TWO_PI = 2.0 * np.pi
C1 = 6.28125
C2 = float(np.float32(np.round((TWO_PI - C1) * 2.0 ** 21) / 2.0 ** 21))
C3 = float(np.float32(TWO_PI - C1 - C2))
MAGIC = 12582912.0
PI_CLAMP = 3.1415925


def columns(*widths):
    at, out = 0, {}
    for name, w in widths:
        out[name] = (at, w)
        at += w
    return out, at


CONST, NCONST = columns(("ident", P), ("ones", P), ("pair_ones", P), ("pair_sel", 2), ("eye", LC),
                        ("level", 6 * LC), ("strict_incl", 2 * LC), ("scan_reset", T),
                        ("rope1", 2 * TB * 8), ("causal", 3 * P), ("late", P),
                        ("inv2", 32), ("zero", 1))
PARAM, NPARAM = columns(("norm_a", 8), ("mu", 48), ("w0", 8), ("a0", 8), ("kk", 8), ("ka", 8), ("rk", 8),
                        ("norm_kv", 8), ("norm_b", 8), ("cond", 8), ("ada_b", 112), ("norm2", 64),
                        ("kv_norm2", 8), ("kv_latent", 2), ("q_latent", 3), ("head_g", 8),
                        ("gate_w", 128), ("gate_b", 2), ("k_norm", HD), ("q_norm", HD))


def constants():
    out = np.zeros((P, NCONST), np.float32)

    def put(name, a):
        at, w = CONST[name]
        a = np.asarray(a, np.float32).reshape(a.shape[0], -1)
        out[:a.shape[0], at:at + w] = a

    p = np.arange(P)
    put("ident", np.eye(P))
    put("ones", np.ones((P, P)))
    put("pair_ones", (p[:, None] // HD == p[None, :] // HD) * 1.0)
    put("pair_sel", (p[:, None] // HD == np.arange(2)) * 1.0)
    s, t = (p % LC)[:, None], np.arange(LC)[None, :]
    put("eye", (s == t) * 1.0)
    put("level", np.stack([((s >> (l + 1)) == (t >> (l + 1))) & ((s >> l) % 2 == 0) & ((t >> l) % 2 == 1)
                           for l in range(6)], 1) * 1.0)
    put("strict_incl", np.stack([s < t, s <= t], 1) * 1.0)
    put("scan_reset", np.broadcast_to((np.arange(T) % LC != 0) * 1.0, (P, T)))
    inv = np.power(np.float32(500000.0), -np.arange(0, 16, 2, dtype=np.float32) / np.float32(16))
    ang = (np.arange(T, dtype=np.float32)[:, None] * inv[None, :]).astype(np.float64)
    tab = np.stack([np.cos(ang), np.sin(ang)]).reshape(2, TB, P, 8).transpose(2, 0, 1, 3)
    put("rope1", np.ascontiguousarray(tab))
    diag = np.where(p[None, :] <= p[:, None], 0.0, NEG)
    put("causal", np.concatenate([diag, np.zeros((P, P)), diag], 1))
    put("late", np.where(p[:, None] <= p[None, :], 0.0, -NEG))
    inv2 = np.power(np.float32(10000.0), -np.arange(32, dtype=np.float32) / np.float32(32))
    put("inv2", np.broadcast_to(inv2, (P, 32)))
    return out


def build(nc, x, cc_d, pc_d, pos_d, gn_d, sel_d, stream, out, debug=None):
    order = []
    with ExitStack() as ctx:
        def sb(name, shape, dt=F32):
            return ctx.enter_context(nc.sbuf_tensor(name, shape, dt))

        sems = {}

        def sem(name):
            if name not in sems:
                sems[name] = ctx.enter_context(nc.semaphore(name))
            return sems[name]

        banks = [ctx.enter_context(nc.psum_tensor(f"bank{b}", [P, 512], F32)) for b in range(8)]
        ring = sb("ring", [P, SLOTS, SLOT])
        arena = sb("arena", [P, 15, 2048])
        cc = sb("cc", [P, NCONST])
        pc = sb("pc", [P, NPARAM])
        gn = sb("gn", [P, 2, D])
        small = sb("small", [P, 1352])
        pos_i = sb("pos_i", [P, TB], I32)

        def con(name):
            at, w = CONST[name]
            return cc[:, at:at + w]

        def par(name):
            at, w = PARAM[name]
            return pc[:, at:at + w]

        ident, ones = con("ident"), con("ones")

        def page(n, d0):
            return arena[:, n, :].rearrange("p (a b) -> p a b", a=d0)

        used = [0]

        def scratch(w):
            used[0] += w
            assert used[0] <= 1352
            return small[:, used[0] - w:used[0]]

        X = page(0, TB)
        XN = page(13, TB)

        counts = {}

        class Count:

            def __init__(self, own):
                self.own, self.last = own, None

            def step(self, name=None):
                s = sem(name or self.own)
                counts[s.name] = counts.get(s.name, 0) + 1
                self.last = (s, counts[s.name])
                return s

            def frees(self, product):
                self.last = evacuated(product)
                return self.last[0]

        def finished(product):
            b, turn = place[product]
            return sem(f"bank_full{b}"), turn + 1

        def evacuated(product):
            b, turn = place[product]
            return sem(f"bank_free{b}"), turn + 1

        place, turns, rotation = {}, {}, {"banks": list(range(8)), "at": 0}
        ada_slots = []

        def bank(product):
            return banks[place[product][0]]

        Vr, Gr = page(1, TB), page(2, TB)
        AR = arena[:, 3:5, :].rearrange("p g b -> p (g b)").rearrange("p (j c a t) -> p j c a t", j=KT, c=NC_, a=2)
        khat, bhat, xx, hT = page(5, KT), page(6, KT), page(7, KT), page(8, KT)
        mix = [page(9, KT), page(10, KT)]
        LW, AA, KK, EE = page(11, KT), page(12, KT), page(13, KT), page(14, KT)
        EN, bonus_p = page(8, KT), page(9, KT)
        Kt, Bt = page(7, TB), page(10, TB)
        PK = arena[:, 11:13, :].rearrange("p g b -> p (g b)").rearrange("p (b h j a t) -> p b h j a t", b=TB, h=2, j=8, a=2)
        PB = arena[:, 8:10, :].rearrange("p g b -> p (g b)").rearrange("p (b h j a t) -> p b h j a t", b=TB, h=2, j=8, a=2)
        TI = page(13, 4).rearrange("p g (j t) -> p g j t", j=8)
        TTI = page(5, 4).rearrange("p g (j t) -> p g j t", j=8)
        XS = page(6, 4).rearrange("p g (j t) -> p g j t", j=8)
        CT = page(14, 4).rearrange("p g (j t) -> p g j t", j=8)
        SBD = arena[:, 6, 0:1024].rearrange("p (j v) -> p j v", j=8)
        Rs, Un = page(14, 2)[:, 0, :], page(14, 2)[:, 1, :]
        Yr = page(13, TB)
        YT = page(8, KT)
        ada_part = scratch(1024).rearrange("p (a n) -> p a n", a=2)
        lora = ada_part[:, 0, :].rearrange("p (a t) -> p a t", a=2)
        g_scan = ada_part[:, 1, 0:T]
        F = scratch(32).rearrange("p (j c) -> p j c", j=8)
        bonus = scratch(32).rearrange("p (b h) -> p b h", b=TB)
        one_m_ka = scratch(8)
        ss = scratch(2)
        stat = scratch(32).rearrange("p (b h) -> p b h", b=TB)
        stat2 = scratch(32).rearrange("p (b h) -> p b h", b=TB)
        cond = scratch(8)
        rs = scratch(32).rearrange("p (h b) -> p h b", b=TB)
        mx = scratch(4)
        rope2 = sb("rope2", [P, 2, TB, 32])
        ADA = sb("ADA", [P, 4 * ADA_PANELS])
        MOD = sb("MOD", [P, 5, 8])
        n2 = par("norm2")
        MOD_FROM = ((8, n2[:, 0:8]), (32, n2[:, 16:24]), (56, par("kv_norm2")), (72, n2[:, 32:40]), (96, n2[:, 48:56]))
        MODS = [(MOD[:, m, :], ADA[:, at:at + 8]) for m, at in enumerate((0, 24, 48, 64, 88))]
        GATE_FROM = ((16, n2[:, 8:16]), (40, n2[:, 24:32]), (80, n2[:, 40:48]), (104, n2[:, 56:64]))
        nmax = scratch(32).rearrange("p (h b) -> p h b", b=TB)
        gcol = scratch(8)
        den = scratch(2).rearrange("p (b o) -> p b o", b=TB)
        gcols = scratch(32).rearrange("p (b n) -> p b n", b=TB)
        mid = lora
        newton = scratch(64).rearrange("p (a n) -> p a n", a=2)
        GNT = page(6, 2)[:, 1:2, :]
        hkvT, hbT, K1, V1, Q1, G1 = page(7, KT), page(8, KT), page(3, TB), page(1, TB), page(4, TB), page(2, TB)
        K1T, Q1T, O1, O1T = page(9, KT), page(10, KT), page(6, TB), page(11, KT)

        def cols(n, a, b):
            return arena[:, n, a:b]

        Ss = cols(12, 0, 768).rearrange("p (a n) -> p a n", a=2)
        Ps = cols(12, 768, 1536).rearrange("p (a n) -> p a n", a=2)
        PTs = cols(14, 0, 768).rearrange("p (a n) -> p a n", a=2)
        hT2 = page(8, KT)
        Q2T = cols(9, 0, 1024).rearrange("p (j t) -> p j t", j=4)
        K2T = cols(10, 0, 1024).rearrange("p (j t) -> p j t", j=4)
        V2 = arena[:, 3:5, :].rearrange("p g b -> p (g b)")[:, 0:TB * MH * (DV + 1)].rearrange(
            "p (b h d) -> p b h d", b=TB, h=MH)
        H2, H2T, Yb, GB = page(6, TB), page(11, KT), page(7, TB), page(1, TB)
        i_row, f_row, t_row, b_row, c_row, m_row, mt_row, em_row = (cols(12, n * T, (n + 1) * T) for n in range(8))
        ones_row = cols(9, 1024, 1024 + T)
        W2 = cols(14, 0, 768).rearrange("p (a n) -> p a n", a=2)
        PT2 = cols(14, 768, 1536).rearrange("p (a n) -> p a n", a=2)
        head_sel = gn[0:8, 0, :]
        DIAGF = gn[:, 1, :]
        DIAG = DIAGF.rearrange("p (j n) -> p j n", j=8)
        AF = page(9, 2).rearrange("p a (k t) -> p a k t", k=4)
        RL = page(10, 2).rearrange("p a (k t) -> p a k t", k=4)
        hkvT2 = page(12, KT)
        CKVR = cols(9, 0, 640).rearrange("p (b n) -> p b n", b=TB)
        CKV = cols(9, 640, 1152).rearrange("p (b n) -> p b n", b=TB)
        CKVT = cols(9, 1152, 1664).rearrange("p (j t) -> p j t", j=2)
        KR = cols(9, 1664, 1920).rearrange("p (b n) -> p b n", b=TB)
        CQ = cols(10, 0, 768).rearrange("p (b n) -> p b n", b=TB)
        CQT = cols(10, 768, 1536).rearrange("p (j t) -> p j t", j=3)
        KRT = cols(10, 1536, 1792)
        KNT, V3, QNT, O3, O3T = page(5, KT), page(3, TB), page(4, KT), page(6, TB), page(11, KT)
        QR = cols(2, 0, 1024).rearrange("p (b n) -> p b n", b=TB)
        QRT = cols(2, 1024, 2048).rearrange("p (j t) -> p j t", j=4)

        def pv_done(name, per, h):
            if h % per == per - 1:
                return finished((name, "O", h // per))
            return sem(name + "_pv"), h // per * (per - 1) + h % per + 1

        block = ctx.enter_context(nc.Block())

        @block.tensor
        def _(pe):
            pn = Count("pe_steps")
            mm = nc.tensor.matmul
            panels = [0]

            def claim(product, banks_from=None):
                if banks_from is None:
                    b = rotation["banks"][rotation["at"] % len(rotation["banks"])]
                    rotation["at"] += 1
                else:
                    b = banks_from
                assert product not in place, product
                turn = turns.get(b, 0)
                turns[b] = turn + 1
                place[product] = (b, turn)
                if turn:
                    pe.wait_ge(sem(f"bank_free{b}"), turn)
                return banks[b]

            def filled(product):
                pn.last = finished(product)
                return pn.last[0]

            def panel(name):
                i = panels[0]
                panels[0] += 1
                order.append([name, None])
                pe.wait_ge(sem(f"slot_loaded{i % SLOTS}"), 16 * (i // SLOTS + 1))
                return ring[:, i % SLOTS, :]

            def panel_used():
                order[-1][1] = pn.last

            def wt(W, n):
                return W[:, 0:KT * n].rearrange("p (k n) -> p k n", k=KT)

            def project_T(name, weights, src, wait=None, k_tiles=KT, m_tiles=4):
                for i in range(m_tiles // 2):
                    b = claim((*name, i))
                    for half in range(2):
                        ct = 2 * i + half
                        for k in range(k_tiles):
                            if wait and i == half == 0:
                                pe.wait_ge(sem(wait[0]), wait[1] + k + 1)
                            ins = mm(b[:, half * T:(half + 1) * T], weights[:, k, ct * P:(ct + 1) * P], src[:, k, :],
                                     start=(k == 0), stop=(k == k_tiles - 1))
                    ins.then_inc(filled((*name, i)), 1)

            def project_tok(name, weights, src, n=512, k_tiles=KT, wait=None):
                for tb in range(TB):
                    b = claim((*name, tb))
                    for k in range(k_tiles):
                        if wait and tb == 0:
                            pe.wait_ge(sem(wait[0]), wait[1] + k + 1)
                        ins = mm(b[:, 0:n], src[:, k, tb * P:(tb + 1) * P], weights[:, k, 0:n],
                                 start=(k == 0), stop=(k == k_tiles - 1))
                    ins.then_inc(filled((*name, tb)), 1)

            def transposes(name, src, tiles=KT):
                for i in range((tiles + 1) // 2):
                    b = claim((name, i))
                    for jj in range(min(2, tiles - 2 * i)):
                        for tb in range(TB):
                            j = 2 * i + jj
                            ins = nc.tensor.transpose(b[:, jj * T + tb * P:jj * T + (tb + 1) * P],
                                                      src[:, tb, j * P:(j + 1) * P], ident)
                    ins.then_inc(filled((name, i)), 1)

            ada_at = {"taken": 0, "summed": 0}

            def ada_columns():
                i = ada_at["summed"]
                ada_at["summed"] += 1
                b = claim(("ada", i))
                pe.wait_ge(sem("ada_part"), i + 1)
                for ct in range(4):
                    ins = mm(b[:, ct * P:(ct + 1) * P], ada_part[:, i % 2, ct * P:(ct + 1) * P], ones,
                             start=True, stop=True)
                ins.then_inc(filled(("ada", i)), 1)

            def ada(n, rest=0):
                for _ in range(n):
                    i = ada_at["taken"]
                    ada_at["taken"] += 1
                    ada_slots.append(panels[0])
                    panels[0] += 1
                    order.append([("ada", i), (sem("ada_part"), i + 1)])
                    if i - ada_at["summed"] >= 2:
                        ada_columns()
                for _ in range(rest):
                    ada_columns()

            def attention(name, heads, dv, scores, V):
                per = 512 // (TB * dv)

                def score(h):
                    b = claim((name, "S", h))
                    scores(h, b).then_inc(filled((name, "S", h)), 1)

                def turn_p(h):
                    b = claim((name, "PT", h))
                    pe.wait_ge(sem(name + "_p"), h + 1)
                    for n in range(3):
                        ins = nc.tensor.transpose(b[:, n * P:(n + 1) * P], Ps[:, h % 2, n * P:(n + 1) * P], ident)
                    ins.then_inc(filled((name, "PT", h)), 1)

                def pv(h):
                    if h % per == 0:
                        claim((name, "O", h // per), 5 + h // per % 2)
                    b = bank((name, "O", h // per))
                    pe.wait_ge(*evacuated((name, "PT", h)))
                    o = (h % per) * TB * dv
                    mm(b[:, o:o + dv], PTs[:, h % 2, 0:P], V[:, 0, h * dv:(h + 1) * dv], start=True, stop=True)
                    for kb in range(2):
                        ins = mm(b[:, o + dv:o + 2 * dv], PTs[:, h % 2, (1 + kb) * P:(2 + kb) * P],
                                 V[:, kb, h * dv:(h + 1) * dv], start=(kb == 0), stop=(kb == 1))
                    if h % per == per - 1:
                        ins.then_inc(filled((name, "O", h // per)), 1)
                    else:
                        ins.then_inc(pn.step(name + "_pv"), 1)

                kept, rotation["banks"] = rotation["banks"], list(range(5))
                for h in range(heads + 2):
                    if h < heads:
                        score(h)
                    if 1 <= h <= heads:
                        turn_p(h - 1)
                    if h >= 2:
                        pv(h - 2)
                rotation["banks"] = kept

            pe.wait_ge(sem("loads"), 16 * 4)
            pe.wait_ge(sem("xn"), 2)
            transposes("hT_a", XN)
            W = panel("lora")
            b = claim("lora")
            for a in range(2):
                for k in range(KT):
                    pe.wait_ge(sem("mix"), 8 * a + k + 1)
                    ins = mm(b[0:64, a * T:(a + 1) * T], W[:, a * 512 + k * 64:a * 512 + (k + 1) * 64], mix[a][:, k, :],
                             start=(k == 0), stop=(k == KT - 1))
            ins.then_inc(filled("lora"), 1)
            pe.wait_ge(*evacuated("lora"))
            for j in range(KT):
                b = claim(("za", j))
                for a in range(2):
                    ins = mm(b[:, a * T:(a + 1) * T], W[0:64, 1024 + a * D + j * P:1024 + a * D + (j + 1) * P],
                             lora[0:64, a, :], start=True, stop=True)
                ins.then_inc(filled(("za", j)), 1)
            panel_used()
            for n, name in ((2, "k"), (3, "r")):
                for half in range(2):
                    project_T((name, half), wt(panel((name, half)), 512), mix[n % 2],
                              wait=("mix", 8 * n) if half == 0 else None)
                    panel_used()
            pe.wait_ge(sem("kk_sq"), 2)
            for i in range(4):
                b = claim(("kk_ss", i))
                for jj in range(2):
                    ins = mm(b[:, jj * T:(jj + 1) * T], con("pair_ones"), bhat[:, 2 * i + jj, :], start=True, stop=True)
                ins.then_inc(filled(("kk_ss", i)), 1)
            for n, name in ((4, "v"), (5, "g")):
                for half in range(2):
                    project_tok((name, half), wt(panel((name, half)), 512), mix[n % 2],
                                wait=("mix", 8 * n) if half == 0 else None)
                    panel_used()
            ada(2)
            pe.wait_ge(sem("bonus_p"), 1)
            b = claim("bonus")
            for j in range(KT):
                for tb in range(TB):
                    ins = mm(b[:, tb * NH + 2 * j:tb * NH + 2 * j + 2], bonus_p[:, j, tb * P:(tb + 1) * P], con("pair_sel"),
                             start=True, stop=True)
            ins.then_inc(filled("bonus"), 1)
            pe.wait_ge(sem("hats"), 1)
            for name, src in (("kt", khat), ("bt", bhat)):
                for i in range(4):
                    b = claim((name, i))
                    for tb in range(TB):
                        for jj in range(2):
                            ins = nc.tensor.transpose(b[:, tb * T + jj * P:tb * T + (jj + 1) * P],
                                                      src[:, 2 * i + jj, tb * P:(tb + 1) * P], ident)
                    ins.then_inc(filled((name, i)), 1)
            for tb in range(TB):
                for hp in range(2):
                    for jg in range(2):
                        for name, src in (("gk", khat), ("gb", bhat)):
                            b = claim((name, tb, hp, jg))
                            for jj in range(4):
                                j = 4 * jg + jj
                                for q in range(2):
                                    c = 2 * tb + q
                                    ins = mm(b[q * LC:(q + 1) * LC, jj * P:(jj + 1) * P],
                                             src[hp * HD:(hp + 1) * HD, j, c * LC:(c + 1) * LC],
                                             AR[hp * HD:(hp + 1) * HD, j, c, :, :].rearrange("p a t -> p (a t)"),
                                             start=True, stop=True)
                            ins.then_inc(filled((name, tb, hp, jg)), 1)

            def tiles64(product, lhs, rhs):
                b = claim(product)
                for j in range(8):
                    for q in range(2):
                        ins = mm(b[q * LC:(q + 1) * LC, j * LC:(j + 1) * LC], lhs(q, j), rhs(q, j), start=True, stop=True)
                ins.then_inc(filled(product), 1)

            def rows(buf, g):
                return lambda q, j: buf[q * LC:(q + 1) * LC, g, j, :]

            for g in range(4):
                pe.wait_ge(sem("tt"), g + 1)
                tiles64(("T0", g), rows(TTI, g), lambda q, j: con("eye")[q * LC:(q + 1) * LC, :])
            for l in range(1, 6):
                for g in range(4):
                    pe.wait_ge(sem("ct"), 4 * (l - 1) + g + 1)
                    if l == 1:
                        pe.wait_ge(*evacuated(("T0", g)))
                    else:
                        pe.wait_ge(*evacuated(("T", l - 1, g)))
                    tiles64(("X", l, g), rows(CT, g), rows(TI, g))
                for g in range(4):
                    pe.wait_ge(*evacuated(("X", l, g)))
                    if l > 1:
                        pe.wait_ge(*evacuated(("TT", l - 1, g)))
                    if l < 5:
                        tiles64(("T", l, g), rows(TTI, g), rows(XS, g))
                    tiles64(("TT", l, g), rows(XS, g), rows(TTI, g))
                ada(1)
            for c in range(NC_):
                tb, q = c // 2, c % 2
                r0, r1 = q * LC, (q + 1) * LC
                for hg in range(2):
                    def from_state(b, a):
                        for jj in range(4):
                            mm(b[r0:r1, jj * P:(jj + 1) * P], AR[:, 4 * hg + jj, c, a, :], SBD[:, 4 * hg + jj, :],
                               start=(jj == 0), stop=False, skip_group_check=True)

                    b = claim(("R", c, hg))
                    if c:
                        pe.wait_ge(sem("state"), 2 * (c - 1) + hg + 1)
                        from_state(b, 0)
                    for jj in range(4):
                        for hp in range(2):
                            j = 4 * hg + jj
                            ins = mm(b[r0:r1, jj * P + hp * HD:jj * P + (hp + 1) * HD], PK[r0:r1, tb, hp, j, 0, :],
                                     Vr[r0:r1, tb, (2 * j + hp) * HD:(2 * j + hp + 1) * HD],
                                     start=(c == 0), stop=True, skip_group_check=True)
                    ins.then_inc(filled(("R", c, hg)), 1)
                for hg in range(2):
                    b = claim(("U", c, hg))
                    pe.wait_ge(*evacuated(("R", c, hg)))
                    if c == 0 and hg == 0:
                        for g in range(4):
                            pe.wait_ge(*evacuated(("TT", 5, g)))
                    for jj in range(4):
                        for hp in range(2):
                            j = 4 * hg + jj
                            o = (2 * j + hp) * HD
                            ins = mm(b[r0:r1, jj * P + hp * HD:jj * P + (hp + 1) * HD], TTI[r0:r1, 2 * tb + hp, j, :],
                                     Rs[r0:r1, o:o + HD], start=True, stop=True)
                    ins.then_inc(filled(("U", c, hg)), 1)
                for hg in range(2):
                    b = claim(("y", c, hg))
                    if c:
                        for jj in range(4):
                            mm(b[r0:r1, jj * P:(jj + 1) * P], AR[:, 4 * hg + jj, c, 1, :], SBD[:, 4 * hg + jj, :],
                               start=(jj == 0), stop=False, skip_group_check=True)
                    pe.wait_ge(*evacuated(("U", c, hg)))
                    for jj in range(4):
                        for hp in range(2):
                            j = 4 * hg + jj
                            o = (2 * j + hp) * HD
                            dst = b[r0:r1, jj * P + hp * HD:jj * P + (hp + 1) * HD]
                            mm(dst, PK[r0:r1, tb, hp, j, 1, :], Vr[r0:r1, tb, o:o + HD],
                               start=(c == 0), stop=False, skip_group_check=True)
                            ins = mm(dst, PB[r0:r1, tb, hp, j, 1, :], Un[r0:r1, o:o + HD],
                                     start=False, stop=True, skip_group_check=True)
                    ins.then_inc(filled(("y", c, hg)), 1)
                    if c < NC_ - 1:
                        b = claim(("S", c, hg))
                        for jj in range(4):
                            j = 4 * hg + jj
                            mm(b[:, jj * P:(jj + 1) * P], Kt[r0:r1, tb, j * P:(j + 1) * P], Vr[r0:r1, tb, j * P:(j + 1) * P],
                               start=True, stop=False)
                            ins = mm(b[:, jj * P:(jj + 1) * P], Bt[r0:r1, tb, j * P:(j + 1) * P], Un[r0:r1, j * P:(j + 1) * P],
                                     start=False, stop=True)
                        ins.then_inc(filled(("S", c, hg)), 1)
            pe.wait_ge(sem("y_gated"), 2)
            transposes("yT", Yr)
            pe.wait_ge(*evacuated(("yT", 3)))
            for half in range(2):
                project_tok(("wo_a", half), wt(panel(("wo_a", half)), 512), YT)
                panel_used()

            pe.wait_ge(sem("xn"), 4)
            transposes("hT_b", XN)
            pe.wait_ge(*evacuated(("hT_b", 3)))
            for name, src in (("k1", hkvT), ("v1", hkvT), ("q1", hbT), ("g1", hbT)):
                for half in range(2):
                    project_tok((name, half), wt(panel((name, half)), 512), src)
                    panel_used()
                    if name in ("v1", "q1"):
                        ada(1)
            ada(1, rest=2)
            pe.wait_ge(sem("k1_rope"), 1)
            transposes("k1T", K1)
            pe.wait_ge(sem("q1_rope"), 1)
            transposes("q1T", Q1)
            pe.wait_ge(*evacuated(("q1T", 3)))

            def scores1(h, b):
                j, r0 = h // 2, (h % 2) * HD
                mm(b[:, 0:P], Q1T[r0:r0 + HD, j, 0:P], K1T[r0:r0 + HD, j, 0:P], start=True, stop=True)
                return mm(b[:, P:3 * P], Q1T[r0:r0 + HD, j, P:T], K1T[r0:r0 + HD, j, :], start=True, stop=True)

            attention("at1", NH, HD, scores1, V1)
            pe.wait_ge(sem("o1"), 1)
            transposes("o1T", O1)
            pe.wait_ge(*evacuated(("o1T", 3)))
            for half in range(2):
                project_tok(("wo_b", half), wt(panel(("wo_b", half)), 512), O1T)
                panel_used()

            def spread(i):
                for half in range(2):
                    b = claim(("gb", i, half))
                    for jj in range(4):
                        pe.wait_ge(sem("diag"), 8 * i + 4 * half + jj + 1)
                        ins = mm(b[:, jj * P:(jj + 1) * P], ones, DIAG[:, 4 * half + jj, :], start=True, stop=True)
                    ins.then_inc(filled(("gb", i, half)), 1)

            def mlp(l):
                pe.wait_ge(sem("xn"), 8 + 4 * l)
                transposes(f"hT_m{l}", XN)
                pe.wait_ge(*evacuated((f"hT_m{l}", 3)))
                rotation["banks"] = [4, 5, 6, 7]
                for tb in range(TB):
                    for half in range(2):
                        claim(("mlp", l, tb, half), 2 * tb + half)

                def up(n):
                    project_T(("up", l, n), wt(panel(("w1", l, n)), 512), hT2)
                    panel_used()

                def down(n):
                    W = panel(("w2", l, n)).rearrange("p (k n) -> p k n", k=4)
                    pe.wait_ge(sem("relu2"), 2 * (8 * l + n) + 2)
                    for k in range(4):
                        for tb in range(TB):
                            for half in range(2):
                                ins = mm(bank(("mlp", l, tb, half))[:, :], AF[:, n % 2, k, tb * P:(tb + 1) * P],
                                         W[:, k, half * 512:(half + 1) * 512], start=(n == 0 and k == 0),
                                         stop=(n == 7 and k == 3))
                                if n == 7 and k == 3:
                                    ins.then_inc(filled(("mlp", l, tb, half)), 1)
                    if n < 7:
                        ins.then_inc(pn.step("mlp_down"), 1)
                    panel_used()
                    if l == 0:
                        ada(2, rest=2 * (n == 7))

                for n in range(9):
                    if n < 8:
                        up(n)
                    if n:
                        down(n - 1)
                rotation["banks"] = list(range(8))

            rotation["banks"] = list(range(8))
            spread(0)
            spread(1)
            pe.wait_ge(sem("xn"), 6)
            transposes("hT_c", XN)
            pe.wait_ge(*evacuated(("hT_c", 3)))
            b = claim("gates")
            for a in range(2):
                for k in range(KT):
                    ins = mm(b[0:8, a * T:(a + 1) * T], par("gate_w")[:, k * 16 + a * 8:k * 16 + a * 8 + 8], hT2[:, k, :],
                             start=(k == 0), stop=(k == KT - 1))
            ins.then_inc(filled("gates"), 1)
            for name in ("q2", "k2"):
                project_T((name,), wt(panel(name), 512), hT2)
                panel_used()
            for name in ("v2", "og"):
                for half in range(2):
                    project_tok((name, half), wt(panel((name, half)), 512), hT2)
                    panel_used()
            pe.wait_ge(sem("gate_rows"), 1)
            b = claim("gate_cols")
            for tb in range(TB):
                nc.tensor.transpose(b[:, tb * 16:tb * 16 + 8], c_row[0:8, tb * P:(tb + 1) * P], ident[0:8, 0:8])
                ins = nc.tensor.transpose(b[:, tb * 16 + 8:tb * 16 + 16], em_row[0:8, tb * P:(tb + 1) * P], ident[0:8, 0:8])
            ins.then_inc(filled("gate_cols"), 1)
            pe.wait_ge(*evacuated(("v2", 1, 1)))
            pe.wait_ge(sem("head_sel"), 16)
            for h in range(MH + 2):
                if h < MH:
                    b = claim(("m", h))
                    mm(b[:, 0:T], head_sel[:, h * P:(h + 1) * P], m_row[0:8, :], start=True, stop=True).then_inc(filled(("m", h)), 1)
                    b = claim(("qk", h))
                    j, r0 = h // 2, (h % 2) * DKM
                    mm(b[:, 0:T], K2T[r0:r0 + DKM, j, 0:P], Q2T[r0:r0 + DKM, j, :], start=True, stop=True)
                    mm(b[:, T:T + P], K2T[r0:r0 + DKM, j, P:T], Q2T[r0:r0 + DKM, j, P:T], start=True, stop=True).then_inc(filled(("qk", h)), 1)
                if h >= 2:
                    g = h - 2
                    b = claim(("num", g))
                    pe.wait_ge(*evacuated(("qk", g)))
                    w = PT2[:, g % 2, :]
                    mm(b[:, 0:129], w[:, 0:P], V2[:, 0, g, :], start=True, stop=True)
                    mm(b[:, 129:258], w[:, P:T], V2[:, 0, g, :], start=True, stop=False)
                    mm(b[:, 129:258], w[:, T:T + P], V2[:, 1, g, :], start=False, stop=True).then_inc(filled(("num", g)), 1)
            pe.wait_ge(sem("h2"), 1)
            transposes("h2T", H2)
            pe.wait_ge(*evacuated(("h2T", 3)))
            for half in range(2):
                project_tok(("wo_c", half), wt(panel(("wo_c", half)), 512), H2T)
                panel_used()
            mlp(0)

            spread(2)
            spread(3)
            pe.wait_ge(sem("xn"), 10)
            transposes("hT_d", XN)
            pe.wait_ge(*evacuated(("hT_d", 3)))
            Wa = panel("kv_a")
            Wk = wt(Wa, KVL + RD)
            project_tok(("ckv",), Wk, hkvT2, n=KVL + RD)
            Wq = panel("q_a")
            project_tok(("cq",), wt(Wq, QL), hT2, n=QL)
            panel_used()
            pe.wait_ge(sem("ckv_n"), 1)
            b = claim("ckvT")
            for j in range(2):
                for tb in range(TB):
                    ins = nc.tensor.transpose(b[:, j * T + tb * P:j * T + (tb + 1) * P], CKV[:, tb, j * P:(j + 1) * P], ident)
            ins.then_inc(filled("ckvT"), 1)
            b = claim("krT")
            for tb in range(TB):
                ins = nc.tensor.transpose(b[:, tb * P:(tb + 1) * P], KR[:, tb, :], ident)
            ins.then_inc(filled("krT"), 1)
            pe.wait_ge(sem("cq_n"), 1)
            transposes("cqT", CQ, tiles=3)
            pe.wait_ge(*evacuated(("cqT", 1)))
            Wqr = Wa[:, 2560:4096].rearrange("p (k n) -> p k n", k=3)
            project_tok(("qr",), Wqr, CQT, k_tiles=3)
            order[-2][1] = pn.last
            Wb = panel("kv_b")
            pe.wait_ge(*evacuated("krT"))
            for half in range(2):
                project_T(("kn", half), Wb[:, half * 1024:(half + 1) * 1024].rearrange("p (k n) -> p k n", k=2), CKVT, k_tiles=2)
            for half in range(2):
                project_tok(("v3", half), Wb[:, 2048 + half * 1024:2048 + (half + 1) * 1024].rearrange("p (k n) -> p k n", k=2),
                            CKVT, k_tiles=2)
            panel_used()
            Wn = panel("q_b")
            for half in range(2):
                project_T(("qn", half), Wn[:, half * 1536:(half + 1) * 1536].rearrange("p (k n) -> p k n", k=3), CQT, k_tiles=3)
            panel_used()
            pe.wait_ge(sem("qr_rope"), 1)
            transposes("qrT", QR, tiles=4)
            pe.wait_ge(*evacuated(("qrT", 1)))

            def scores3(h, b):
                j, r0 = h // 2, (h % 2) * RD
                mm(b[:, 0:P], QNT[:, h, 0:P], KNT[:, h, 0:P], start=True, stop=False)
                mm(b[:, 0:P], QRT[r0:r0 + RD, j, 0:P], KRT[r0:r0 + RD, 0:P], start=False, stop=True)
                mm(b[:, P:3 * P], QNT[:, h, P:T], KNT[:, h, :], start=True, stop=False)
                return mm(b[:, P:3 * P], QRT[r0:r0 + RD, j, P:T], KRT[r0:r0 + RD, :], start=False, stop=True)

            attention("at3", MH, DV, scores3, V3)
            pe.wait_ge(*evacuated(("at3", "O", 3)))
            transposes("o3T", O3)
            pe.wait_ge(*evacuated(("o3T", 3)))
            for half in range(2):
                project_tok(("wo_d", half), wt(panel(("wo_d", half)), 512), O3T)
                panel_used()
            mlp(1)

        @block.sync
        def _(sp):
            for i, (name, released) in enumerate(order):
                if i >= SLOTS:
                    sp.wait_ge(*order[i - SLOTS][1])
                sp.dma_start(ring[:, i % SLOTS, :], stream[i]).then_inc(sem(f"slot_loaded{i % SLOTS}"), 16)
            for tb in range(TB):
                sp.wait_ge(sem("final"), tb + 1)
                sp.dma_start(out[0, tb * P:(tb + 1) * P, :], X[:, tb, :]).then_inc(sem("stored"), 16)
            sp.wait_ge(sem("stored"), 16 * TB)

        @block.gpsimd
        def _(pool):
            level = con("level").rearrange("p (l t) -> p l t", l=6)
            for l in range(1, 6):
                for g in range(4):
                    if l == 1:
                        pool.wait_ge(sem("tt"), g + 1)
                    else:
                        pool.wait_ge(*finished(("X", l - 1, g)))
                    nc.gpsimd.tensor_tensor(CT[:, g], PB[:, g // 2, g % 2, :, 0, :],
                                            level[:, l:l + 1, :].to_broadcast([P, 8, LC]), ALU.mult).then_inc(sem("ct"), 1)

        @block.scalar
        def _(act_):
            ac = Count("act_steps")
            act = nc.scalar.activation

            act_.dma_start(X, x.rearrange("a (b p) d -> p (a b) d", p=P)).then_inc(sem("loads"), 16)
            act_.dma_start(cc[:, :], cc_d).then_inc(sem("loads"), 16)
            act_.dma_start(pc[:, :], pc_d).then_inc(sem("loads"), 16)
            act_.dma_start(pos_i[:, :], pos_d).then_inc(sem("loads"), 16)
            for a in range(2):
                act_.dma_start(gn[:, a, :], gn_d[a:a + 1, :].to_broadcast([P, D])).then_inc(sem("gn_rows"), 16)
            act_.wait_ge(sem("loads"), 64)
            act(cond, par("cond"), ACT.Silu).then_inc(ac.step("cond"), 1)

            def copy(dst, product, n=512, **kw):
                act_.wait_ge(*finished(product))
                act(dst, bank(product)[:, 0:n].rearrange("p (a b) -> p a b", a=dst.shape[1]) if len(dst.shape) == 3 else bank(product)[:, 0:n],
                               kw.get("func", ACT.Copy)).then_inc(ac.frees(product), 1)

            ada_at = {"taken": 0, "summed": 0}

            def ada_columns():
                i = ada_at["summed"]
                ada_at["summed"] += 1
                act_.wait_ge(*finished(("ada", i)))
                act(ADA[:, 4 * i:4 * i + 4], bank(("ada", i))[:, 0:512:P], ACT.Copy).then_inc(ac.frees(("ada", i)), 1)

            def ada(n, rest=0):
                for _ in range(n):
                    i = ada_at["taken"]
                    ada_at["taken"] += 1
                    if i - ada_at["summed"] >= 2:
                        ada_columns()
                for _ in range(rest):
                    ada_columns()

            def scaled(name, dst, scale, bias=None, tiles=KT):
                for i in range((tiles + 1) // 2):
                    act_.wait_ge(*finished((name, i)))
                    for jj in range(min(2, tiles - 2 * i)):
                        j = 2 * i + jj
                        ins = act(dst[:, j, :], bank((name, i))[:, jj * T:(jj + 1) * T], ACT.Identity,
                                  scale=scale[:, j:j + 1], bias=0.0 if bias is None else bias[:, j:j + 1])
                        if j % 2 == 1 or j == tiles - 1:
                            ins.then_inc(ac.frees((name, i)), 1)
                        else:
                            ins.then_inc(ac.step(), 1)

            def plain(name, dst, tiles=KT):
                for i in range((tiles + 1) // 2):
                    n = min(2, tiles - 2 * i)
                    copy(dst[:, 2 * i:2 * i + n, :], (name, i), n * T)

            scaled("hT_a", hT, par("norm_a"))
            act_.wait_ge(sem("angles"), 1)
            for a in range(2):
                act(rope2[:, a], rope2[:, a], ACT.Sin).then_inc(ac.step("tables"), 1)
            act_.wait_ge(*finished("lora"))
            act(lora[0:64, 0, :], bank("lora")[0:64, 0:T], ACT.Tanh).then_inc(ac.step(), 1)
            act(lora[0:64, 1, :], bank("lora")[0:64, T:2 * T], ACT.Copy).then_inc(ac.frees("lora"), 1)
            for j in range(KT):
                act_.wait_ge(*finished(("za", j)))
                act(LW[:, j, :], bank(("za", j))[:, 0:T], ACT.Sigmoid, bias=par("w0")[:, j:j + 1]).then_inc(ac.step("sig"), 1)
                act(AA[:, j, :], bank(("za", j))[:, T:2 * T], ACT.Sigmoid, bias=par("a0")[:, j:j + 1]).then_inc(ac.frees(("za", j)), 1)
            for half in range(2):
                for i in range(2):
                    copy(khat[:, 4 * half + 2 * i:4 * half + 2 * i + 2, :], ("k", half, i))
            for h in range(2):
                act_.wait_ge(sem("kkr"), 4 * h + 4)
                act(bhat[:, 4 * h:4 * h + 4, :], KK[:, 4 * h:4 * h + 4, :], ACT.Square).then_inc(ac.step("kk_sq"), 1)
            for half in range(2):
                for i in range(2):
                    j = 4 * half + 2 * i
                    act_.wait_ge(*finished(("r", half, i)))
                    for jj in range(2):
                        ins = act(AR[:, j + jj, :, 1, :], bank(("r", half, i))[:, jj * T:(jj + 1) * T].rearrange("p (c t) -> p c t", c=4), ACT.Copy)
                        if jj == 0:
                            ins.then_inc(ac.step(), 1)
                    ins.then_inc(ac.frees(("r", half, i)), 1)
            for i in range(4):
                copy(bhat[:, 2 * i:2 * i + 2, :], ("kk_ss", i), func=ACT.Sqrt)
            for half in range(2):
                for tb in range(TB):
                    copy(Vr[:, tb, half * 512:(half + 1) * 512], ("v", half, tb))
            act_.wait_ge(sem("mix"), 48)
            for h in range(2):
                s = slice(4 * h, 4 * h + 4)
                act_.wait_ge(sem("cum"), 4 * h + 4)
                act(EN[:, s, :], EE[:, s, :], ACT.Exp, scale=KAPPA).then_inc(ac.step(), 1)
                act(LW[:, s, :], LW[:, s, :], ACT.Exp, scale=-KAPPA).then_inc(ac.step(), 1)
                act_.wait_ge(*ac.last)
                act(EE[:, s, :], EE[:, s, :], ACT.Exp, scale=-KAPPA).then_inc(ac.step("exps"), 1)
            act(F[:, :, 0:3], F[:, :, 0:3], ACT.Exp, scale=-KAPPA).then_inc(ac.step("exps"), 1)
            for half in range(2):
                for tb in range(TB):
                    copy(Gr[:, tb, half * 512:(half + 1) * 512], ("g", half, tb), func=ACT.Silu)
            ada(2)
            for name, dst in (("kt", Kt), ("bt", Bt)):
                for i in range(4):
                    copy(dst[:, :, i * T:(i + 1) * T], (name, i))
            for g in range(4):
                copy(TI[:, g].rearrange("p j t -> p (j t)"), ("T0", g))
            for l in range(1, 6):
                for g in range(4):
                    copy(XS[:, g].rearrange("p j t -> p (j t)"), ("X", l, g))
                ada(1)
            for c in range(NC_):
                tb, q = c // 2, c % 2
                r = slice(q * LC, (q + 1) * LC)
                for hg in range(2):
                    act_.wait_ge(*finished(("U", c, hg)))
                    act(Un[r, hg * 512:(hg + 1) * 512], bank(("U", c, hg))[r, :], ACT.Copy, scale=-1.0).then_inc(ac.frees(("U", c, hg)), 1)
                for hg in range(2):
                    act_.wait_ge(*finished(("y", c, hg)))
                    act(Yr[r, tb, hg * 512:(hg + 1) * 512], bank(("y", c, hg))[r, :], ACT.Copy).then_inc(ac.frees(("y", c, hg)), 1)
            plain("yT", YT)

            def attention(name, heads, dv, scale):
                for h in range(heads + 1):
                    if h < heads:
                        if h >= 2:
                            act_.wait_ge(*finished((name, "PT", h - 2)))
                        act_.wait_ge(sem(name + "_max"), h + 1)
                        act(Ps[:, h % 2, 0:P], Ss[:, h % 2, 0:P], ACT.Exp, scale=scale, bias=nmax[:, h, 0:1],
                                   accum_out=rs[:, h, 0:1]).then_inc(ac.step(), 1)
                        act(Ps[:, h % 2, P:3 * P], Ss[:, h % 2, P:3 * P], ACT.Exp, scale=scale, bias=nmax[:, h, 1:2],
                                   accum_out=rs[:, h, 1:2]).then_inc(ac.step(name + "_p"), 1)
                    if h >= 1:
                        if h >= 3:
                            act_.wait_ge(*pv_done(name, 512 // (TB * dv), h - 3))
                        copy(PTs[:, (h - 1) % 2, :], (name, "PT", h - 1), 3 * P)

            for i in range(4):
                act_.wait_ge(*finished(("hT_b", i)))
                for jj in range(2):
                    j = 2 * i + jj
                    for n, (dst, w) in enumerate(((hkvT, "norm_kv"), (hbT, "norm_b"))):
                        ins = act(dst[:, j, :], bank(("hT_b", i))[:, jj * T:(jj + 1) * T], ACT.Copy, scale=par(w)[:, j:j + 1])
                        if (jj, n) == (1, 1):
                            ins.then_inc(ac.frees(("hT_b", i)), 1)
                        else:
                            ins.then_inc(ac.step(), 1)
            for name, dst, f in (("k1", K1, ACT.Copy), ("v1", V1, ACT.Copy), ("q1", Q1, ACT.Copy), ("g1", G1, ACT.Silu)):
                for half in range(2):
                    for tb in range(TB):
                        copy(dst[:, tb, half * 512:(half + 1) * 512], (name, half, tb), func=f)
                    if name in ("v1", "q1"):
                        ada(1)
            ada(1, rest=2)
            plain("k1T", K1T)
            plain("q1T", Q1T)
            attention("at1", NH, HD, 0.125)
            plain("o1T", O1T)

            def mod_scaled(name, which, dst):
                act_.wait_ge(sem("mod"), which + 1)
                scaled(name, dst, MODS[which][0], MODS[which][1])

            def mlp(l):
                mod_scaled(f"hT_m{l}", (1, 4)[l], hT2)
                for n in range(8):
                    for i in range(2):
                        p = ("up", l, n, i)
                        m = 2 * (8 * l + n) + i
                        act_.wait_ge(*finished(p))
                        if m >= 4:
                            act_.wait_ge(sem("relu2"), m - 3)
                        act(RL[:, n % 2, 2 * i:2 * i + 2, :], bank(p)[:, :].rearrange("p (a t) -> p a t", a=2), ACT.Relu).then_inc(ac.frees(p), 1)
                    if l == 0 and n >= 2:
                        ada(2)
                if l == 0:
                    ada(4, rest=2)
                for tb in range(TB):
                    for half in range(2):
                        copy(Yb[:, tb, half * 512:(half + 1) * 512], ("mlp", l, tb, half))

            def post(name):
                for half in range(2):
                    for tb in range(TB):
                        copy(Yb[:, tb, half * 512:(half + 1) * 512], (name, half, tb))

            act_.wait_ge(sem("y_gated"), 2)
            act_.dma_start(head_sel, sel_d).then_inc(sem("head_sel"), 16)
            mod_scaled("hT_c", 0, hT2)
            gb = par("gate_b")
            act_.wait_ge(*finished("gates"))
            act(i_row[0:8, :], bank("gates")[0:8, 0:T], ACT.Identity, bias=gb[0:8, 0:1]).then_inc(ac.step(), 1)
            act(f_row[0:8, :], bank("gates")[0:8, T:2 * T], ACT.Identity, bias=gb[0:8, 1:2]).then_inc(ac.step("gate_if"), 1)
            act(t_row[0:8, :], bank("gates")[0:8, T:2 * T], ACT.Abs, bias=gb[0:8, 1:2]).then_inc(ac.frees("gates"), 1)
            act_.wait_ge(*ac.last)
            act(t_row[0:8, :], t_row[0:8, :], ACT.Exp, scale=-1.0).then_inc(ac.step(), 1)
            act_.wait_ge(*ac.last)
            act(t_row[0:8, :], t_row[0:8, :], ACT.Ln, bias=1.0).then_inc(ac.step("gate_ln"), 1)
            for name, dst in (("q2", Q2T), ("k2", K2T)):
                for i in range(2):
                    copy(dst[:, 2 * i:2 * i + 2, :], (name, i))
            for half in range(2):
                for tb in range(TB):
                    copy(V2[:, tb, 4 * half:4 * half + 4, 0:DV], ("v2", half, tb))
            act_.wait_ge(sem("m_total"), 1)
            act(em_row[0:8, :], mt_row[0:8, :], ACT.Exp, scale=-1.0).then_inc(ac.step("gate_rows"), 1)
            for half in range(2):
                for tb in range(TB):
                    copy(G1[:, tb, half * 512:(half + 1) * 512], ("og", half, tb), func=ACT.Sigmoid)
            for h in range(MH):
                act_.wait_ge(*evacuated(("m", h)))
                act(W2[:, h % 2, :], W2[:, h % 2, :], ACT.Exp, scale=-1.0).then_inc(ac.step("wexp"), 1)
            scaled("h2T", H2T, par("head_g"))
            post("wo_c")
            mlp(0)

            act_.wait_ge(sem("mod"), 4)
            for i in range(4):
                act_.wait_ge(*finished(("hT_d", i)))
                for jj in range(2):
                    j = 2 * i + jj
                    for n, (dst, m) in enumerate(((hkvT2, 2), (hT2, 3))):
                        ins = act(dst[:, j, :], bank(("hT_d", i))[:, jj * T:(jj + 1) * T], ACT.Identity,
                                  scale=MODS[m][0][:, j:j + 1], bias=MODS[m][1][:, j:j + 1])
                        if (jj, n) == (1, 1):
                            ins.then_inc(ac.frees(("hT_d", i)), 1)
                        else:
                            ins.then_inc(ac.step(), 1)
            for tb in range(TB):
                copy(CKVR[:, tb, :], ("ckv", tb), KVL + RD)
            for tb in range(TB):
                copy(CQ[:, tb, :], ("cq", tb), QL)
            act_.wait_ge(*finished("ckvT"))
            for j in range(2):
                ins = act(CKVT[:, j, :], bank("ckvT")[:, j * T:(j + 1) * T], ACT.Copy, scale=par("kv_latent")[:, j:j + 1])
                if j == 0:
                    ins.then_inc(ac.step(), 1)
            ins.then_inc(ac.frees("ckvT"), 1)
            copy(KRT, "krT", T)
            scaled("cqT", CQT, par("q_latent"), tiles=3)
            for tb in range(TB):
                copy(QR[:, tb, :], ("qr", tb))
            for half in range(2):
                for i in range(2):
                    copy(KNT[:, 4 * half + 2 * i:4 * half + 2 * i + 2, :], ("kn", half, i))
            for half in range(2):
                for tb in range(TB):
                    copy(V3[:, tb, half * 512:(half + 1) * 512], ("v3", half, tb))
            for half in range(2):
                for i in range(2):
                    copy(QNT[:, 4 * half + 2 * i:4 * half + 2 * i + 2, :], ("qn", half, i))
            plain("qrT", QRT, tiles=4)
            attention("at3", MH, DV, MLA_SCALE)
            plain("o3T", O3T)
            post("wo_d")
            mlp(1)

        @block.vector
        def _(dve):
            dv = Count("dve_steps")
            V = nc.vector
            tt, ts, stt = V.tensor_tensor, V.tensor_scalar, V.scalar_tensor_tensor

            def rsqrt(dst, src, mul, eps):
                ts(dst, src, mul, eps, ALU.mult, ALU.add).then_inc(dv.step(), 1)
                dve.wait_ge(*dv.last)
                w = dst.shape[-1]
                y, z = newton[:, 0, 0:w], newton[:, 1, 0:w]
                ts(z.bitcast(I32), dst.bitcast(I32), 1, None, ALU.logical_shift_right).then_inc(dv.step(), 1)
                dve.wait_ge(*dv.last)
                ts(y.bitcast(I32), z.bitcast(I32), -1.0, float(0x5F3759DF), ALU.mult, ALU.add).then_inc(dv.step(), 1)
                dve.wait_ge(*dv.last)
                for step in range(3):
                    tt(z, y, y, ALU.mult).then_inc(dv.step(), 1)
                    dve.wait_ge(*dv.last)
                    stt(z, z, -0.5, dst, ALU.mult, ALU.mult).then_inc(dv.step(), 1)
                    dve.wait_ge(*dv.last)
                    stt(dst if step == 2 else y, z, 1.5, y, ALU.add, ALU.mult).then_inc(dv.step(), 1)
                    dve.wait_ge(*dv.last)

            def norm():
                for tb in range(TB):
                    V.tensor_tensor_reduce(XN[:, tb, :], X[:, tb, :], X[:, tb, :], 1.0, 0.0, ALU.mult, ALU.add,
                                                  accum_out=ss[:, tb:tb + 1]).then_inc(dv.step(), 1)
                dve.wait_ge(*dv.last)
                rsqrt(ss, ss, 1.0 / D, EPS)
                for tb in range(TB):
                    ts(XN[:, tb, :], X[:, tb, :], ss[:, tb:tb + 1], None, ALU.mult).then_inc(dv.step("xn"), 1)

            def add_to_x(name):
                for half in range(2):
                    for tb in range(TB):
                        s = X[:, tb, half * 512:(half + 1) * 512]
                        dve.wait_ge(*finished((name, half, tb)))
                        tt(s, s, bank((name, half, tb))[:, :], ALU.add).then_inc(dv.frees((name, half, tb)), 1)
                dve.wait_ge(*dv.last)

            ada_at = [0]

            def ada(n):
                for _ in range(n):
                    i, k = divmod(ada_at[0], KT)
                    ada_at[0] += 1
                    slot, part = ada_slots[i], ada_part[:, i % 2, :]
                    if k == 0:
                        if i >= 2:
                            dve.wait_ge(*finished(("ada", i - 2)))
                        dve.wait_ge(sem(f"slot_loaded{slot % SLOTS}"), 16 * (slot // SLOTS + 1))
                        dve.wait_ge(*dv.last)
                    else:
                        dve.wait_ge(sem("ada_sum"), (KT - 1) * i + k)
                    W = ring[:, slot % SLOTS, k * 512:(k + 1) * 512]
                    if k == 0:
                        ts(part, W, cond[:, 0:1], None, ALU.mult).then_inc(dv.step("ada_sum"), 1)
                    else:
                        stt(part, W, cond[:, k:k + 1], part, ALU.mult, ALU.add).then_inc(
                            dv.step("ada_part" if k == KT - 1 else "ada_sum"), 1)

            dve.wait_ge(sem("loads"), 64)
            dve.wait_ge(sem("cond"), 1)
            norm()
            ts(one_m_ka, par("ka"), -1.0, 1.0, ALU.mult, ALU.add).then_inc(dv.step(), 1)
            ang, n_, r_ = (EE[:, a, 0:64].rearrange("p (b f) -> p b f", b=TB) for a in range(3))
            dve.wait_ge(*dv.last)
            V.tensor_copy(ss, pos_i[:, :]).then_inc(dv.step(), 1)
            dve.wait_ge(*dv.last)
            for tb in range(TB):
                ts(ang[:, tb, :], con("inv2"), ss[:, tb:tb + 1], None, ALU.mult).then_inc(dv.step(), 1)
            dve.wait_ge(*dv.last)
            ts(n_, ang, 1.0 / TWO_PI, MAGIC, ALU.mult, ALU.add).then_inc(dv.step(), 1)
            dve.wait_ge(*dv.last)
            ts(n_, n_, -MAGIC, None, ALU.add).then_inc(dv.step(), 1)
            dve.wait_ge(*dv.last)
            stt(r_, n_, -C1, ang, ALU.mult, ALU.add).then_inc(dv.step(), 1)
            dve.wait_ge(*dv.last)
            stt(r_, n_, -C2, r_, ALU.mult, ALU.add).then_inc(dv.step(), 1)
            dve.wait_ge(*dv.last)
            stt(r_, n_, -C3, r_, ALU.mult, ALU.add).then_inc(dv.step(), 1)
            dve.wait_ge(*dv.last)
            ts(rope2[:, 1], r_, PI_CLAMP, -PI_CLAMP, ALU.min, ALU.max).then_inc(dv.step(), 1)
            dve.wait_ge(*dv.last)
            ts(rope2[:, 0], rope2[:, 1], -1.0, None, ALU.mult).then_inc(dv.step(), 1)
            dve.wait_ge(*dv.last)
            tt(rope2[:, 0], rope2[:, 0], rope2[:, 1], ALU.min).then_inc(dv.step(), 1)
            dve.wait_ge(*dv.last)
            ts(rope2[:, 0], rope2[:, 0], float(np.pi / 2), None, ALU.add).then_inc(dv.step("angles"), 1)
            dve.wait_ge(*evacuated(("hT_a", 3)))
            tt(xx[:, :, 1:T], hT[:, :, 0:T - 1], hT[:, :, 1:T], ALU.subtract).then_inc(dv.step(), 1)
            ts(xx[:, :, 0:1], hT[:, :, 0:1], -1.0, None, ALU.mult).then_inc(dv.step(), 1)
            dve.wait_ge(*dv.last)
            last_use = {2: "lora", 3: "lora", 4: ("k", 1, 1), 5: ("r", 1, 1)}

            def mixes(n, which):
                if n in last_use:
                    dve.wait_ge(*finished(last_use[n]))
                mu = par("mu")[:, 8 * which:8 * which + 8]
                for j in range(KT):
                    stt(mix[n % 2][:, j, :], xx[:, j, :], mu[:, j:j + 1], hT[:, j, :], ALU.mult, ALU.add).then_inc(dv.step("mix"), 1)

            for n, which in enumerate((1, 4, 2, 0)):
                mixes(n, which)
            for j in range(KT):
                dve.wait_ge(*evacuated(("k", j // 4, (j % 4) // 2)))
                ts(KK[:, j, :], khat[:, j, :], par("kk")[:, j:j + 1], None, ALU.mult).then_inc(dv.step("kkr"), 1)
            mixes(4, 3)
            dve.wait_ge(*evacuated(("za", 7)))
            scan = g_scan.rearrange("p (c t) -> p c t", c=NC_)
            for j in range(KT):
                dve.wait_ge(*dv.last)
                V.tensor_tensor_scan(g_scan, con("scan_reset"), LW[:, j, :], 0.0, ALU.mult, ALU.add).then_inc(dv.step(), 1)
                dve.wait_ge(*dv.last)
                e = EE[:, j, :].rearrange("p (c t) -> p c t", c=NC_)
                tt(e, scan, scan[:, :, 31:32].to_broadcast([P, NC_, LC]), ALU.subtract).then_inc(dv.step(), 1)
                dve.wait_ge(*dv.last)
                tt(F[:, j, 0:3], e[:, 0:3, 63], scan[:, 1:4, 31], ALU.add).then_inc(dv.step(), 1)
                tt(LW[:, j, :], EE[:, j, :], LW[:, j, :], ALU.subtract).then_inc(dv.step("cum"), 1)
            for j in range(KT):
                ts(mid[:, j % 2, :], AA[:, j, :], par("ka")[:, j:j + 1], one_m_ka[:, j:j + 1], ALU.mult, ALU.add).then_inc(dv.step(), 1)
                dve.wait_ge(*dv.last)
                tt(khat[:, j, :], khat[:, j, :], mid[:, j % 2, :], ALU.mult).then_inc(dv.step(), 1)
            mixes(5, 5)
            for i in range(4):
                s = slice(2 * i, 2 * i + 2)
                dve.wait_ge(*evacuated(("kk_ss", i)))
                ts(bhat[:, s, :], bhat[:, s, :], 1e-12, None, ALU.max).then_inc(dv.step(), 1)
                dve.wait_ge(*dv.last)
                V.reciprocal(bhat[:, s, :], bhat[:, s, :]).then_inc(dv.step(), 1)
                dve.wait_ge(*dv.last)
                tt(KK[:, s, :], KK[:, s, :], bhat[:, s, :], ALU.mult).then_inc(dv.step(), 1)
                dve.wait_ge(*dv.last)
                tt(bhat[:, s, :], KK[:, s, :], AA[:, s, :], ALU.mult).then_inc(dv.step(), 1)
            dve.wait_ge(*evacuated(("r", 1, 1)))
            dve.wait_ge(*finished(("v", 1, 1)))
            for j in range(KT):
                ch = lambda a: a.rearrange("p (c t) -> p c t", c=NC_)
                ins = stt(ch(bonus_p[:, j, :]), AR[:, j, :, 1, :], par("rk")[:, j:j + 1], ch(khat[:, j, :]), ALU.mult, ALU.mult)
                ins.then_inc(dv.step("bonus_p" if j == KT - 1 else None), 1)
            dve.wait_ge(*dv.last)
            dve.wait_ge(sem("exps"), 3)
            for j in range(KT):
                tt(AR[:, j, :, 1, :], AR[:, j, :, 1, :], ch(EE[:, j, :]), ALU.mult).then_inc(dv.step(), 1)
                tt(AR[:, j, :, 0, :], ch(KK[:, j, :]), ch(LW[:, j, :]), ALU.mult).then_inc(dv.step(), 1)
            tt(bhat, bhat, EN, ALU.mult).then_inc(dv.step(), 1)
            tt(khat, khat, EN, ALU.mult).then_inc(dv.step("hats"), 1)
            dve.wait_ge(*finished("bonus"))
            V.tensor_copy(bonus, bank("bonus")[:, 0:32].rearrange("p (b h) -> p b h", b=TB)).then_inc(dv.frees("bonus"), 1)
            si = con("strict_incl").rearrange("p (o n) -> p o n", o=1).to_broadcast([P, 4, P])
            level = con("level").rearrange("p (l t) -> p l t", l=6)
            eye = con("eye").rearrange("p (o t) -> p o t", o=1).to_broadcast([P, 8, LC])
            for tb in range(TB):
                for hp in range(2):
                    for jg in range(2):
                        for name, dst in (("gk", PK), ("gb", PB)):
                            p = (name, tb, hp, jg)
                            dve.wait_ge(*finished(p))
                            d = dst[:, tb, hp, 4 * jg:4 * jg + 4, :, :].rearrange("p j a t -> p j (a t)")
                            tt(d, bank(p)[:, :].rearrange("p (j n) -> p j n", j=4), si, ALU.mult).then_inc(dv.frees(p), 1)
                        ada(2)
            dve.wait_ge(*dv.last)
            for g in range(4):
                tt(CT[:, g], PB[:, g // 2, g % 2, :, 0, :], level[:, 0:1, :].to_broadcast([P, 8, LC]), ALU.mult).then_inc(dv.step(), 1)
                dve.wait_ge(*dv.last)
                tt(TTI[:, g], eye, CT[:, g], ALU.subtract).then_inc(dv.step("tt"), 1)
            for l in range(1, 6):
                for g in range(4):
                    for name, dst in (("T", TI), ("TT", TTI)):
                        if (l, name) == (5, "T"):
                            continue
                        dve.wait_ge(*finished((name, l, g)))
                        tt(dst[:, g], dst[:, g], bank((name, l, g))[:, :].rearrange("p (j t) -> p j t", j=8),
                                      ALU.subtract).then_inc(dv.frees((name, l, g)), 1)
                    ada(2)
            V.memset(SBD, 0.0).then_inc(dv.step(), 1)
            dve.wait_ge(*dv.last)
            dve.wait_ge(sem("gn_rows"), 32)

            def heads(a):
                return a.rearrange("p (h d) -> p h d", d=HD)

            def group_norm(tb):
                y, tmp = Yr[:, tb, :], GNT[:, 0, :]
                wide = [P, NH, HD]
                dve.wait_ge(*evacuated(("y", 2 * tb + 1, 1)))
                V.tensor_reduce(stat[:, tb, :], heads(y), AX.X, ALU.add).then_inc(dv.step(), 1)
                dve.wait_ge(*dv.last)
                ts(stat[:, tb, :], stat[:, tb, :], 1.0 / HD, None, ALU.mult).then_inc(dv.step(), 1)
                dve.wait_ge(*dv.last)
                tt(heads(y), heads(y), stat[:, tb, :].unsqueeze(2).to_broadcast(wide), ALU.subtract).then_inc(dv.step(), 1)
                dve.wait_ge(*dv.last)
                tt(tmp, y, y, ALU.mult).then_inc(dv.step(), 1)
                dve.wait_ge(*dv.last)
                V.tensor_reduce(stat2[:, tb, :], heads(tmp), AX.X, ALU.add).then_inc(dv.step(), 1)
                dve.wait_ge(*dv.last)
                rsqrt(stat2[:, tb, :], stat2[:, tb, :], 1.0 / HD, GN_EPS)
                tt(heads(y), heads(y), stat2[:, tb, :].unsqueeze(2).to_broadcast(wide), ALU.mult).then_inc(dv.step(), 1)
                tt(heads(tmp), heads(Vr[:, tb, :]), bonus[:, tb, :].unsqueeze(2).to_broadcast(wide), ALU.mult).then_inc(dv.step(), 1)
                dve.wait_ge(*dv.last)
                tt(y, y, gn[:, 0, :], ALU.mult).then_inc(dv.step(), 1)
                tt(tmp, tmp, gn[:, 1, :], ALU.add).then_inc(dv.step(), 1)
                dve.wait_ge(*dv.last)
                tt(y, y, tmp, ALU.add).then_inc(dv.step(), 1)
                dve.wait_ge(*dv.last)
                tt(y, y, Gr[:, tb, :], ALU.mult).then_inc(dv.step("y_gated"), 1)

            for c in range(NC_):
                q = c % 2
                r = slice(q * LC, (q + 1) * LC)
                for hg in range(2):
                    p = ("R", c, hg)
                    dve.wait_ge(*finished(p))
                    V.tensor_copy(Rs[r, hg * 512:(hg + 1) * 512], bank(p)[r, :]).then_inc(dv.frees(p), 1)
                if c < NC_ - 1:
                    for hg in range(2):
                        p = ("S", c, hg)
                        dve.wait_ge(*finished(p))
                        parts = []
                        for hp in range(2):
                            k = slice(hp * HD, (hp + 1) * HD)
                            js = slice(4 * hg, 4 * hg + 4)
                            st = SBD[k, js, hp * HD:(hp + 1) * HD]
                            ins = tt(st, st, bank(p)[k, :].rearrange("p (j v) -> p j v", j=4)[:, :, hp * HD:(hp + 1) * HD], ALU.add)
                            parts.append((st, F[k, js, c:c + 1].to_broadcast([HD, 4, HD])))
                            if hp == 0:
                                ins.then_inc(dv.step(), 1)
                        ins.then_inc(dv.frees(p), 1)
                        dve.wait_ge(*dv.last)
                        for hp, (st, f) in enumerate(parts):
                            tt(st, st, f, ALU.mult).then_inc(dv.step("state" if hp else None), 1)
                if c == 2:
                    group_norm(0)
            group_norm(1)
            add_to_x("wo_a")

            norm()

            def head_norm(buf, w, n, nh, d, sq):
                b3 = buf.rearrange("p b (h d) -> p (b h) d", d=d)
                s3 = sq.rearrange("p b (h d) -> p (b h) d", d=d)
                st = stat.rearrange("p b h -> p (b h)")[:, 0:n * nh]
                tt(s3, b3, b3, ALU.mult).then_inc(dv.step(), 1)
                dve.wait_ge(*dv.last)
                V.tensor_reduce(st, s3, AX.X, ALU.add).then_inc(dv.step(), 1)
                dve.wait_ge(*dv.last)
                rsqrt(st, st, 1.0 / d, EPS)
                tt(b3, b3, st.unsqueeze(2).to_broadcast([P, n * nh, d]), ALU.mult).then_inc(dv.step(), 1)
                if w is not None:
                    dve.wait_ge(*dv.last)
                    tt(b3, b3, w.rearrange("p (o d) -> p o d", o=1).to_broadcast([P, n * nh, d]), ALU.mult).then_inc(dv.step(), 1)
                dve.wait_ge(*dv.last)

            def rope(x1, x2, cos, sin, t, to, out1=None, out2=None):
                tt(t[0], x1, cos, ALU.mult).then_inc(dv.step(), 1)
                tt(t[1], x2, sin, ALU.mult).then_inc(dv.step(), 1)
                tt(t[2], x2, cos, ALU.mult).then_inc(dv.step(), 1)
                tt(t[3], x1, sin, ALU.mult).then_inc(dv.step(), 1)
                dve.wait_ge(*dv.last)
                tt(out1 if out1 is not None else x1, t[0], t[1], ALU.subtract).then_inc(dv.step(), 1)
                tt(out2 if out2 is not None else x2, t[2], t[3], ALU.add).then_inc(dv.step(to), 1)

            r1 = con("rope1").rearrange("p (a b f) -> p a b f", a=2, b=TB)
            for buf, w, name in ((K1, "k_norm", "k1"), (Q1, "q_norm", "q1")):
                if name == "q1":
                    ada(4 * KT)
                dve.wait_ge(*evacuated((name, 1, 1)))
                head_norm(buf, par(w), TB, NH, HD, page(5, TB))
                for tb in range(TB):
                    b3 = buf[:, tb, :].rearrange("p (h d) -> p h d", d=HD)
                    c8 = [r1[:, a, tb:tb + 1, :].to_broadcast([P, NH, 8]) for a in range(2)]
                    t = [arena[:, 5, a * 128:(a + 1) * 128].rearrange("p (h f) -> p h f", h=NH) for a in range(4)]
                    rope(b3[:, :, 0:8], b3[:, :, 8:16], c8[0], c8[1], t, name + "_rope" if tb else None)
                    dve.wait_ge(*dv.last)
            ada(KT)

            def attention(name, heads, dvd, scale, O, gate=None):
                per = 512 // (TB * dvd)

                def gather(g):
                    p = (name, "O", g)
                    dve.wait_ge(*finished(p))
                    hs = slice(g * per, (g + 1) * per)
                    V.reciprocal(rs[:, hs, :], rs[:, hs, :]).then_inc(dv.step(), 1)
                    dve.wait_ge(*dv.last)
                    o = O[:, :, g * per * dvd:(g + 1) * per * dvd].rearrange("p b (h d) -> p h b d", d=dvd)
                    tt(o, bank(p)[:, :].rearrange("p (h b d) -> p h b d", h=per, b=TB),
                                  rs[:, hs, :].unsqueeze(3).to_broadcast([P, per, TB, dvd]), ALU.mult).then_inc(dv.frees(p), 1)

                done = 0
                for h in range(heads):
                    if h >= 2:
                        dve.wait_ge(sem(name + "_p"), h - 1)
                    dve.wait_ge(*finished((name, "S", h)))
                    tt(Ss[:, h % 2, :], bank((name, "S", h))[:, 0:3 * P], con("causal"), ALU.add).then_inc(dv.frees((name, "S", h)), 1)
                    dve.wait_ge(*dv.last)
                    V.tensor_reduce(mx[:, 0:1], Ss[:, h % 2, 0:P], AX.X, ALU.max).then_inc(dv.step(), 1)
                    V.tensor_reduce(mx[:, 1:2], Ss[:, h % 2, P:3 * P], AX.X, ALU.max).then_inc(dv.step(), 1)
                    dve.wait_ge(*dv.last)
                    ts(nmax[:, h, :], mx[:, 0:2], -scale, None, ALU.mult).then_inc(dv.step(name + "_max"), 1)
                    if (done + 1) * per <= h - 3:
                        gather(done)
                        done += 1
                while done * per < heads:
                    gather(done)
                    done += 1

            attention("at1", NH, HD, 0.125, O1)
            dve.wait_ge(*evacuated(("g1", 1, 1)))
            dve.wait_ge(*dv.last)
            tt(O1, O1, G1, ALU.mult).then_inc(dv.step("o1"), 1)
            add_to_x("wo_b")

            def modulation(first, last, modulated):
                dve.wait_ge(*evacuated(("ada", last - 1)))
                columns = slice(4 * first, 4 * last)
                tt(ADA[:, columns], ADA[:, columns], par("ada_b")[:, columns], ALU.add).then_inc(dv.step(), 1)
                dve.wait_ge(*dv.last)
                for m in modulated:
                    at, g = MOD_FROM[m]
                    stt(MODS[m][0], ADA[:, at:at + 8], 1.0, g, ALU.add, ALU.mult).then_inc(dv.step("mod"), 1)

            modulation(0, 12, (0, 1))

            def gate_row(i):
                at, g = GATE_FROM[i]
                tt(gcol, ADA[:, at:at + 8], g, ALU.mult).then_inc(dv.step(), 1)
                dve.wait_ge(*dv.last)
                for j in range(KT):
                    ts(DIAG[:, j, :], ident, gcol[:, j:j + 1], None, ALU.mult).then_inc(dv.step("diag"), 1)
                for half in range(2):
                    dve.wait_ge(*finished(("gb", i, half)))
                    V.tensor_copy(GB[:, i % 2, half * 512:(half + 1) * 512], bank(("gb", i, half))[:, :]).then_inc(dv.frees(("gb", i, half)), 1)
                dve.wait_ge(*dv.last)

            def post_norm(i, last, to=None):
                dve.wait_ge(*evacuated(last))
                for tb in range(TB):
                    V.tensor_tensor_reduce(XN[:, tb, :], Yb[:, tb, :], Yb[:, tb, :], 1.0, 0.0, ALU.mult, ALU.add,
                                                  accum_out=ss[:, tb:tb + 1]).then_inc(dv.step(), 1)
                dve.wait_ge(*dv.last)
                rsqrt(ss, ss, 1.0 / D, EPS)
                for tb in range(TB):
                    stt(Yb[:, tb, :], Yb[:, tb, :], ss[:, tb:tb + 1], GB[:, i % 2, :], ALU.mult, ALU.mult).then_inc(dv.step(), 1)
                dve.wait_ge(*dv.last)
                for tb in range(TB):
                    tt(X[:, tb, :], X[:, tb, :], Yb[:, tb, :], ALU.add).then_inc(dv.step(to), 1)
                dve.wait_ge(*dv.last)

            def mlp(l):
                for n in range(8):
                    for i in range(2):
                        dve.wait_ge(*evacuated(("up", l, n, i)))
                        if n >= 2 and i == 0:
                            dve.wait_ge(sem("mlp_down"), 7 * l + n - 1)
                        r = RL[:, n % 2, 2 * i:2 * i + 2, :]
                        tt(AF[:, n % 2, 2 * i:2 * i + 2, :], r, r, ALU.mult).then_inc(dv.step("relu2"), 1)
                        if l == 0 and n:
                            ada(KT)
                if l == 0:
                    ada(2 * KT)

            gate_row(0)
            gate_row(1)
            norm()
            dve.wait_ge(sem("gate_ln"), 1)
            stt(f_row[0:8, :], f_row[0:8, :], 0.0, t_row[0:8, :], ALU.min, ALU.subtract).then_inc(dv.step(), 1)
            dve.wait_ge(*dv.last)
            V.memset(ones_row[0:8, :], 1.0).then_inc(dv.step(), 1)
            dve.wait_ge(*dv.last)
            V.tensor_tensor_scan(b_row[0:8, :], ones_row[0:8, :], f_row[0:8, :], 0.0, ALU.mult, ALU.add).then_inc(dv.step(), 1)
            dve.wait_ge(*dv.last)
            tt(c_row[0:8, :], i_row[0:8, :], b_row[0:8, :], ALU.subtract).then_inc(dv.step(), 1)
            dve.wait_ge(*dv.last)
            V.tensor_tensor_scan(m_row[0:8, :], c_row[0:8, :], c_row[0:8, :], 0.0, ALU.max, ALU.max).then_inc(dv.step(), 1)
            dve.wait_ge(*dv.last)
            tt(mt_row[0:8, :], b_row[0:8, :], m_row[0:8, :], ALU.add).then_inc(dv.step("m_total"), 1)
            V.memset(V2[:, :, :, DV:DV + 1], 1.0).then_inc(dv.step(), 1)
            dve.wait_ge(*finished("gate_cols"))
            V.tensor_copy(gcols, bank("gate_cols")[:, 0:32].rearrange("p (b n) -> p b n", b=TB)).then_inc(dv.frees("gate_cols"), 1)
            dve.wait_ge(*dv.last)

            def finish_head(g):
                p = ("num", g)
                dve.wait_ge(*finished(p))
                nd = bank(p)[:, 0:258].rearrange("p (b n) -> p b n", b=TB)
                dve.wait_ge(*dv.last)
                ts(den, nd[:, :, DV:DV + 1], -1.0, None, ALU.mult).then_inc(dv.step(), 1)
                dve.wait_ge(*dv.last)
                tt(den, den, nd[:, :, DV:DV + 1], ALU.max).then_inc(dv.step(), 1)
                dve.wait_ge(*dv.last)
                tt(den, den, gcols[:, :, 8 + g:9 + g], ALU.max).then_inc(dv.step(), 1)
                dve.wait_ge(*dv.last)
                V.reciprocal(den, den).then_inc(dv.step(), 1)
                dve.wait_ge(*dv.last)
                tt(H2[:, :, g * DV:(g + 1) * DV], nd[:, :, 0:DV], den.to_broadcast([P, TB, DV]), ALU.mult).then_inc(dv.frees(p), 1)

            for h in range(MH + 1):
                if h < MH:
                    p = ("m", h)
                    dve.wait_ge(*finished(p))
                    late = con("late")
                    w = W2[:, h % 2, :]
                    stt(w[:, 0:P], bank(p)[:, 0:P], gcols[:, 0, h:h + 1], late, ALU.subtract, ALU.max).then_inc(dv.step(), 1)
                    ts(w[:, P:T], bank(p)[:, P:T], gcols[:, 0, h:h + 1], 0.0, ALU.subtract, ALU.max).then_inc(dv.step(), 1)
                    stt(w[:, T:T + P], bank(p)[:, P:T], gcols[:, 1, h:h + 1], late, ALU.subtract, ALU.max).then_inc(dv.frees(p), 1)
                if h >= 1:
                    g = h - 1
                    p = ("qk", g)
                    dve.wait_ge(*finished(p))
                    dve.wait_ge(sem("wexp"), g + 1)
                    if g >= 2:
                        dve.wait_ge(*finished(("num", g - 2)))
                    stt(PT2[:, g % 2, :], bank(p)[:, 0:3 * P], DKM ** -0.5, W2[:, g % 2, :], ALU.mult, ALU.mult).then_inc(dv.frees(p), 1)
                    dve.wait_ge(*dv.last)
                    if g >= 1:
                        finish_head(g - 1)
            finish_head(MH - 1)
            dve.wait_ge(*dv.last)
            head_norm(H2, None, TB, MH, DV, Yb)
            dve.wait_ge(*evacuated(("og", 1, 1)))
            tt(H2, H2, G1, ALU.mult).then_inc(dv.step("h2"), 1)
            post_norm(0, ("wo_c", 1, 1))
            norm()
            mlp(0)
            post_norm(1, ("mlp", 0, 1, 1))

            modulation(12, 28, (2, 3, 4))
            gate_row(2)
            gate_row(3)
            norm()
            dve.wait_ge(*evacuated(("ckv", 1)))
            sq = DIAGF
            for tb in range(TB):
                dve.wait_ge(*dv.last)
                V.tensor_tensor_reduce(sq[:, 0:KVL], CKVR[:, tb, 0:KVL], CKVR[:, tb, 0:KVL], 1.0, 0.0, ALU.mult,
                                              ALU.add, accum_out=ss[:, tb:tb + 1]).then_inc(dv.step(), 1)
            dve.wait_ge(*dv.last)
            rsqrt(ss, ss, 1.0 / KVL, EPS)
            for tb in range(TB):
                ts(CKV[:, tb, :], CKVR[:, tb, 0:KVL], ss[:, tb:tb + 1], None, ALU.mult).then_inc(dv.step(), 1)
            dve.wait_ge(sem("tables"), 2)
            cosb, sinb = rope2[:, 0], rope2[:, 1]
            t = [sq[:, 512 + a * 64:512 + (a + 1) * 64].rearrange("p (b f) -> p b f", b=TB) for a in range(4)]
            rope(CKVR[:, :, KVL:KVL + 32], CKVR[:, :, KVL + 32:KVL + 64], cosb, sinb, t, None, KR[:, :, 0:32], KR[:, :, 32:64])
            dve.wait_ge(*dv.last)
            V.tensor_copy(KR[:, :, 64:128], KR[:, :, 0:64]).then_inc(dv.step("ckv_n"), 1)
            dve.wait_ge(*evacuated(("cq", 1)))
            for tb in range(TB):
                dve.wait_ge(*dv.last)
                V.tensor_tensor_reduce(sq[:, 0:QL], CQ[:, tb, :], CQ[:, tb, :], 1.0, 0.0, ALU.mult,
                                              ALU.add, accum_out=ss[:, tb:tb + 1]).then_inc(dv.step(), 1)
            dve.wait_ge(*dv.last)
            rsqrt(ss, ss, 1.0 / QL, EPS)
            for tb in range(TB):
                ins = ts(CQ[:, tb, :], CQ[:, tb, :], ss[:, tb:tb + 1], None, ALU.mult)
                ins.then_inc(dv.step("cq_n" if tb else None), 1)
            dve.wait_ge(*evacuated(("qr", 1)))
            for tb in range(TB):
                b3 = QR[:, tb, :].rearrange("p (h d) -> p h d", d=RD)
                c32 = [rope2[:, a, tb:tb + 1, :].to_broadcast([P, MH, 32]) for a in range(2)]
                t = [sq[:, a * 256:(a + 1) * 256].rearrange("p (h f) -> p h f", h=MH) for a in range(4)]
                rope(b3[:, :, 0:32], b3[:, :, 32:64], c32[0], c32[1], t, "qr_rope" if tb else None)
                dve.wait_ge(*dv.last)
            attention("at3", MH, DV, MLA_SCALE, O3)
            post_norm(2, ("wo_d", 1, 1))
            norm()
            mlp(1)
            post_norm(3, ("mlp", 1, 1, 1), "final")
    return [name for name, _ in order]


def lay_out(order, w):
    def tiles(a, k=KT):
        n = a.shape[1]
        return a.reshape(k, P, n).transpose(1, 0, 2).reshape(P, k * n)

    wa, wi, wkv, wb = w["w_in_a"][0], w["a_w_in_2"][0], w["w_kv"], w["w_in_b"][0]
    ada = np.concatenate([w["ada_w_2"][0], w["kv_ada_w_2"], w["ada_w_2"][1]], 1)
    kvb = w["kv_w_b_2"].reshape(KVL, MH, 2 * DV)
    qb = w["b_w_q_b_2"][0].reshape(QL, MH, DV + RD)
    cut = {"k": wa[:, 1088:2112], "r": wa[:, 0:1024], "v": wa[:, 2112:3136], "g": wa[:, 3200:4224],
           "wo_a": w["w_out_a"][0], "k1": wkv[:, :D], "v1": wkv[:, D:], "q1": wb[:, :D], "g1": wb[:, D:],
           "wo_b": w["w_out_b"][0], "v2": wi[:, 1024:2048], "og": wi[:, 2064:3088], "wo_c": w["a_w_out_2"][0],
           "wo_d": w["b_w_out_2"][0], "ada": ada}
    out = np.zeros((len(order), P, SLOT), np.float32)
    for i, name in enumerate(order):
        if name == "lora":
            out[i, :, 0:512], out[i, :, 512:1024] = tiles(wa[:, 1024:1088]), tiles(wa[:, 3136:3200])
            out[i, 0:64, 1024:2048], out[i, 0:64, 2048:3072] = w["w2_a"][0], w["a2_a"][0]
        elif name in ("q2", "k2"):
            out[i] = tiles(wi[:, 512 * (name == "k2"):][:, :512])
        elif name == "kv_a":
            out[i, :, 0:2560] = tiles(w["kv_w_a_2"])
            out[i, :, 2560:4096] = tiles(qb[:, :, DV:].reshape(QL, 512), 3)
        elif name == "q_a":
            out[i, :, 0:3072] = tiles(w["b_w_q_a_2"][0])
        elif name == "kv_b":
            for half in range(2):
                hs = slice(4 * half, 4 * half + 4)
                out[i, :, half * 1024:(half + 1) * 1024] = tiles(kvb[:, hs, :DV].reshape(KVL, 512), 2)
                out[i, :, 2048 + half * 1024:3072 + half * 1024] = tiles(kvb[:, hs, DV:].reshape(KVL, 512), 2)
        elif name == "q_b":
            for half in range(2):
                out[i, :, half * 1536:(half + 1) * 1536] = tiles(qb[:, 4 * half:4 * half + 4, :DV].reshape(QL, 512), 3)
        elif name[0] == "w1":
            _, l, n = name
            out[i] = tiles(w["mlp_w1_2"][l][:, n * 512:(n + 1) * 512])
        elif name[0] == "w2":
            _, l, n = name
            out[i] = tiles(w["mlp_w2_2"][l][n * 512:(n + 1) * 512], 4)
        else:
            kind, n = name
            out[i] = tiles(cut[kind][:, n * 512:(n + 1) * 512])
    return out


def lay_out_parameters(w):
    out = np.zeros((P, NPARAM), np.float32)

    def put(name, a):
        at, n = PARAM[name]
        out[:a.shape[0], at:at + n] = a

    def col(a):
        return a.reshape(-1, P).T

    for name, key in (("norm_a", "norm_a"), ("mu", "mu_a"), ("w0", "w0_a"), ("a0", "a0_a"), ("kk", "kk_a"), ("ka", "ka_a"),
                      ("rk", "rk_a"), ("norm_kv", "norm_kv"), ("norm_b", "norm_b"), ("cond", "c_2"), ("norm2", "norm_g_2"),
                      ("kv_norm2", "kv_norm_g_2"), ("kv_latent", "kv_latent_g_2"), ("q_latent", "b_q_latent_g_2"),
                      ("head_g", "a_head_g_2")):
        put(name, col(w[key]))
    put("ada_b", col(np.concatenate([w["ada_b_2"][0], w["kv_ada_b_2"], w["ada_b_2"][1]])))
    put("gate_w", w["a_w_in_2"][0][:, 2048:2064].reshape(KT, P, 16).transpose(1, 0, 2).reshape(P, 128))
    put("gate_b", w["a_gate_b_2"][0].T)
    put("k_norm", np.broadcast_to(w["k_norm"], (P, HD)))
    put("q_norm", np.broadcast_to(w["q_norm_b"][0], (P, HD)))
    return out


PANELS = 95


def kernel(**inputs):
    import concourse.bacc as _bacc
    from concourse.bass_utils import run_bass_kernel_spmd as _run

    w = {k: np.asarray(v) for k, v in inputs.items()}
    nc = _bacc.Bacc("TRN2", target_bir_lowering=False, num_devices=1)
    arrays = {"x": w["x"], "consts": constants(), "params": lay_out_parameters(w),
              "positions": np.ascontiguousarray(w["positions_2"].reshape(TB, P).T),
              "gn": np.concatenate([w["gn_w_a"], w["gn_b_a"]]),
              "head_sel": np.ascontiguousarray(np.broadcast_to(np.eye(8, dtype=np.float32)[:, :, None], (8, 8, P)).reshape(8, 8 * P))}
    args = [nc.dram_tensor(f"in_{k}", a.shape, mybir.dt.from_np(a.dtype), kind="ExternalInput").ap()
            for k, a in arrays.items()]
    stream = nc.dram_tensor("in_stream", (PANELS, P, SLOT), F32, kind="ExternalInput").ap()
    out = nc.dram_tensor("out", (1, T, D), F32, kind="ExternalOutput").ap()
    order = build(nc, *args, stream, out)
    assert len(order) == PANELS
    feed = {f"in_{k}": a for k, a in arrays.items()}
    feed["in_stream"] = lay_out(order, w)
    r = _run(nc, [feed], core_ids=[0])
    return r.results[0]["out"]
```

```python
from contextlib import ExitStack

import concourse.bass as bass
import numpy as np
from concourse import mybir

F32 = mybir.dt.float32
I32 = mybir.dt.int32
F32R = mybir.dt.float32r
ALU = mybir.AluOpType
ACT = mybir.ActivationFunctionType
AX = mybir.AxisListType

P = 128
D = 1024
KT = D // P
T = 256
TB = T // P
HD = 64
NH = D // HD
LC = 64
NC_ = T // LC
EPS = 1e-6
GN_EPS = 64e-5
KAPPA = float(np.exp(-0.5))
NEG = -1e30
MH = 8
DKM = 64
DV = 128
KVL = 256
QL = 384
RD = 64
FF = 4 * D
SLOT = 4096
SLOTS = 4
PAGES = 15
ADA_PANELS = 28
MLA_SCALE = float((DV + RD) ** -0.5)
TWO_PI = 2.0 * np.pi
C1 = 6.28125
C2 = float(np.float32(np.round((TWO_PI - C1) * 2.0 ** 21) / 2.0 ** 21))
C3 = float(np.float32(TWO_PI - C1 - C2))
MAGIC = 12582912.0
PI_CLAMP = 3.1415925


def columns(*widths):
    at, out = 0, {}
    for name, w in widths:
        out[name] = (at, w)
        at += w
    return out, at


CONST, NCONST = columns(("ident", P), ("ones", P), ("pair_ones", P), ("pair_sel", 2), ("eye", LC),
                        ("level", 6 * LC), ("strict_incl", 2 * LC), ("scan_reset", T),
                        ("rope1", 2 * TB * 8), ("causal", 3 * P), ("late", P),
                        ("inv2", 32), ("zero", 1))
PARAM, NPARAM = columns(("norm_a", 8), ("mu", 48), ("w0", 8), ("a0", 8), ("kk", 8), ("ka", 8), ("rk", 8),
                        ("norm_kv", 8), ("norm_b", 8), ("cond", 8), ("ada_b", 112), ("norm2", 64),
                        ("kv_norm2", 8), ("kv_latent", 2), ("q_latent", 3), ("head_g", 8),
                        ("gate_w", 128), ("gate_b", 2), ("k_norm", HD), ("q_norm", HD))


def constants():
    out = np.zeros((P, NCONST), np.float32)

    def put(name, a):
        at, w = CONST[name]
        a = np.asarray(a, np.float32).reshape(a.shape[0], -1)
        out[:a.shape[0], at:at + w] = a

    p = np.arange(P)
    put("ident", np.eye(P))
    put("ones", np.ones((P, P)))
    put("pair_ones", (p[:, None] // HD == p[None, :] // HD) * 1.0)
    put("pair_sel", (p[:, None] // HD == np.arange(2)) * 1.0)
    s, t = (p % LC)[:, None], np.arange(LC)[None, :]
    put("eye", (s == t) * 1.0)
    put("level", np.stack([((s >> (l + 1)) == (t >> (l + 1))) & ((s >> l) % 2 == 0) & ((t >> l) % 2 == 1)
                           for l in range(6)], 1) * 1.0)
    put("strict_incl", np.stack([s < t, s <= t], 1) * 1.0)
    put("scan_reset", np.broadcast_to((np.arange(T) % LC != 0) * 1.0, (P, T)))
    inv = np.power(np.float32(500000.0), -np.arange(0, 16, 2, dtype=np.float32) / np.float32(16))
    ang = (np.arange(T, dtype=np.float32)[:, None] * inv[None, :]).astype(np.float64)
    tab = np.stack([np.cos(ang), np.sin(ang)]).reshape(2, TB, P, 8).transpose(2, 0, 1, 3)
    put("rope1", np.ascontiguousarray(tab))
    diag = np.where(p[None, :] <= p[:, None], 0.0, NEG)
    put("causal", np.concatenate([diag, np.zeros((P, P)), diag], 1))
    put("late", np.where(p[:, None] <= p[None, :], 0.0, -NEG))
    inv2 = np.power(np.float32(10000.0), -np.arange(32, dtype=np.float32) / np.float32(32))
    put("inv2", np.broadcast_to(inv2, (P, 32)))
    return out


def build(nc, x, cc_d, pc_d, pos_d, gn_d, sel_d, stream, out, debug=None):
    order = []
    with ExitStack() as ctx:
        def sb(name, shape, dt=F32):
            return ctx.enter_context(nc.sbuf_tensor(name, shape, dt))

        sems = {}

        def sem(name):
            if name not in sems:
                sems[name] = ctx.enter_context(nc.semaphore(name))
            return sems[name]

        banks = [ctx.enter_context(nc.psum_tensor(f"bank{b}", [P, 512], F32)) for b in range(8)]
        with ExitStack() as overlay:
            ring_parts, arena_parts = ([overlay.enter_context(nc.sbuf_tensor(f"{name}{n}", [P, size], F32R)) for n in range(count)]
                                       for name, count, size in (("slot_parts", SLOTS, SLOT), ("page_parts", PAGES, 2048)))
        ring = sb("ring", [P, SLOTS, SLOT])
        arena = sb("arena", [P, PAGES, 2048])
        cc = sb("cc", [P, NCONST])
        pc = sb("pc", [P, NPARAM])
        gn = sb("gn", [P, 2, D])
        small = sb("small", [P, 1352])
        pos_i = sb("pos_i", [P, TB], I32)

        def con(name):
            at, w = CONST[name]
            return cc[:, at:at + w]

        def par(name):
            at, w = PARAM[name]
            return pc[:, at:at + w]

        ident, ones = con("ident"), con("ones")

        def page(n, d0):
            return arena[:, n, :].rearrange("p (a b) -> p a b", a=d0)

        used = [0]

        def scratch(w):
            used[0] += w
            assert used[0] <= 1352
            return small[:, used[0] - w:used[0]]

        X = page(0, TB)
        XN = page(13, TB)

        counts = {}

        class Count:

            def __init__(self, own):
                self.own, self.last = own, None

            def step(self, name=None):
                s = sem(name or self.own)
                counts[s.name] = counts.get(s.name, 0) + 1
                self.last = (s, counts[s.name])
                return s

            def frees(self, product):
                self.last = evacuated(product)
                return self.last[0]

        def finished(product):
            b, turn = place[product]
            return sem(f"bank_full{b}"), turn + 1

        def evacuated(product):
            b, turn = place[product]
            return sem(f"bank_free{b}"), turn + 1

        place, turns, rotation = {}, {}, {"banks": list(range(8)), "at": 0}
        units, unit_of = [], {}
        ada_slots = []
        down_used = {}

        def bank(product):
            return banks[place[product][0]]

        Vr, Gr = page(1, TB), page(2, TB)
        AR = arena[:, 3:5, :].rearrange("p g b -> p (g b)").rearrange("p (j c a t) -> p j c a t", j=KT, c=NC_, a=2)
        khat, bhat, xx, hT = page(5, KT), page(6, KT), page(7, KT), page(8, KT)
        mix = [page(9, KT), page(10, KT)]
        LW, AA, KK, EE = page(11, KT), page(12, KT), page(13, KT), page(14, KT)
        EN, bonus_p = page(8, KT), page(9, KT)
        Kt, Bt = page(7, TB), page(10, TB)
        PK = arena[:, 11:13, :].rearrange("p g b -> p (g b)").rearrange("p (b h j a t) -> p b h j a t", b=TB, h=2, j=8, a=2)
        PB = arena[:, 8:10, :].rearrange("p g b -> p (g b)").rearrange("p (b h j a t) -> p b h j a t", b=TB, h=2, j=8, a=2)
        TI = page(13, 4).rearrange("p g (j t) -> p g j t", j=8)
        TTI = page(5, 4).rearrange("p g (j t) -> p g j t", j=8)
        XS = page(6, 4).rearrange("p g (j t) -> p g j t", j=8)
        CT = page(14, 4).rearrange("p g (j t) -> p g j t", j=8)
        SBD = arena[:, 6, 0:1024].rearrange("p (j v) -> p j v", j=8)
        Rs, Un = page(14, 2)[:, 0, :], page(14, 2)[:, 1, :]
        Yr = page(13, TB)
        YT = page(8, KT)
        ada_part = scratch(1024).rearrange("p (a n) -> p a n", a=2)
        lora = ada_part[:, 0, :].rearrange("p (a t) -> p a t", a=2)
        g_scan = ada_part[:, 1, 0:T]
        F = scratch(32).rearrange("p (j c) -> p j c", j=8)
        bonus = scratch(32).rearrange("p (b h) -> p b h", b=TB)
        one_m_ka = scratch(8)
        ss = scratch(2)
        stat = scratch(32).rearrange("p (b h) -> p b h", b=TB)
        stat2 = scratch(32).rearrange("p (b h) -> p b h", b=TB)
        cond = scratch(8)
        rs = scratch(32).rearrange("p (h b) -> p h b", b=TB)
        mx = scratch(4)
        h_sq = stat[:, 0, :].rearrange("p (b h) -> p b h", b=TB)
        y_sq, x_sq = stat2[:, 0, 0:4], stat2[:, 1, 0:2]
        rope2 = sb("rope2", [P, 2, TB, 32])
        ADA = sb("ADA", [P, 4 * ADA_PANELS])
        MOD = sb("MOD", [P, 5, 8])
        n2 = par("norm2")
        MOD_FROM = ((8, n2[:, 0:8]), (32, n2[:, 16:24]), (56, par("kv_norm2")), (72, n2[:, 32:40]), (96, n2[:, 48:56]))
        MODS = [(MOD[:, m, :], ADA[:, at:at + 8]) for m, at in enumerate((0, 24, 48, 64, 88))]
        GATE_FROM = ((16, n2[:, 8:16]), (40, n2[:, 24:32]), (80, n2[:, 40:48]), (104, n2[:, 56:64]))
        nmax = scratch(32).rearrange("p (h b) -> p h b", b=TB)
        gcol = scratch(8)
        den = scratch(2).rearrange("p (b o) -> p b o", b=TB)
        gcols = scratch(32).rearrange("p (b n) -> p b n", b=TB)
        mid = lora
        newton = scratch(64).rearrange("p (a n) -> p a n", a=2)
        GNT = page(6, 2)[:, 1:2, :]
        hkvT, hbT, K1, V1, Q1, G1 = page(7, KT), page(8, KT), page(3, TB), page(1, TB), page(4, TB), page(2, TB)
        K1T, O1, O1T = page(9, KT), page(6, TB), page(11, KT)

        def cols(n, a, b):
            return arena[:, n, a:b]

        Ss = cols(12, 0, 768).rearrange("p (a n) -> p a n", a=2)
        Ps = cols(12, 768, 1536).rearrange("p (a n) -> p a n", a=2)
        PTs = cols(14, 0, 768).rearrange("p (a n) -> p a n", a=2)
        Q1T_OF = [page(10, KT), page(3, KT)]
        hT2 = page(8, KT)
        Q2T_OF = [cols(9, 0, 1024).rearrange("p (j t) -> p j t", j=4), cols(10, 1024, 2048).rearrange("p (j t) -> p j t", j=4)]
        K2T = cols(10, 0, 1024).rearrange("p (j t) -> p j t", j=4)
        V2 = arena[:, 3:5, :].rearrange("p g b -> p (g b)")[:, 0:TB * MH * (DV + 1)].rearrange(
            "p (b h d) -> p b h d", b=TB, h=MH)
        H2, H2T, Yb, GB = page(6, TB), page(11, KT), page(7, TB), page(1, TB)
        i_row, f_row, t_row, b_row, c_row, m_row, mt_row, em_row = (cols(12, n * T, (n + 1) * T) for n in range(8))
        ones_row = cols(9, 1024, 1024 + T)
        W2 = cols(14, 0, 768).rearrange("p (a n) -> p a n", a=2)
        PT2 = cols(14, 768, 1536).rearrange("p (a n) -> p a n", a=2)
        head_sel = gn[0:8, 0, :]
        DIAGF = gn[:, 1, :]
        DIAG = DIAGF.rearrange("p (j n) -> p j n", j=8)
        AF = page(9, 2).rearrange("p a (k t) -> p a k t", k=4)
        Y_PAGES, O1_PAGES, H2_PAGES, O3_PAGES = (8, 9, 8), (11, 9, 11), (11, 5, 11), (11, 5, 11)
        HKV_PAGES, HB_PAGES, MLSTM_PAGES, MLP_PAGES = (7, 9, 7), (8, 10, 8), (8, 5, 7), (8, 5, 8)
        AF_HI, AF_LO = (arena_parts[n][:, :].rearrange("p (a k t) -> p a k t", a=2, k=4) for n in (6, 9))
        RL = page(10, 2).rearrange("p a (k t) -> p a k t", k=4)
        hkvT2 = page(12, KT)
        CKVR = cols(9, 0, 640).rearrange("p (b n) -> p b n", b=TB)
        CKV = cols(9, 640, 1152).rearrange("p (b n) -> p b n", b=TB)
        CKVT = cols(9, 1152, 1664).rearrange("p (j t) -> p j t", j=2)
        KR = cols(9, 1664, 1920).rearrange("p (b n) -> p b n", b=TB)
        CQ = cols(10, 0, 768).rearrange("p (b n) -> p b n", b=TB)
        CQT = cols(10, 768, 1536).rearrange("p (j t) -> p j t", j=3)
        KRT_OF = [cols(10, 1536, 1792), cols(10, 1792, 2048)]
        KNT, V3, QNT, O3, O3T = page(5, KT), page(3, TB), page(4, KT), page(6, TB), page(11, KT)
        QR = cols(2, 0, 1024).rearrange("p (b n) -> p b n", b=TB)
        QRT = cols(2, 1024, 2048).rearrange("p (j t) -> p j t", j=4)

        def pv_done(name, per, h):
            if h % per == per - 1:
                return finished((name, "O", h // per))
            return sem(name + "_pv"), h // per * (per - 1) + h % per + 1

        def unit_parts(u):
            unit = units[u]
            half, rows = unit["half"], unit["rows"]
            n = SLOT // rows // 2
            hi = arena_parts[unit["page"]][:, :].rearrange("p (k n) -> p k n", k=rows)
            lo = ring_parts[unit["slot"] % SLOTS][:, :].rearrange("p (k n) -> p k n", k=rows)
            return hi, lo[:, :, half * n:(half + 1) * n]

        def unit_values(u):
            unit = units[u]
            half, rows = unit["half"], unit["rows"]
            n = SLOT // rows // 2
            hi = arena_parts[unit["page"]][:, :].rearrange("p (k n) -> p k n", k=rows).bitcast(F32)
            lo = ring[:, unit["slot"] % SLOTS, :].rearrange("p (k n) -> p k n", k=rows)
            return hi, lo[:, :, half * n:(half + 1) * n]

        AHEAD = 2
        stage = [""]

        def ahead(product):
            u = unit_of[product]
            return max(v for v in range(u, min(u + AHEAD + 1, len(units))) if units[v]["stage"] == units[u]["stage"])

        def split_parts(pages):
            return [arena_parts[n][:, :].rearrange("p (k t) -> p k t", k=KT) for n in pages[1:]]

        block = ctx.enter_context(nc.Block())

        @block.tensor
        def _(pe):
            pn = Count("pe_steps")
            mm = nc.tensor.matmul
            panels = [0]

            def claim(product, banks_from=None):
                if banks_from is None:
                    b = rotation["banks"][rotation["at"] % len(rotation["banks"])]
                    rotation["at"] += 1
                else:
                    b = banks_from
                assert product not in place, product
                turn = turns.get(b, 0)
                turns[b] = turn + 1
                place[product] = (b, turn)
                if turn:
                    pe.wait_ge(sem(f"bank_free{b}"), turn)
                return banks[b]

            def filled(product):
                pn.last = finished(product)
                return pn.last[0]

            def panel(name):
                i = panels[0]
                panels[0] += 1
                order.append([name, None])
                pe.wait_ge(sem(f"slot_loaded{i % SLOTS}"), 16 * (i // SLOTS + 1))
                return ring[:, i % SLOTS, :]

            def panel_used():
                order[-1][1] = pn.last

            def wt(W, n):
                return W[:, 0:KT * n].rearrange("p (k n) -> p k n", k=KT)

            def project_T(name, weights, src, wait=None, k_tiles=KT, m_tiles=4):
                for i in range(m_tiles // 2):
                    b = claim((*name, i))
                    for half in range(2):
                        ct = 2 * i + half
                        for k in range(k_tiles):
                            if wait and i == half == 0:
                                pe.wait_ge(sem(wait[0]), wait[1] + k + 1)
                            ins = mm(b[:, half * T:(half + 1) * T], weights[:, k, ct * P:(ct + 1) * P], src[:, k, :],
                                     start=(k == 0), stop=(k == k_tiles - 1))
                    ins.then_inc(filled((*name, i)), 1)

            def split_panel(name, pages):
                order.append([name, None])
                i = panels[0]
                panels[0] += 1
                unit_of[name] = len(units)
                for half in range(2):
                    units.append({"slot": i, "half": half, "page": pages[len(units) % len(pages)], "rows": 4 if name[0] == "w2" else KT,
                                  "stage": stage[0]})

            def use_unit():
                u = unit_at[0]
                unit_at[0] += 1
                pe.wait_ge(sem("w_lo"), u + 1)
                return unit_parts(u)

            def unit_used(product=None):
                s = filled(product) if product else pn.step()
                units[unit_at[0] - 1]["used"] = pn.last
                if (unit_at[0] - 1) % 2:
                    order[-1][1] = pn.last
                return s

            unit_at = [0]

            def three(out, a, b, start, stop):
                mm(out, a[0], b[0], start=start, stop=False)
                mm(out, a[0], b[1], start=False, stop=False)
                return mm(out, a[1], b[0], start=False, stop=stop)

            def split_T(name, src, pages, wait=None, between=None):
                split_panel(name, pages)
                for i in range(2):
                    b = claim((*name, i))
                    W = use_unit()
                    unit_of[(*name, i)] = unit_at[0] - 1
                    for half in range(2):
                        for k in range(KT):
                            if wait and i == half == 0:
                                pe.wait_ge(sem(wait[0]), wait[1] + k // 2 + 1)
                            ins = three(b[:, half * T:(half + 1) * T], [w[:, k, half * P:(half + 1) * P] for w in W],
                                        [a[:, k, :] for a in src], k == 0, k == KT - 1)
                    ins.then_inc(unit_used((*name, i)), 1)
                    if between and i == 0:
                        between()

            def split_tok(name, src, pages, wait=None):
                split_panel(name, pages)
                bs = [claim((*name, tb)) for tb in range(TB)]
                for i in range(2):
                    W = use_unit()
                    for tb in range(TB):
                        unit_of[(*name, tb)] = unit_at[0] - 1
                        for k in range(KT):
                            if wait and i == tb == 0:
                                pe.wait_ge(sem(wait[0]), wait[1] + k // 2 + 1)
                            ins = three(bs[tb][:, i * 256:(i + 1) * 256], [a[:, k, tb * P:(tb + 1) * P] for a in src],
                                        [w[:, k, :] for w in W], k == 0, k == KT - 1)
                        if i == 1 and tb == 0:
                            ins.then_inc(filled((*name, 0)), 1)
                    ins.then_inc(unit_used((*name, 1) if i else None), 1)

            def project_tok(name, weights, src, n=512, k_tiles=KT, wait=None, transposed=None):
                for tb in range(TB):
                    b = claim((*name, tb))
                    for k in range(k_tiles):
                        if wait and tb == 0:
                            pe.wait_ge(sem(wait[0]), wait[1] + k + 1)
                        if transposed and tb == 0 and k % 2 == 0:
                            pe.wait_ge(*evacuated((transposed, k // 2)))
                        ins = mm(b[:, 0:n], src[:, k, tb * P:(tb + 1) * P], weights[:, k, 0:n],
                                 start=(k == 0), stop=(k == k_tiles - 1))
                    ins.then_inc(filled((*name, tb)), 1)

            def transposes(name, src, tiles=KT, ready=None):
                for i in range((tiles + 1) // 2):
                    b = claim((name, i))
                    if ready:
                        pe.wait_ge(*ready(i))
                    for jj in range(min(2, tiles - 2 * i)):
                        for tb in range(TB):
                            j = 2 * i + jj
                            ins = nc.tensor.transpose(b[:, jj * T + tb * P:jj * T + (tb + 1) * P],
                                                      src[:, tb, j * P:(j + 1) * P], ident)
                    ins.then_inc(filled((name, i)), 1)

            ada_at = {"taken": 0, "summed": 0}

            def ada_columns():
                i = ada_at["summed"]
                ada_at["summed"] += 1
                b = claim(("ada", i))
                pe.wait_ge(sem("ada_part"), i + 1)
                for ct in range(4):
                    ins = mm(b[:, ct * P:(ct + 1) * P], ada_part[:, i % 2, ct * P:(ct + 1) * P], ones,
                             start=True, stop=True)
                ins.then_inc(filled(("ada", i)), 1)

            def ada(n, rest=0, defer=False):
                for _ in range(n):
                    i = ada_at["taken"]
                    ada_at["taken"] += 1
                    ada_slots.append(panels[0])
                    panels[0] += 1
                    order.append([("ada", i), (sem("ada_part"), i + 1)])
                    if i - ada_at["summed"] >= 2 and not defer:
                        ada_columns()
                for _ in range(rest):
                    ada_columns()

            def attention(name, heads, dv, scores, V):
                per = 512 // (TB * dv)

                def score(h):
                    b = claim((name, "S", h))
                    scores(h, b).then_inc(filled((name, "S", h)), 1)

                def turn_p(h):
                    b = claim((name, "PT", h))
                    pe.wait_ge(sem(name + "_p"), h + 1)
                    for n in range(3):
                        ins = nc.tensor.transpose(b[:, n * P:(n + 1) * P], Ps[:, h % 2, n * P:(n + 1) * P], ident)
                    ins.then_inc(filled((name, "PT", h)), 1)

                def pv(h):
                    if h % per == 0:
                        claim((name, "O", h // per), 5 + h // per % 2)
                    b = bank((name, "O", h // per))
                    pe.wait_ge(*evacuated((name, "PT", h)))
                    o = (h % per) * TB * dv
                    mm(b[:, o:o + dv], PTs[:, h % 2, 0:P], V[:, 0, h * dv:(h + 1) * dv], start=True, stop=True)
                    for kb in range(2):
                        ins = mm(b[:, o + dv:o + 2 * dv], PTs[:, h % 2, (1 + kb) * P:(2 + kb) * P],
                                 V[:, kb, h * dv:(h + 1) * dv], start=(kb == 0), stop=(kb == 1))
                    if h % per == per - 1:
                        ins.then_inc(filled((name, "O", h // per)), 1)
                    else:
                        ins.then_inc(pn.step(name + "_pv"), 1)

                kept, rotation["banks"] = rotation["banks"], list(range(5))
                for h in range(heads + 2):
                    if h < heads:
                        score(h)
                    if 1 <= h <= heads:
                        turn_p(h - 1)
                    if h >= 2:
                        pv(h - 2)
                rotation["banks"] = kept

            pe.wait_ge(sem("loads"), 48)
            pe.wait_ge(sem("xn"), 2)
            transposes("hT_a", XN)
            W = panel("lora")
            b = claim("lora")
            for a in range(2):
                for k in range(KT):
                    pe.wait_ge(sem("mix"), 8 * a + k + 1)
                    ins = mm(b[0:64, a * T:(a + 1) * T], W[:, a * 512 + k * 64:a * 512 + (k + 1) * 64], mix[a][:, k, :],
                             start=(k == 0), stop=(k == KT - 1))
            ins.then_inc(filled("lora"), 1)
            pe.wait_ge(*evacuated("lora"))
            for j in range(KT):
                b = claim(("za", j))
                for a in range(2):
                    ins = mm(b[:, a * T:(a + 1) * T], W[0:64, 1024 + a * D + j * P:1024 + a * D + (j + 1) * P],
                             lora[0:64, a, :], start=True, stop=True)
                ins.then_inc(filled(("za", j)), 1)
            panel_used()
            for n, name in ((2, "k"), (3, "r")):
                for half in range(2):
                    project_T((name, half), wt(panel((name, half)), 512), mix[n % 2],
                              wait=("mix", 8 * n) if half == 0 else None)
                    panel_used()
            pe.wait_ge(sem("kk_sq"), 2)
            for i in range(4):
                b = claim(("kk_ss", i))
                for jj in range(2):
                    ins = mm(b[:, jj * T:(jj + 1) * T], con("pair_ones"), bhat[:, 2 * i + jj, :], start=True, stop=True)
                ins.then_inc(filled(("kk_ss", i)), 1)
            for n, name in ((4, "v"), (5, "g")):
                for half in range(2):
                    project_tok((name, half), wt(panel((name, half)), 512), mix[n % 2],
                                wait=("mix", 8 * n) if half == 0 else None)
                    panel_used()
            ada(2)
            pe.wait_ge(sem("bonus_p"), 1)
            b = claim("bonus")
            for j in range(KT):
                for tb in range(TB):
                    ins = mm(b[:, tb * NH + 2 * j:tb * NH + 2 * j + 2], bonus_p[:, j, tb * P:(tb + 1) * P], con("pair_sel"),
                             start=True, stop=True)
            ins.then_inc(filled("bonus"), 1)
            pe.wait_ge(sem("hats"), 1)
            for name, src in (("kt", khat), ("bt", bhat)):
                for i in range(4):
                    b = claim((name, i))
                    for tb in range(TB):
                        for jj in range(2):
                            ins = nc.tensor.transpose(b[:, tb * T + jj * P:tb * T + (jj + 1) * P],
                                                      src[:, 2 * i + jj, tb * P:(tb + 1) * P], ident)
                    ins.then_inc(filled((name, i)), 1)
            for tb in range(TB):
                for hp in range(2):
                    for jg in range(2):
                        for name, src in (("gk", khat), ("gb", bhat)):
                            b = claim((name, tb, hp, jg))
                            for jj in range(4):
                                j = 4 * jg + jj
                                for q in range(2):
                                    c = 2 * tb + q
                                    ins = mm(b[q * LC:(q + 1) * LC, jj * P:(jj + 1) * P],
                                             src[hp * HD:(hp + 1) * HD, j, c * LC:(c + 1) * LC],
                                             AR[hp * HD:(hp + 1) * HD, j, c, :, :].rearrange("p a t -> p (a t)"),
                                             start=True, stop=True)
                            ins.then_inc(filled((name, tb, hp, jg)), 1)

            def tiles64(product, lhs, rhs):
                b = claim(product)
                for j in range(8):
                    for q in range(2):
                        ins = mm(b[q * LC:(q + 1) * LC, j * LC:(j + 1) * LC], lhs(q, j), rhs(q, j), start=True, stop=True)
                ins.then_inc(filled(product), 1)

            def rows(buf, g):
                return lambda q, j: buf[q * LC:(q + 1) * LC, g, j, :]

            for g in range(4):
                pe.wait_ge(sem("tt"), g + 1)
                tiles64(("T0", g), rows(TTI, g), lambda q, j: con("eye")[q * LC:(q + 1) * LC, :])
            for l in range(1, 6):
                for g in range(4):
                    pe.wait_ge(sem("ct"), 4 * (l - 1) + g + 1)
                    if l == 1:
                        pe.wait_ge(*evacuated(("T0", g)))
                    else:
                        pe.wait_ge(*evacuated(("T", l - 1, g)))
                    tiles64(("X", l, g), rows(CT, g), rows(TI, g))
                ada(1)
                for g in range(4):
                    pe.wait_ge(*evacuated(("X", l, g)))
                    if l > 1:
                        pe.wait_ge(*evacuated(("TT", l - 1, g)))
                    if l < 5:
                        tiles64(("T", l, g), rows(TTI, g), rows(XS, g))
                    tiles64(("TT", l, g), rows(XS, g), rows(TTI, g))
                ada(1)
            for c in range(NC_):
                tb, q = c // 2, c % 2
                r0, r1 = q * LC, (q + 1) * LC
                for hg in range(2):
                    def from_state(b, a):
                        for jj in range(4):
                            mm(b[r0:r1, jj * P:(jj + 1) * P], AR[:, 4 * hg + jj, c, a, :], SBD[:, 4 * hg + jj, :],
                               start=(jj == 0), stop=False, skip_group_check=True)

                    b = claim(("R", c, hg))
                    if c:
                        pe.wait_ge(sem("state"), 2 * (c - 1) + hg + 1)
                        from_state(b, 0)
                    for jj in range(4):
                        for hp in range(2):
                            j = 4 * hg + jj
                            ins = mm(b[r0:r1, jj * P + hp * HD:jj * P + (hp + 1) * HD], PK[r0:r1, tb, hp, j, 0, :],
                                     Vr[r0:r1, tb, (2 * j + hp) * HD:(2 * j + hp + 1) * HD],
                                     start=(c == 0), stop=True, skip_group_check=True)
                    ins.then_inc(filled(("R", c, hg)), 1)
                for hg in range(2):
                    b = claim(("U", c, hg))
                    pe.wait_ge(*evacuated(("R", c, hg)))
                    if c == 0 and hg == 0:
                        for g in range(4):
                            pe.wait_ge(*evacuated(("TT", 5, g)))
                    for jj in range(4):
                        for hp in range(2):
                            j = 4 * hg + jj
                            o = (2 * j + hp) * HD
                            ins = mm(b[r0:r1, jj * P + hp * HD:jj * P + (hp + 1) * HD], TTI[r0:r1, 2 * tb + hp, j, :],
                                     Rs[r0:r1, o:o + HD], start=True, stop=True)
                    ins.then_inc(filled(("U", c, hg)), 1)
                for hg in range(2):
                    b = claim(("y", c, hg))
                    for jj in range(4 if c else 0):
                        mm(b[r0:r1, jj * P:(jj + 1) * P], AR[:, 4 * hg + jj, c, 1, :], SBD[:, 4 * hg + jj, :],
                           start=(jj == 0), stop=False, skip_group_check=True)
                for hg in range(2 if c < NC_ - 1 else 0):
                    pe.wait_ge(*evacuated(("U", c, hg)))
                    b = claim(("S", c, hg))
                    for jj in range(4):
                        j = 4 * hg + jj
                        mm(b[:, jj * P:(jj + 1) * P], Kt[r0:r1, tb, j * P:(j + 1) * P], Vr[r0:r1, tb, j * P:(j + 1) * P],
                           start=True, stop=False)
                        ins = mm(b[:, jj * P:(jj + 1) * P], Bt[r0:r1, tb, j * P:(j + 1) * P], Un[r0:r1, j * P:(j + 1) * P],
                                 start=False, stop=True)
                    ins.then_inc(filled(("S", c, hg)), 1)
                for hg in range(2):
                    b = bank(("y", c, hg))
                    pe.wait_ge(*evacuated(("U", c, hg)))
                    for jj in range(4):
                        for hp in range(2):
                            j = 4 * hg + jj
                            o = (2 * j + hp) * HD
                            dst = b[r0:r1, jj * P + hp * HD:jj * P + (hp + 1) * HD]
                            mm(dst, PK[r0:r1, tb, hp, j, 1, :], Vr[r0:r1, tb, o:o + HD],
                               start=(c == 0), stop=False, skip_group_check=True)
                            ins = mm(dst, PB[r0:r1, tb, hp, j, 1, :], Un[r0:r1, o:o + HD],
                                     start=False, stop=True, skip_group_check=True)
                    ins.then_inc(filled(("y", c, hg)), 1)
                if c == 0:
                    ada(0, rest=2)
            transposes("yT", Yr, ready=lambda i: (sem("y_gated"), 3 + i // 2))
            stage[0] = "attention"
            for half in range(2):
                split_tok(("wo_a", half), split_parts(Y_PAGES), (11, 12, 14), wait=("yT_split", 0) if half == 0 else None)

            pe.wait_ge(sem("xn"), 4)
            transposes("hT_b", XN)
            stage[0] = "attention"
            for name, src in (("k1", 0), ("v1", 0), ("q1", 1), ("g1", 1)):
                for half in range(2):
                    split_tok((name, half), split_parts((HKV_PAGES, HB_PAGES)[src]), (11, 12, 14),
                              wait=("hT_b_split", 0) if name == "k1" and half == 0 else None)
            pe.wait_ge(sem("k1_rope"), 1)
            transposes("k1T", K1)
            pe.wait_ge(sem("q1_rope"), 1)
            transposes("q1T", Q1)
            pe.wait_ge(*evacuated(("q1T", 3)))
            pe.wait_ge(sem("zeros"), 2)

            def scores1(h, b):
                j, q = h // 2, Q1T_OF[h % 2]
                mm(b[:, 0:P], q[:, j, 0:P], K1T[:, j, 0:P], start=True, stop=True)
                return mm(b[:, P:3 * P], q[:, j, P:T], K1T[:, j, :], start=True, stop=True)

            attention("at1", NH, HD, scores1, V1)
            pe.wait_ge(sem("o1"), 1)
            transposes("o1T", O1)
            stage[0] = "wo_b"
            for half in range(2):
                split_tok(("wo_b", half), split_parts(O1_PAGES), (3, 4, 5), wait=("o1T_split", 0) if half == 0 else None)

            def spread(i):
                for half in range(2):
                    b = claim(("gb", i, half))
                    for jj in range(4):
                        pe.wait_ge(sem("diag"), 8 * i + 4 * half + jj + 1)
                        ins = mm(b[:, jj * P:(jj + 1) * P], ones, DIAG[:, 4 * half + jj, :], start=True, stop=True)
                    ins.then_inc(filled(("gb", i, half)), 1)

            def mlp(l):
                stage[0] = f"mlp{l}"
                pe.wait_ge(sem("xn"), 8 + 4 * l)
                transposes(f"hT_m{l}", XN)
                rotation["banks"] = [4, 5, 6, 7]
                for tb in range(TB):
                    for half in range(2):
                        claim(("mlp", l, tb, half), 2 * tb + half)

                h = split_parts(MLP_PAGES)

                def up(n):
                    split_T(("up", l, n), h, (3, 4, 14), wait=(f"hT_m{l}_split", 0) if n == 0 else None,
                            between=ada_columns if l == 0 and n else None)

                def down(n):
                    split_panel(("w2", l, n), (3, 4, 14))
                    pe.wait_ge(sem("relu2"), 2 * (8 * l + n) + 2)
                    A = AF_HI[:, n % 2], AF_LO[:, n % 2]
                    for half in range(2):
                        W = use_unit()
                        for k in range(4):
                            for tb in range(TB):
                                ins = three(bank(("mlp", l, tb, half))[:, :], [a[:, k, tb * P:(tb + 1) * P] for a in A],
                                            [w[:, k, :] for w in W], n == 0 and k == 0, n == 7 and k == 3)
                                if n == 7 and k == 3 and tb == 0:
                                    ins.then_inc(filled(("mlp", l, 0, half)), 1)
                        ins.then_inc(unit_used(("mlp", l, 1, half) if n == 7 else None), 1)
                    down_used[l, n] = pn.last
                    for tb in range(TB):
                        for half in range(2):
                            unit_of["mlp", l, tb, half] = unit_at[0] - 1

                for n in range(9):
                    if n < 8:
                        up(n)
                        if l == 0:
                            ada(1, defer=True)
                    if n:
                        down(n - 1)
                if l == 0:
                    ada(0, rest=1)
                rotation["banks"] = list(range(8))

            rotation["banks"] = list(range(8))
            spread(0)
            spread(1)
            pe.wait_ge(sem("xn"), 6)
            transposes("hT_c", XN)
            stage[0] = "mlstm"
            for name in ("q2", "k2"):
                split_T((name,), split_parts(MLSTM_PAGES), (6, 11, 14), wait=("hT_c_split", 0) if name == "q2" else None)
            b = claim("gates")
            for a in range(2):
                for k in range(KT):
                    ins = mm(b[0:8, a * T:(a + 1) * T], par("gate_w")[:, k * 16 + a * 8:k * 16 + a * 8 + 8], hT2[:, k, :],
                             start=(k == 0), stop=(k == KT - 1))
            ins.then_inc(filled("gates"), 1)
            for name in ("v2", "og"):
                ada(1)
                for half in range(2):
                    split_tok((name, half), split_parts(MLSTM_PAGES), (6, 11, 14))
            ada(1)
            pe.wait_ge(sem("gate_rows"), 1)
            b = claim("gate_cols")
            for tb in range(TB):
                nc.tensor.transpose(b[:, tb * 16:tb * 16 + 8], c_row[0:8, tb * P:(tb + 1) * P], ident[0:8, 0:8])
                ins = nc.tensor.transpose(b[:, tb * 16 + 8:tb * 16 + 16], em_row[0:8, tb * P:(tb + 1) * P], ident[0:8, 0:8])
            ins.then_inc(filled("gate_cols"), 1)
            pe.wait_ge(*evacuated(("v2", 1, 1)))
            pe.wait_ge(sem("head_sel"), 16)
            pe.wait_ge(sem("zeros"), 4)
            for h in range(MH + 2):
                if h < MH:
                    b = claim(("m", h))
                    mm(b[:, 0:T], head_sel[:, h * P:(h + 1) * P], m_row[0:8, :], start=True, stop=True).then_inc(filled(("m", h)), 1)
                    b = claim(("qk", h))
                    j, q = h // 2, Q2T_OF[h % 2]
                    mm(b[:, 0:T], K2T[:, j, 0:P], q[:, j, :], start=True, stop=True)
                    mm(b[:, T:T + P], K2T[:, j, P:T], q[:, j, P:T], start=True, stop=True).then_inc(filled(("qk", h)), 1)
                if h >= 2:
                    g = h - 2
                    b = claim(("num", g))
                    pe.wait_ge(*evacuated(("qk", g)))
                    w = PT2[:, g % 2, :]
                    mm(b[:, 0:129], w[:, 0:P], V2[:, 0, g, :], start=True, stop=True)
                    mm(b[:, 129:258], w[:, P:T], V2[:, 0, g, :], start=True, stop=False)
                    mm(b[:, 129:258], w[:, T:T + P], V2[:, 1, g, :], start=False, stop=True).then_inc(filled(("num", g)), 1)
            transposes("h2T", H2, ready=lambda i: (sem("h2"), 1 + i // 2))
            stage[0] = "mlp0"
            for half in range(2):
                split_tok(("wo_c", half), split_parts(H2_PAGES), (3, 4, 14), wait=("h2T_split", 0) if half == 0 else None)
                if half == 0:
                    ada(1)
            ada(0, rest=2)
            mlp(0)

            spread(2)
            pe.wait_ge(sem("xn"), 10)
            transposes("hT_d", XN)
            project_tok(("cq",), wt(panel("q_a"), QL), hT2, n=QL, transposed="hT_d")
            panel_used()
            Wa = panel("kv_a")
            project_tok(("ckv",), wt(Wa, KVL + RD), hkvT2, n=KVL + RD)
            pe.wait_ge(sem("cq_n"), 1)
            transposes("cqT", CQ, tiles=3)
            project_tok(("qr",), Wa[:, 2560:4096].rearrange("p (k n) -> p k n", k=3), CQT, k_tiles=3, transposed="cqT")
            panel_used()
            pe.wait_ge(sem("ckv_n"), 1)
            b = claim("ckvT")
            for j in range(2):
                for tb in range(TB):
                    ins = nc.tensor.transpose(b[:, j * T + tb * P:j * T + (tb + 1) * P], CKV[:, tb, j * P:(j + 1) * P], ident)
            ins.then_inc(filled("ckvT"), 1)
            b = claim("krT")
            for tb in range(TB):
                ins = nc.tensor.transpose(b[:, tb * P:(tb + 1) * P], KR[:, tb, :], ident)
            ins.then_inc(filled("krT"), 1)
            Wn = panel("q_b")
            for half in range(2):
                project_T(("qn", half), Wn[:, half * 1536:(half + 1) * 1536].rearrange("p (k n) -> p k n", k=3), CQT, k_tiles=3)
            panel_used()
            Wb = panel("kv_b")
            pe.wait_ge(*evacuated("ckvT"))
            for half in range(2):
                project_T(("kn", half), Wb[:, half * 1024:(half + 1) * 1024].rearrange("p (k n) -> p k n", k=2), CKVT, k_tiles=2)
            for half in range(2):
                project_tok(("v3", half), Wb[:, 2048 + half * 1024:2048 + (half + 1) * 1024].rearrange("p (k n) -> p k n", k=2),
                            CKVT, k_tiles=2)
            panel_used()
            ada(4, defer=True)
            ada(0, rest=2)
            pe.wait_ge(sem("qr_rope"), 1)
            transposes("qrT", QR, tiles=4)
            pe.wait_ge(*evacuated(("qrT", 1)))

            def scores3(h, b):
                j, kr = h // 2, KRT_OF[h % 2]
                mm(b[:, 0:P], QNT[:, h, 0:P], KNT[:, h, 0:P], start=True, stop=False)
                mm(b[:, 0:P], QRT[:, j, 0:P], kr[:, 0:P], start=False, stop=True)
                mm(b[:, P:3 * P], QNT[:, h, P:T], KNT[:, h, :], start=True, stop=False)
                return mm(b[:, P:3 * P], QRT[:, j, P:T], kr, start=False, stop=True)

            pe.wait_ge(sem("zeros"), 6)
            attention("at3", MH, DV, scores3, V3)
            ada(0, rest=2)
            pe.wait_ge(*evacuated(("at3", "O", 3)))
            transposes("o3T", O3)
            stage[0] = "mlp1"
            for half in range(2):
                split_tok(("wo_d", half), split_parts(O3_PAGES), (3, 4, 14), wait=("o3T_split", 0) if half == 0 else None)
                if half == 0:
                    spread(3)
            mlp(1)

        @block.sync
        def _(sp):
            for tb in range(TB):
                sp.dma_start(X[:, tb, :], x[0, tb * P:(tb + 1) * P, :]).then_inc(sem(f"x_loaded{tb}"), 16)
            sp.wait_ge(sem("loads"), 48)
            for i, (name, released) in enumerate(order):
                if i >= SLOTS:
                    sp.wait_ge(*order[i - SLOTS][1])
                sp.dma_start(ring[:, i % SLOTS, :], stream[i]).then_inc(sem(f"slot_loaded{i % SLOTS}"), 16)
            for tb in range(TB):
                sp.wait_ge(sem("final"), tb + 1)
                sp.dma_start(out[0, tb * P:(tb + 1) * P, :], X[:, tb, :]).then_inc(sem("stored"), 16)
            sp.wait_ge(sem("stored"), 16 * TB)

        @block.gpsimd
        def _(pool):
            level = con("level").rearrange("p (l t) -> p l t", l=6)
            for l in range(1, 6):
                for g in range(4):
                    if l == 1:
                        pool.wait_ge(sem("tt"), g + 1)
                    else:
                        pool.wait_ge(*finished(("X", l - 1, g)))
                    nc.gpsimd.tensor_tensor(CT[:, g], PB[:, g // 2, g % 2, :, 0, :],
                                            level[:, l:l + 1, :].to_broadcast([P, 8, LC]), ALU.mult).then_inc(sem("ct"), 1)
            for g in range(4):
                pool.wait_ge(*finished(("TT", 5, g)))
            nc.gpsimd.memset(SBD, 0.0).then_inc(sem("state_zero"), 1)

            def zero_for_the_other(a):
                for n in range(2):
                    nc.gpsimd.memset(a[n][(1 - n) * HD:(2 - n) * HD], 0.0).then_inc(sem("zeros"), 1)

            pool.wait_ge(*finished(("k1T", 3)))
            zero_for_the_other(Q1T_OF)
            pool.wait_ge(*finished(("wo_b", 1, 1)))
            zero_for_the_other(Q2T_OF)
            pool.wait_ge(*finished(("mlp", 0, 1, 1)))
            zero_for_the_other(KRT_OF)

        @block.scalar
        def _(act_):
            ac = Count("act_steps")
            act = nc.scalar.activation

            act_.dma_start(cc[:, :], cc_d).then_inc(sem("loads"), 16)
            act_.dma_start(pc[:, :], pc_d).then_inc(sem("loads"), 16)
            act_.dma_start(pos_i[:, :], pos_d).then_inc(sem("loads"), 16)
            for a in range(2):
                act_.dma_start(gn[:, a, :], gn_d[a:a + 1, :].to_broadcast([P, D])).then_inc(sem("gn_rows"), 16)
            act_.wait_ge(sem("loads"), 48)
            act(cond, par("cond"), ACT.Silu).then_inc(ac.step("cond"), 1)

            def split(u):
                while ac_unit[0] <= u:
                    n = ac_unit[0]
                    ac_unit[0] += 1
                    unit = units[n]
                    act_.wait_ge(sem(f"slot_loaded{unit['slot'] % SLOTS}"), 16 * (unit["slot"] // SLOTS + 1))
                    if page_used.get(unit["page"]):
                        act_.wait_ge(*page_used[unit["page"]])
                    page_used[unit["page"]] = unit["used"]
                    act(unit_parts(n)[0], unit_values(n)[1], ACT.Copy).then_inc(ac.step("w_hi"), 1)

            ac_unit, page_used = [0], {}

            def x_squares(branch=None):
                for tb in range(TB):
                    if branch == "x":
                        act_.wait_ge(sem(f"x_loaded{tb}"), 16)
                    elif branch:
                        for half in range(2):
                            act_.wait_ge(*evacuated((branch, half, tb)))
                    else:
                        x_new[0] += 1
                        act_.wait_ge(sem("x_new"), x_new[0])
                    act(XN[:, tb, :], X[:, tb, :], ACT.Square, accum_out=x_sq[:, tb:tb + 1]).then_inc(ac.step("x_sq"), 1)

            def y_squares(products):
                for half in range(2):
                    for tb in range(TB):
                        p = products(half, tb)
                        split(ahead(p))
                        act_.wait_ge(*finished(p))
                        act(XN[:, tb, half * 512:(half + 1) * 512], bank(p)[:, :], ACT.Square,
                            accum_out=y_sq[:, 2 * tb + half:2 * tb + half + 1]).then_inc(ac.step("y_sq"), 1)

            x_new = [0]

            def copy(dst, product, n=512, **kw):
                if product in unit_of:
                    split(ahead(product))
                act_.wait_ge(*finished(product))
                act(dst, bank(product)[:, 0:n].rearrange("p (a b) -> p a b", a=dst.shape[1]) if len(dst.shape) == 3 else bank(product)[:, 0:n],
                               kw.get("func", ACT.Copy)).then_inc(ac.frees(product), 1)

            ada_at = {"taken": 0, "summed": 0}

            def ada_columns():
                i = ada_at["summed"]
                ada_at["summed"] += 1
                act_.wait_ge(*finished(("ada", i)))
                act(ADA[:, 4 * i:4 * i + 4], bank(("ada", i))[:, 0:512:P], ACT.Copy).then_inc(ac.frees(("ada", i)), 1)

            def ada(n, rest=0, defer=False):
                for _ in range(n):
                    i = ada_at["taken"]
                    ada_at["taken"] += 1
                    if i - ada_at["summed"] >= 2 and not defer:
                        ada_columns()
                for _ in range(rest):
                    ada_columns()

            def scaled(name, dst, scale, bias=None, tiles=KT):
                for i in range((tiles + 1) // 2):
                    act_.wait_ge(*finished((name, i)))
                    for jj in range(min(2, tiles - 2 * i)):
                        j = 2 * i + jj
                        ins = act(dst[:, j, :], bank((name, i))[:, jj * T:(jj + 1) * T], ACT.Identity,
                                  scale=scale[:, j:j + 1], bias=0.0 if bias is None else bias[:, j:j + 1])
                        if j % 2 == 1 or j == tiles - 1:
                            ins.then_inc(ac.frees((name, i)), 1)
                        else:
                            ins.then_inc(ac.step(), 1)

            def pair(dst, product, n=512):
                act_.wait_ge(*finished(product))
                for head in range(2):
                    r = slice(head * HD, (head + 1) * HD)
                    src = bank(product)[r, 0:n]
                    if len(dst[head].shape) == 3:
                        src = src.rearrange("p (a b) -> p a b", a=dst[head].shape[1])
                    act(dst[head][r], src, ACT.Copy).then_inc(ac.frees(product) if head else ac.step(), 1)

            def pairs(name, dst):
                for i in range(4):
                    pair([d[:, 2 * i:2 * i + 2, :] for d in dst], (name, i))

            def plain(name, dst, tiles=KT):
                for i in range((tiles + 1) // 2):
                    n = min(2, tiles - 2 * i)
                    copy(dst[:, 2 * i:2 * i + n, :], (name, i), n * T)

            x_squares("x")
            scaled("hT_a", hT, par("norm_a"))
            act_.wait_ge(sem("angles"), 1)
            for a in range(2):
                act(rope2[:, a], rope2[:, a], ACT.Sin).then_inc(ac.step("tables"), 1)
            act_.wait_ge(*finished("lora"))
            act(lora[0:64, 0, :], bank("lora")[0:64, 0:T], ACT.Tanh).then_inc(ac.step(), 1)
            act(lora[0:64, 1, :], bank("lora")[0:64, T:2 * T], ACT.Copy).then_inc(ac.frees("lora"), 1)
            for j in range(KT):
                act_.wait_ge(*finished(("za", j)))
                act(LW[:, j, :], bank(("za", j))[:, 0:T], ACT.Sigmoid, bias=par("w0")[:, j:j + 1]).then_inc(ac.step("sig"), 1)
                act(AA[:, j, :], bank(("za", j))[:, T:2 * T], ACT.Sigmoid, bias=par("a0")[:, j:j + 1]).then_inc(ac.frees(("za", j)), 1)
            for half in range(2):
                for i in range(2):
                    copy(khat[:, 4 * half + 2 * i:4 * half + 2 * i + 2, :], ("k", half, i))
            for h in range(2):
                act_.wait_ge(sem("kkr"), 4 * h + 4)
                act(bhat[:, 4 * h:4 * h + 4, :], KK[:, 4 * h:4 * h + 4, :], ACT.Square).then_inc(ac.step("kk_sq"), 1)
            for half in range(2):
                for i in range(2):
                    j = 4 * half + 2 * i
                    act_.wait_ge(*finished(("r", half, i)))
                    for jj in range(2):
                        ins = act(AR[:, j + jj, :, 1, :], bank(("r", half, i))[:, jj * T:(jj + 1) * T].rearrange("p (c t) -> p c t", c=4), ACT.Copy)
                        if jj == 0:
                            ins.then_inc(ac.step(), 1)
                    ins.then_inc(ac.frees(("r", half, i)), 1)
            for i in range(4):
                copy(bhat[:, 2 * i:2 * i + 2, :], ("kk_ss", i), func=ACT.Sqrt)
            for half in range(2):
                for tb in range(TB):
                    copy(Vr[:, tb, half * 512:(half + 1) * 512], ("v", half, tb))
            act_.wait_ge(sem("mix"), 48)
            for h in range(2):
                s = slice(4 * h, 4 * h + 4)
                act_.wait_ge(sem("cum"), 4 * h + 4)
                act(EN[:, s, :], EE[:, s, :], ACT.Exp, scale=KAPPA).then_inc(ac.step(), 1)
                act(LW[:, s, :], LW[:, s, :], ACT.Exp, scale=-KAPPA).then_inc(ac.step(), 1)
                act_.wait_ge(*ac.last)
                act(EE[:, s, :], EE[:, s, :], ACT.Exp, scale=-KAPPA).then_inc(ac.step("exps"), 1)
            act(F[:, :, 0:3], F[:, :, 0:3], ACT.Exp, scale=-KAPPA).then_inc(ac.step("exps"), 1)
            for half in range(2):
                for tb in range(TB):
                    copy(Gr[:, tb, half * 512:(half + 1) * 512], ("g", half, tb), func=ACT.Silu)
            ada(2)
            for name, dst in (("kt", Kt), ("bt", Bt)):
                for i in range(4):
                    copy(dst[:, :, i * T:(i + 1) * T], (name, i))
            for g in range(4):
                copy(TI[:, g].rearrange("p j t -> p (j t)"), ("T0", g))
            for l in range(1, 6):
                for g in range(4):
                    copy(XS[:, g].rearrange("p j t -> p (j t)"), ("X", l, g))
                ada(2)
            for c in range(NC_):
                tb, q = c // 2, c % 2
                r = slice(q * LC, (q + 1) * LC)
                for hg in range(2):
                    act_.wait_ge(*finished(("U", c, hg)))
                    act(Un[r, hg * 512:(hg + 1) * 512], bank(("U", c, hg))[r, :], ACT.Copy, scale=-1.0).then_inc(ac.frees(("U", c, hg)), 1)
                for hg in range(2):
                    act_.wait_ge(*finished(("y", c, hg)))
                    act(Yr[r, tb, hg * 512:(hg + 1) * 512], bank(("y", c, hg))[r, :], ACT.Copy).then_inc(ac.frees(("y", c, hg)), 1)
                if c == 0:
                    ada(0, rest=2)
            page_used.update({p: finished(("y", NC_ - 1, 1)) for p in (11, 12, 14)})
            split(unit_of["wo_a", 0] + 1)
            plain("yT", YT)

            def attention(name, heads, dv, scale):
                for h in range(heads + 1):
                    if h < heads:
                        if h >= 2:
                            act_.wait_ge(*finished((name, "PT", h - 2)))
                        act_.wait_ge(sem(name + "_max"), h + 1)
                        act(Ps[:, h % 2, 0:P], Ss[:, h % 2, 0:P], ACT.Exp, scale=scale, bias=nmax[:, h, 0:1],
                                   accum_out=rs[:, h, 0:1]).then_inc(ac.step(), 1)
                        act(Ps[:, h % 2, P:3 * P], Ss[:, h % 2, P:3 * P], ACT.Exp, scale=scale, bias=nmax[:, h, 1:2],
                                   accum_out=rs[:, h, 1:2]).then_inc(ac.step(name + "_p"), 1)
                    if h >= 1:
                        if h >= 3:
                            act_.wait_ge(*pv_done(name, 512 // (TB * dv), h - 3))
                        copy(PTs[:, (h - 1) % 2, :], (name, "PT", h - 1), 3 * P)

            split(unit_of["k1", 0])
            x_squares("wo_a")
            split(unit_of["k1", 0] + AHEAD)
            for i in range(4):
                act_.wait_ge(*finished(("hT_b", i)))
                for jj in range(2):
                    j = 2 * i + jj
                    for n, (dst, w) in enumerate(((hkvT, "norm_kv"), (hbT, "norm_b"))):
                        ins = act(dst[:, j, :], bank(("hT_b", i))[:, jj * T:(jj + 1) * T], ACT.Copy, scale=par(w)[:, j:j + 1])
                        if (jj, n) == (1, 1):
                            ins.then_inc(ac.frees(("hT_b", i)), 1)
                        else:
                            ins.then_inc(ac.step(), 1)
            for name, dst, f in (("k1", K1, ACT.Copy), ("v1", V1, ACT.Copy), ("q1", Q1, ACT.Copy), ("g1", G1, ACT.Silu)):
                for half in range(2):
                    for tb in range(TB):
                        copy(dst[:, tb, half * 512:(half + 1) * 512], (name, half, tb), func=f)
            plain("k1T", K1T)
            pairs("q1T", Q1T_OF)
            attention("at1", NH, HD, 0.125)
            page_used.update({3: finished(("at1", "S", NH - 1)), 4: finished(("q1T", 3)), 5: finished(("q1T", 3))})
            split(unit_of["wo_b", 0] + AHEAD)
            plain("o1T", O1T)
            split(unit_of["wo_b", 1] + 1)

            def mod_scaled(name, which, dst):
                act_.wait_ge(sem("mod"), which + 1)
                scaled(name, dst, MODS[which][0], MODS[which][1])

            def mlp(l):
                split(unit_of["up", l, 0, 0] + AHEAD)
                mod_scaled(f"hT_m{l}", (1, 4)[l], hT2)
                for n in range(8):
                    for i in range(2):
                        p = ("up", l, n, i)
                        m = 2 * (8 * l + n) + i
                        split(ahead(p))
                        act_.wait_ge(*finished(p))
                        if n >= 2 and i == 0:
                            act_.wait_ge(*down_used[l, n - 2])
                        act(RL[:, n % 2, 2 * i:2 * i + 2, :], bank(p)[:, :].rearrange("p (a t) -> p a t", a=2), ACT.Relu).then_inc(ac.frees(p), 1)
                        act_.wait_ge(*ac.last)
                        act(AF[:, n % 2, 2 * i:2 * i + 2, :], RL[:, n % 2, 2 * i:2 * i + 2, :], ACT.Square).then_inc(ac.step(), 1)
                        act_.wait_ge(*ac.last)
                        act(AF_HI[:, n % 2, 2 * i:2 * i + 2, :], AF[:, n % 2, 2 * i:2 * i + 2, :],
                            ACT.Copy).then_inc(ac.step("squared"), 1)
                        if l == 0 and n and i == 0:
                            ada_columns()
                    if l == 0:
                        ada(1, defer=True)
                split(unit_of["mlp", l, 1, 1])
                if l == 0:
                    ada_columns()
                y_squares(lambda half, tb: ("mlp", l, tb, half))
                if l == 0:
                    x_squares()

            act_.wait_ge(sem("y_gated"), 4)
            act_.dma_start(head_sel, sel_d).then_inc(sem("head_sel"), 16)
            page_used.update({p: finished(("wo_b", 1, 1)) for p in (6, 11, 14)})
            x_squares("wo_b")
            split(ahead(("q2", 0)))
            mod_scaled("hT_c", 0, hT2)
            for i in range(2):
                split(ahead(("q2", i)))
                pair([d[:, 2 * i:2 * i + 2, :] for d in Q2T_OF], ("q2", i))
            for i in range(2):
                copy(K2T[:, 2 * i:2 * i + 2, :], ("k2", i))
            gb = par("gate_b")
            act_.wait_ge(*finished("gates"))
            act(i_row[0:8, :], bank("gates")[0:8, 0:T], ACT.Identity, bias=gb[0:8, 0:1]).then_inc(ac.step(), 1)
            act(f_row[0:8, :], bank("gates")[0:8, T:2 * T], ACT.Identity, bias=gb[0:8, 1:2]).then_inc(ac.step("gate_if"), 1)
            act(t_row[0:8, :], bank("gates")[0:8, T:2 * T], ACT.Abs, bias=gb[0:8, 1:2]).then_inc(ac.frees("gates"), 1)
            act_.wait_ge(*ac.last)
            act(t_row[0:8, :], t_row[0:8, :], ACT.Exp, scale=-1.0).then_inc(ac.step(), 1)
            act_.wait_ge(*ac.last)
            act(t_row[0:8, :], t_row[0:8, :], ACT.Ln, bias=1.0).then_inc(ac.step("gate_ln"), 1)
            ada(1)
            for half in range(2):
                for tb in range(TB):
                    copy(V2[:, tb, 4 * half:4 * half + 4, 0:DV], ("v2", half, tb))
            ada(1)
            act_.wait_ge(sem("m_total"), 1)
            act(em_row[0:8, :], mt_row[0:8, :], ACT.Exp, scale=-1.0).then_inc(ac.step("gate_rows"), 1)
            for half in range(2):
                for tb in range(TB):
                    copy(G1[:, tb, half * 512:(half + 1) * 512], ("og", half, tb), func=ACT.Sigmoid)
            ada(1)

            def h_squares(g):
                act_.wait_ge(*evacuated(("num", g)))
                for tb in range(TB):
                    act(Yb[:, tb, g * DV:(g + 1) * DV], H2[:, tb, g * DV:(g + 1) * DV], ACT.Square,
                        accum_out=h_sq[:, tb, g:g + 1]).then_inc(ac.step("h_sq"), 1)

            for h in range(MH):
                act_.wait_ge(*evacuated(("m", h)))
                act(W2[:, h % 2, :], W2[:, h % 2, :], ACT.Exp, scale=-1.0).then_inc(ac.step("wexp"), 1)
                if h >= 2:
                    h_squares(h - 2)
            h_squares(MH - 2)
            h_squares(MH - 1)
            page_used.update({p: finished(("num", MH - 1)) for p in (3, 4, 14)})
            split(unit_of["wo_c", 0] + AHEAD)
            scaled("h2T", H2T, par("head_g"))
            split(unit_of["wo_c", 1] + 1)
            ada(1)
            y_squares(lambda half, tb: ("wo_c", half, tb))
            ada(0, rest=2)
            x_squares()
            mlp(0)

            act_.wait_ge(sem("mod"), 4)
            for i in range(4):
                act_.wait_ge(*finished(("hT_d", i)))
                for jj in range(2):
                    j = 2 * i + jj
                    for n, (dst, m) in enumerate(((hkvT2, 2), (hT2, 3))):
                        ins = act(dst[:, j, :], bank(("hT_d", i))[:, jj * T:(jj + 1) * T], ACT.Identity,
                                  scale=MODS[m][0][:, j:j + 1], bias=MODS[m][1][:, j:j + 1])
                        if (jj, n) == (1, 1):
                            ins.then_inc(ac.frees(("hT_d", i)), 1)
                        else:
                            ins.then_inc(ac.step(), 1)
            for tb in range(TB):
                copy(CQ[:, tb, :], ("cq", tb), QL)
            for tb in range(TB):
                copy(CKVR[:, tb, :], ("ckv", tb), KVL + RD)
            scaled("cqT", CQT, par("q_latent"), tiles=3)
            for tb in range(TB):
                copy(QR[:, tb, :], ("qr", tb))
            act_.wait_ge(*finished("ckvT"))
            for j in range(2):
                ins = act(CKVT[:, j, :], bank("ckvT")[:, j * T:(j + 1) * T], ACT.Copy, scale=par("kv_latent")[:, j:j + 1])
                if j == 0:
                    ins.then_inc(ac.step(), 1)
            ins.then_inc(ac.frees("ckvT"), 1)
            pair(KRT_OF, "krT", T)
            for half in range(2):
                for i in range(2):
                    copy(QNT[:, 4 * half + 2 * i:4 * half + 2 * i + 2, :], ("qn", half, i))
            for half in range(2):
                for i in range(2):
                    copy(KNT[:, 4 * half + 2 * i:4 * half + 2 * i + 2, :], ("kn", half, i))
            for half in range(2):
                for tb in range(TB):
                    copy(V3[:, tb, half * 512:(half + 1) * 512], ("v3", half, tb))
            ada(4, defer=True)
            ada(0, rest=2)
            plain("qrT", QRT, tiles=4)
            attention("at3", MH, DV, MLA_SCALE)
            ada(0, rest=2)
            page_used.update({p: finished(("at3", "O", 3)) for p in (3, 4, 14)})
            split(unit_of["wo_d", 0] + AHEAD)
            plain("o3T", O3T)
            y_squares(lambda half, tb: ("wo_d", half, tb))
            x_squares()
            mlp(1)

        @block.vector
        def _(dve):
            dv = Count("dve_steps")
            V = nc.vector
            tt, ts, stt = V.tensor_tensor, V.tensor_scalar, V.scalar_tensor_tensor

            def rsqrt(dst, src, mul, eps):
                ts(dst, src, mul, eps, ALU.mult, ALU.add).then_inc(dv.step(), 1)
                dve.wait_ge(*dv.last)
                w = dst.shape[-1]
                y, z = newton[:, 0, 0:w], newton[:, 1, 0:w]
                ts(z.bitcast(I32), dst.bitcast(I32), 1, None, ALU.logical_shift_right).then_inc(dv.step(), 1)
                dve.wait_ge(*dv.last)
                ts(y.bitcast(I32), z.bitcast(I32), -1.0, float(0x5F3759DF), ALU.mult, ALU.add).then_inc(dv.step(), 1)
                dve.wait_ge(*dv.last)
                for step in range(3):
                    tt(z, y, y, ALU.mult).then_inc(dv.step(), 1)
                    dve.wait_ge(*dv.last)
                    stt(z, z, -0.5, dst, ALU.mult, ALU.mult).then_inc(dv.step(), 1)
                    dve.wait_ge(*dv.last)
                    stt(dst if step == 2 else y, z, 1.5, y, ALU.add, ALU.mult).then_inc(dv.step(), 1)
                    dve.wait_ge(*dv.last)

            norms = [0]

            def norm():
                norms[0] += TB
                dve.wait_ge(sem("x_sq"), norms[0])
                rsqrt(ss, x_sq, 1.0 / D, EPS)
                for tb in range(TB):
                    ts(XN[:, tb, :], X[:, tb, :], ss[:, tb:tb + 1], None, ALU.mult).then_inc(dv.step("xn"), 1)

            def add_to_x(name):
                for half in range(2):
                    for tb in range(TB):
                        s = X[:, tb, half * 512:(half + 1) * 512]
                        dve.wait_ge(*finished((name, half, tb)))
                        tt(s, s, bank((name, half, tb))[:, :], ALU.add).then_inc(dv.frees((name, half, tb)), 1)
                dve.wait_ge(*dv.last)

            ada_at = [0]

            def ada(n):
                for _ in range(n):
                    i, k = divmod(ada_at[0], KT)
                    ada_at[0] += 1
                    slot, part = ada_slots[i], ada_part[:, i % 2, :]
                    if k == 0:
                        if i >= 2:
                            dve.wait_ge(*finished(("ada", i - 2)))
                        dve.wait_ge(sem(f"slot_loaded{slot % SLOTS}"), 16 * (slot // SLOTS + 1))
                        dve.wait_ge(*dv.last)
                    else:
                        dve.wait_ge(sem("ada_sum"), (KT - 1) * i + k)
                    W = ring[:, slot % SLOTS, k * 512:(k + 1) * 512]
                    if k == 0:
                        ts(part, W, cond[:, 0:1], None, ALU.mult).then_inc(dv.step("ada_sum"), 1)
                    else:
                        stt(part, W, cond[:, k:k + 1], part, ALU.mult, ALU.add).then_inc(
                            dv.step("ada_part" if k == KT - 1 else "ada_sum"), 1)

            dv_unit = [0]

            def split(u):
                while dv_unit[0] <= u:
                    n = dv_unit[0]
                    dv_unit[0] += 1
                    hi, lo = unit_values(n)
                    dve.wait_ge(sem("w_hi"), n + 1)
                    tt(unit_parts(n)[1], lo, hi, ALU.subtract).then_inc(dv.step("w_lo"), 1)
                    n -= unit_of["up", 0, 0, 0]
                    if n in (1, 2) or 4 <= n < 32 and n % 4 < 2:
                        ada(KT // 2)

            def next_unit(product):
                n = dv_unit[0]
                if n < len(units) and units[n]["stage"] == units[unit_of[product]]["stage"]:
                    split(n)
                    return n - unit_of[product]
                return -1

            def split_output(name, transposed, pages):
                split(unit_of[name, 0])
                split_h(transposed, pages)
                split(unit_of[name, 1] + 1)

            def split_h(name, *buffers):
                for i in range(4):
                    js = slice(2 * i, 2 * i + 2)
                    dve.wait_ge(*evacuated((name, i)))
                    for n, pages in enumerate(buffers):
                        value = page(pages[0], KT)[:, js, :]
                        hi, lo = (a[:, js, :] for a in split_parts(pages))
                        V.tensor_copy(hi, value).then_inc(dv.step(), 1)
                        dve.wait_ge(*dv.last)
                        tt(lo, value, hi.bitcast(F32), ALU.subtract).then_inc(
                            dv.step(name + "_split" if n == len(buffers) - 1 else None), 1)

            for tb in range(TB):
                dve.wait_ge(sem(f"x_loaded{tb}"), 16)
            norm()
            dve.wait_ge(sem("loads"), 48)
            dve.wait_ge(sem("cond"), 1)
            ts(one_m_ka, par("ka"), -1.0, 1.0, ALU.mult, ALU.add).then_inc(dv.step(), 1)
            ang, n_, r_ = (EE[:, a, 0:64].rearrange("p (b f) -> p b f", b=TB) for a in range(3))
            dve.wait_ge(*dv.last)
            V.tensor_copy(ss, pos_i[:, :]).then_inc(dv.step(), 1)
            dve.wait_ge(*dv.last)
            for tb in range(TB):
                ts(ang[:, tb, :], con("inv2"), ss[:, tb:tb + 1], None, ALU.mult).then_inc(dv.step(), 1)
            dve.wait_ge(*dv.last)
            ts(n_, ang, 1.0 / TWO_PI, MAGIC, ALU.mult, ALU.add).then_inc(dv.step(), 1)
            dve.wait_ge(*dv.last)
            ts(n_, n_, -MAGIC, None, ALU.add).then_inc(dv.step(), 1)
            dve.wait_ge(*dv.last)
            stt(r_, n_, -C1, ang, ALU.mult, ALU.add).then_inc(dv.step(), 1)
            dve.wait_ge(*dv.last)
            stt(r_, n_, -C2, r_, ALU.mult, ALU.add).then_inc(dv.step(), 1)
            dve.wait_ge(*dv.last)
            stt(r_, n_, -C3, r_, ALU.mult, ALU.add).then_inc(dv.step(), 1)
            dve.wait_ge(*dv.last)
            ts(rope2[:, 1], r_, PI_CLAMP, -PI_CLAMP, ALU.min, ALU.max).then_inc(dv.step(), 1)
            dve.wait_ge(*dv.last)
            ts(rope2[:, 0], rope2[:, 1], -1.0, None, ALU.mult).then_inc(dv.step(), 1)
            dve.wait_ge(*dv.last)
            tt(rope2[:, 0], rope2[:, 0], rope2[:, 1], ALU.min).then_inc(dv.step(), 1)
            dve.wait_ge(*dv.last)
            ts(rope2[:, 0], rope2[:, 0], float(np.pi / 2), None, ALU.add).then_inc(dv.step("angles"), 1)
            dve.wait_ge(*evacuated(("hT_a", 3)))
            tt(xx[:, :, 1:T], hT[:, :, 0:T - 1], hT[:, :, 1:T], ALU.subtract).then_inc(dv.step(), 1)
            ts(xx[:, :, 0:1], hT[:, :, 0:1], -1.0, None, ALU.mult).then_inc(dv.step(), 1)
            dve.wait_ge(*dv.last)
            last_use = {2: "lora", 3: "lora", 4: ("k", 1, 1), 5: ("r", 1, 1)}

            def mixes(n, which):
                if n in last_use:
                    dve.wait_ge(*finished(last_use[n]))
                mu = par("mu")[:, 8 * which:8 * which + 8]
                for j in range(KT):
                    stt(mix[n % 2][:, j, :], xx[:, j, :], mu[:, j:j + 1], hT[:, j, :], ALU.mult, ALU.add).then_inc(dv.step("mix"), 1)

            for n, which in enumerate((1, 4, 2, 0)):
                mixes(n, which)
            for j in range(KT):
                dve.wait_ge(*evacuated(("k", j // 4, (j % 4) // 2)))
                ts(KK[:, j, :], khat[:, j, :], par("kk")[:, j:j + 1], None, ALU.mult).then_inc(dv.step("kkr"), 1)
            mixes(4, 3)
            dve.wait_ge(*evacuated(("za", 7)))
            scan = g_scan.rearrange("p (c t) -> p c t", c=NC_)
            for j in range(KT):
                dve.wait_ge(*dv.last)
                V.tensor_tensor_scan(g_scan, con("scan_reset"), LW[:, j, :], 0.0, ALU.mult, ALU.add).then_inc(dv.step(), 1)
                dve.wait_ge(*dv.last)
                e = EE[:, j, :].rearrange("p (c t) -> p c t", c=NC_)
                tt(e, scan, scan[:, :, 31:32].to_broadcast([P, NC_, LC]), ALU.subtract).then_inc(dv.step(), 1)
                dve.wait_ge(*dv.last)
                tt(F[:, j, 0:3], e[:, 0:3, 63], scan[:, 1:4, 31], ALU.add).then_inc(dv.step(), 1)
                tt(LW[:, j, :], EE[:, j, :], LW[:, j, :], ALU.subtract).then_inc(dv.step("cum"), 1)
            for j in range(KT):
                ts(mid[:, j % 2, :], AA[:, j, :], par("ka")[:, j:j + 1], one_m_ka[:, j:j + 1], ALU.mult, ALU.add).then_inc(dv.step(), 1)
                dve.wait_ge(*dv.last)
                tt(khat[:, j, :], khat[:, j, :], mid[:, j % 2, :], ALU.mult).then_inc(dv.step(), 1)
            mixes(5, 5)
            for i in range(4):
                s = slice(2 * i, 2 * i + 2)
                dve.wait_ge(*evacuated(("kk_ss", i)))
                ts(bhat[:, s, :], bhat[:, s, :], 1e-12, None, ALU.max).then_inc(dv.step(), 1)
                dve.wait_ge(*dv.last)
                V.reciprocal(bhat[:, s, :], bhat[:, s, :]).then_inc(dv.step(), 1)
                dve.wait_ge(*dv.last)
                tt(KK[:, s, :], KK[:, s, :], bhat[:, s, :], ALU.mult).then_inc(dv.step(), 1)
                dve.wait_ge(*dv.last)
                tt(bhat[:, s, :], KK[:, s, :], AA[:, s, :], ALU.mult).then_inc(dv.step(), 1)
            dve.wait_ge(*evacuated(("r", 1, 1)))
            dve.wait_ge(*finished(("v", 1, 1)))
            for j in range(KT):
                ch = lambda a: a.rearrange("p (c t) -> p c t", c=NC_)
                ins = stt(ch(bonus_p[:, j, :]), AR[:, j, :, 1, :], par("rk")[:, j:j + 1], ch(khat[:, j, :]), ALU.mult, ALU.mult)
                ins.then_inc(dv.step("bonus_p" if j == KT - 1 else None), 1)
            dve.wait_ge(*dv.last)
            dve.wait_ge(sem("exps"), 3)
            for j in range(KT):
                tt(AR[:, j, :, 1, :], AR[:, j, :, 1, :], ch(EE[:, j, :]), ALU.mult).then_inc(dv.step(), 1)
                tt(AR[:, j, :, 0, :], ch(KK[:, j, :]), ch(LW[:, j, :]), ALU.mult).then_inc(dv.step(), 1)
            tt(bhat, bhat, EN, ALU.mult).then_inc(dv.step(), 1)
            tt(khat, khat, EN, ALU.mult).then_inc(dv.step("hats"), 1)
            dve.wait_ge(*finished("bonus"))
            V.tensor_copy(bonus, bank("bonus")[:, 0:32].rearrange("p (b h) -> p b h", b=TB)).then_inc(dv.frees("bonus"), 1)
            si = con("strict_incl").rearrange("p (o n) -> p o n", o=1).to_broadcast([P, 4, P])
            level = con("level").rearrange("p (l t) -> p l t", l=6)
            eye = con("eye").rearrange("p (o t) -> p o t", o=1).to_broadcast([P, 8, LC])
            for tb in range(TB):
                for hp in range(2):
                    for jg in range(2):
                        for name, dst in (("gk", PK), ("gb", PB)):
                            p = (name, tb, hp, jg)
                            dve.wait_ge(*finished(p))
                            d = dst[:, tb, hp, 4 * jg:4 * jg + 4, :, :].rearrange("p j a t -> p j (a t)")
                            tt(d, bank(p)[:, :].rearrange("p (j n) -> p j n", j=4), si, ALU.mult).then_inc(dv.frees(p), 1)
                        ada(2)
            dve.wait_ge(*dv.last)
            for g in range(4):
                tt(CT[:, g], PB[:, g // 2, g % 2, :, 0, :], level[:, 0:1, :].to_broadcast([P, 8, LC]), ALU.mult).then_inc(dv.step(), 1)
                dve.wait_ge(*dv.last)
                tt(TTI[:, g], eye, CT[:, g], ALU.subtract).then_inc(dv.step("tt"), 1)
            for l in range(1, 6):
                for g in range(4):
                    for name, dst in (("T", TI), ("TT", TTI)):
                        if (l, name) == (5, "T"):
                            continue
                        dve.wait_ge(*finished((name, l, g)))
                        tt(dst[:, g], dst[:, g], bank((name, l, g))[:, :].rearrange("p (j t) -> p j t", j=8),
                                      ALU.subtract).then_inc(dv.frees((name, l, g)), 1)
                    if (l, g) != (5, 3):
                        ada(4)

            def heads(a):
                return a.rearrange("p (h d) -> p h d", d=HD)

            def gate_and_bonus(tb):
                tmp, g = GNT[:, 0, :], Gr[:, tb, :]
                tt(heads(tmp), heads(Vr[:, tb, :]), bonus[:, tb, :].unsqueeze(2).to_broadcast([P, NH, HD]), ALU.mult).then_inc(dv.step(), 1)
                dve.wait_ge(*dv.last)
                tt(tmp, tmp, gn[:, 1, :], ALU.add).then_inc(dv.step(), 1)
                dve.wait_ge(*dv.last)
                tt(tmp, tmp, g, ALU.mult).then_inc(dv.step(), 1)
                dve.wait_ge(*dv.last)
                tt(g, g, gn[:, 0, :], ALU.mult).then_inc(dv.step(), 1)
                dve.wait_ge(*dv.last)

            def group_norm(tb):
                squares = ada_part.rearrange("p a n -> p (a n)")
                halves = [slice(hg * 512, (hg + 1) * 512) for hg in range(2)]
                wide = [P, NH // 2, HD]
                mean, var = ([a[:, tb, 8 * hg:8 * hg + 8] for hg in range(2)] for a in (stat, stat2))
                for hg, cs in enumerate(halves):
                    y, sq = Yr[:, tb, cs], squares[:, cs]
                    for q in range(2):
                        dve.wait_ge(*evacuated(("y", 2 * tb + q, hg)))
                    V.tensor_reduce(mean[hg], heads(y), AX.X, ALU.add).then_inc(dv.step(), 1)
                    dve.wait_ge(*dv.last)
                    ts(mean[hg], mean[hg], 1.0 / HD, None, ALU.mult).then_inc(dv.step(), 1)
                    dve.wait_ge(*dv.last)
                    tt(heads(y), heads(y), mean[hg].unsqueeze(2).to_broadcast(wide), ALU.subtract).then_inc(dv.step(), 1)
                    dve.wait_ge(*dv.last)
                    tt(sq, y, y, ALU.mult).then_inc(dv.step(), 1)
                    dve.wait_ge(*dv.last)
                    V.tensor_reduce(var[hg], heads(sq), AX.X, ALU.add).then_inc(dv.step(), 1)
                dve.wait_ge(*dv.last)
                rsqrt(stat2[:, tb, :], stat2[:, tb, :], 1.0 / HD, GN_EPS)
                for hg, cs in enumerate(halves):
                    y = Yr[:, tb, cs]
                    tt(heads(y), heads(y), var[hg].unsqueeze(2).to_broadcast(wide), ALU.mult).then_inc(dv.step(), 1)
                    dve.wait_ge(*dv.last)
                    tt(y, y, Gr[:, tb, cs], ALU.mult).then_inc(dv.step(), 1)
                    dve.wait_ge(*dv.last)
                    tt(y, y, GNT[:, 0, cs], ALU.add).then_inc(dv.step("y_gated"), 1)
                dve.wait_ge(*dv.last)

            for c in range(NC_):
                q = c % 2
                r = slice(q * LC, (q + 1) * LC)
                for hg in range(2):
                    p = ("R", c, hg)
                    dve.wait_ge(*finished(p))
                    V.tensor_copy(Rs[r, hg * 512:(hg + 1) * 512], bank(p)[r, :]).then_inc(dv.frees(p), 1)
                if c == 0:
                    ada(4)
                    dve.wait_ge(sem("state_zero"), 1)
                elif c == 1:
                    dve.wait_ge(sem("gn_rows"), 32)
                    gate_and_bonus(0)
                elif c == 2:
                    dve.wait_ge(*finished(("ada", 11)))
                    group_norm(0)
                else:
                    gate_and_bonus(1)
                if c < NC_ - 1:
                    for hg in range(2):
                        p = ("S", c, hg)
                        dve.wait_ge(*finished(p))
                        parts = []
                        for hp in range(2):
                            k = slice(hp * HD, (hp + 1) * HD)
                            js = slice(4 * hg, 4 * hg + 4)
                            st = SBD[k, js, hp * HD:(hp + 1) * HD]
                            ins = tt(st, st, bank(p)[k, :].rearrange("p (j v) -> p j v", j=4)[:, :, hp * HD:(hp + 1) * HD], ALU.add)
                            parts.append((st, F[k, js, c:c + 1].to_broadcast([HD, 4, HD])))
                            if hp == 0:
                                ins.then_inc(dv.step(), 1)
                        ins.then_inc(dv.frees(p), 1)
                        dve.wait_ge(*dv.last)
                        for hp, (st, f) in enumerate(parts):
                            tt(st, st, f, ALU.mult).then_inc(dv.step("state" if hp else None), 1)
            group_norm(1)
            split_output("wo_a", "yT", Y_PAGES)
            add_to_x("wo_a")

            norm()

            split(unit_of["k1", 0])
            split_h("hT_b", HKV_PAGES, HB_PAGES)
            for _ in range(6):
                next_unit(("k1", 0, 0))

            def head_norm(buf, w, n, nh, d, sq, between=None):
                b3 = buf.rearrange("p b (h d) -> p (b h) d", d=d)
                s3 = sq.rearrange("p b (h d) -> p (b h) d", d=d)
                st = stat.rearrange("p b h -> p (b h)")[:, 0:n * nh]
                tt(s3, b3, b3, ALU.mult).then_inc(dv.step(), 1)
                if between:
                    between()
                dve.wait_ge(*dv.last)
                V.tensor_reduce(st, s3, AX.X, ALU.add).then_inc(dv.step(), 1)
                if between:
                    between()
                dve.wait_ge(*dv.last)
                rsqrt(st, st, 1.0 / d, EPS)
                tt(b3, b3, st.unsqueeze(2).to_broadcast([P, n * nh, d]), ALU.mult).then_inc(dv.step(), 1)
                if between:
                    between()
                if w is not None:
                    dve.wait_ge(*dv.last)
                    tt(b3, b3, w.rearrange("p (o d) -> p o d", o=1).to_broadcast([P, n * nh, d]), ALU.mult).then_inc(dv.step(), 1)
                dve.wait_ge(*dv.last)

            def rope(x1, x2, cos, sin, t, to, out1=None, out2=None):
                tt(t[0], x1, cos, ALU.mult).then_inc(dv.step(), 1)
                tt(t[1], x2, sin, ALU.mult).then_inc(dv.step(), 1)
                tt(t[2], x2, cos, ALU.mult).then_inc(dv.step(), 1)
                tt(t[3], x1, sin, ALU.mult).then_inc(dv.step(), 1)
                dve.wait_ge(*dv.last)
                tt(out1 if out1 is not None else x1, t[0], t[1], ALU.subtract).then_inc(dv.step(), 1)
                tt(out2 if out2 is not None else x2, t[2], t[3], ALU.add).then_inc(dv.step(to), 1)

            r1 = con("rope1").rearrange("p (a b f) -> p a b f", a=2, b=TB)
            for buf, w, name in ((K1, "k_norm", "k1"), (Q1, "q_norm", "q1")):
                if name == "q1":
                    for _ in range(16):
                        next_unit(("k1", 0, 0))
                dve.wait_ge(*evacuated((name, 1, 1)))
                head_norm(buf, par(w), TB, NH, HD, page(5, TB), lambda: next_unit(("k1", 0, 0)))
                for tb in range(TB):
                    b3 = buf[:, tb, :].rearrange("p (h d) -> p h d", d=HD)
                    c8 = [r1[:, a, tb:tb + 1, :].to_broadcast([P, NH, 8]) for a in range(2)]
                    t = [arena[:, 5, a * 128:(a + 1) * 128].rearrange("p (h f) -> p h f", h=NH) for a in range(4)]
                    rope(b3[:, :, 0:8], b3[:, :, 8:16], c8[0], c8[1], t, name + "_rope" if tb else None)
                    dve.wait_ge(*dv.last)

            def attention(name, heads, dvd, scale, O, between=None):
                per = 512 // (TB * dvd)

                def gather(g):
                    p = (name, "O", g)
                    dve.wait_ge(*finished(p))
                    hs = slice(g * per, (g + 1) * per)
                    V.reciprocal(rs[:, hs, :], rs[:, hs, :]).then_inc(dv.step(), 1)
                    dve.wait_ge(*dv.last)
                    o = O[:, :, g * per * dvd:(g + 1) * per * dvd].rearrange("p b (h d) -> p h b d", d=dvd)
                    tt(o, bank(p)[:, :].rearrange("p (h b d) -> p h b d", h=per, b=TB),
                                  rs[:, hs, :].unsqueeze(3).to_broadcast([P, per, TB, dvd]), ALU.mult).then_inc(dv.frees(p), 1)

                done = 0
                for h in range(heads):
                    if h >= 2:
                        dve.wait_ge(sem(name + "_p"), h - 1)
                    dve.wait_ge(*finished((name, "S", h)))
                    tt(Ss[:, h % 2, :], bank((name, "S", h))[:, 0:3 * P], con("causal"), ALU.add).then_inc(dv.frees((name, "S", h)), 1)
                    dve.wait_ge(*dv.last)
                    V.tensor_reduce(mx[:, 0:1], Ss[:, h % 2, 0:P], AX.X, ALU.max).then_inc(dv.step(), 1)
                    V.tensor_reduce(mx[:, 1:2], Ss[:, h % 2, P:3 * P], AX.X, ALU.max).then_inc(dv.step(), 1)
                    dve.wait_ge(*dv.last)
                    ts(nmax[:, h, :], mx[:, 0:2], -scale, None, ALU.mult).then_inc(dv.step(name + "_max"), 1)
                    if (done + 1) * per <= h - 3:
                        gather(done)
                        done += 1
                    if between:
                        between()
                while done * per < heads:
                    gather(done)
                    done += 1

            attention("at1", NH, HD, 0.125, O1)
            dve.wait_ge(*evacuated(("g1", 1, 1)))
            dve.wait_ge(*dv.last)
            tt(O1, O1, G1, ALU.mult).then_inc(dv.step("o1"), 1)
            split_output("wo_b", "o1T", O1_PAGES)
            add_to_x("wo_b")

            def modulation(first, last, modulated):
                dve.wait_ge(*evacuated(("ada", last - 1)))
                columns = slice(4 * first, 4 * last)
                tt(ADA[:, columns], ADA[:, columns], par("ada_b")[:, columns], ALU.add).then_inc(dv.step(), 1)
                dve.wait_ge(*dv.last)
                for m in modulated:
                    at, g = MOD_FROM[m]
                    stt(MODS[m][0], ADA[:, at:at + 8], 1.0, g, ALU.add, ALU.mult).then_inc(dv.step("mod"), 1)

            modulation(0, 12, (0, 1))

            def gate_row(i):
                at, g = GATE_FROM[i]
                tt(gcol, ADA[:, at:at + 8], g, ALU.mult).then_inc(dv.step(), 1)
                dve.wait_ge(*dv.last)
                for j in range(KT):
                    ts(DIAG[:, j, :], ident, gcol[:, j:j + 1], None, ALU.mult).then_inc(dv.step("diag"), 1)
                for half in range(2):
                    dve.wait_ge(*finished(("gb", i, half)))
                    V.tensor_copy(GB[:, i % 2, half * 512:(half + 1) * 512], bank(("gb", i, half))[:, :]).then_inc(dv.frees(("gb", i, half)), 1)
                dve.wait_ge(*dv.last)

            def post_norm(i, products, to="x_new"):
                for half in range(2):
                    for tb in range(TB):
                        p, cs = products(half, tb), slice(half * 512, (half + 1) * 512)
                        dve.wait_ge(sem("y_sq"), 4 * i + 2 * half + tb + 1)
                        tt(Yb[:, tb, cs], bank(p)[:, :], GB[:, i % 2, cs], ALU.mult).then_inc(dv.frees(p), 1)
                tt(ss, y_sq[:, 0:4:2], y_sq[:, 1:4:2], ALU.add).then_inc(dv.step(), 1)
                dve.wait_ge(*dv.last)
                rsqrt(ss, ss, 1.0 / D, EPS)
                for half in range(2):
                    for tb in range(TB):
                        dve.wait_ge(*evacuated(products(half, tb)))
                for tb in range(TB):
                    stt(X[:, tb, :], Yb[:, tb, :], ss[:, tb:tb + 1], X[:, tb, :], ALU.mult, ALU.add).then_inc(dv.step(to), 1)
                dve.wait_ge(*dv.last)

            def mlp(l):
                first = unit_of["up", l, 0, 0]
                split(first)
                split_h(f"hT_m{l}", MLP_PAGES)
                split(first + AHEAD)
                for n in range(8):
                    for i in range(2):
                        split(ahead(("up", l, n, i)))
                        a, hi = (buf[:, n % 2, 2 * i:2 * i + 2, :] for buf in (AF, AF_HI.bitcast(F32)))
                        dve.wait_ge(sem("squared"), 2 * (8 * l + n) + i + 1)
                        tt(AF_LO[:, n % 2, 2 * i:2 * i + 2, :], a, hi, ALU.subtract).then_inc(dv.step("relu2"), 1)
                split(unit_of["mlp", l, 1, 1])

            gate_row(0)
            gate_row(1)
            norm()
            split(unit_of["q2", 0])
            split_h("hT_c", MLSTM_PAGES)
            for n in range(5):
                next_unit(("q2", 0))
                if n >= 3:
                    ada(KT // 2)
            dve.wait_ge(sem("gate_ln"), 1)
            stt(f_row[0:8, :], f_row[0:8, :], 0.0, t_row[0:8, :], ALU.min, ALU.subtract).then_inc(dv.step(), 1)
            dve.wait_ge(*dv.last)
            V.memset(ones_row[0:8, :], 1.0).then_inc(dv.step(), 1)
            dve.wait_ge(*dv.last)
            V.tensor_tensor_scan(b_row[0:8, :], ones_row[0:8, :], f_row[0:8, :], 0.0, ALU.mult, ALU.add).then_inc(dv.step(), 1)
            dve.wait_ge(*dv.last)
            tt(c_row[0:8, :], i_row[0:8, :], b_row[0:8, :], ALU.subtract).then_inc(dv.step(), 1)
            dve.wait_ge(*dv.last)
            V.tensor_tensor_scan(m_row[0:8, :], c_row[0:8, :], c_row[0:8, :], 0.0, ALU.max, ALU.max).then_inc(dv.step(), 1)
            dve.wait_ge(*dv.last)
            tt(mt_row[0:8, :], b_row[0:8, :], m_row[0:8, :], ALU.add).then_inc(dv.step("m_total"), 1)
            V.memset(V2[:, :, :, DV:DV + 1], 1.0).then_inc(dv.step(), 1)
            for n in range(6):
                next_unit(("q2", 0))
                if n in (1, 2):
                    ada(KT // 2)
            dve.wait_ge(*finished("gate_cols"))
            V.tensor_copy(gcols, bank("gate_cols")[:, 0:32].rearrange("p (b n) -> p b n", b=TB)).then_inc(dv.frees("gate_cols"), 1)
            dve.wait_ge(*dv.last)

            def gate_head(g):
                h, cs = H2[:, :, g * DV:(g + 1) * DV], slice(g * DV, (g + 1) * DV)
                dve.wait_ge(sem("h_sq"), 2 * g + 2)
                tt(h, h, G1[:, :, cs], ALU.mult).then_inc(dv.step(), 1)

            dve.wait_ge(*evacuated(("og", 1, 1)))

            def finish_head(g):
                if g:
                    gate_head(g - 1)
                p = ("num", g)
                dve.wait_ge(*finished(p))
                nd = bank(p)[:, 0:258].rearrange("p (b n) -> p b n", b=TB)
                dve.wait_ge(*dv.last)
                ts(den, nd[:, :, DV:DV + 1], -1.0, None, ALU.mult).then_inc(dv.step(), 1)
                dve.wait_ge(*dv.last)
                tt(den, den, nd[:, :, DV:DV + 1], ALU.max).then_inc(dv.step(), 1)
                dve.wait_ge(*dv.last)
                tt(den, den, gcols[:, :, 8 + g:9 + g], ALU.max).then_inc(dv.step(), 1)
                dve.wait_ge(*dv.last)
                V.reciprocal(den, den).then_inc(dv.step(), 1)
                dve.wait_ge(*dv.last)
                tt(H2[:, :, g * DV:(g + 1) * DV], nd[:, :, 0:DV], den.to_broadcast([P, TB, DV]), ALU.mult).then_inc(dv.frees(p), 1)

            for h in range(MH + 1):
                if h < MH:
                    p = ("m", h)
                    dve.wait_ge(*finished(p))
                    late = con("late")
                    w = W2[:, h % 2, :]
                    stt(w[:, 0:P], bank(p)[:, 0:P], gcols[:, 0, h:h + 1], late, ALU.subtract, ALU.max).then_inc(dv.step(), 1)
                    ts(w[:, P:T], bank(p)[:, P:T], gcols[:, 0, h:h + 1], 0.0, ALU.subtract, ALU.max).then_inc(dv.step(), 1)
                    stt(w[:, T:T + P], bank(p)[:, P:T], gcols[:, 1, h:h + 1], late, ALU.subtract, ALU.max).then_inc(dv.frees(p), 1)
                if h >= 1:
                    g = h - 1
                    p = ("qk", g)
                    dve.wait_ge(*finished(p))
                    dve.wait_ge(sem("wexp"), g + 1)
                    if g >= 2:
                        dve.wait_ge(*finished(("num", g - 2)))
                    stt(PT2[:, g % 2, :], bank(p)[:, 0:3 * P], DKM ** -0.5, W2[:, g % 2, :], ALU.mult, ALU.mult).then_inc(dv.frees(p), 1)
                    dve.wait_ge(*dv.last)
                    if g >= 1:
                        finish_head(g - 1)
                if h < MH:
                    ada(1)
            finish_head(MH - 1)
            dve.wait_ge(*dv.last)
            gate_head(MH - 1)
            dve.wait_ge(*dv.last)
            rsqrt(stat[:, 0, :], stat[:, 0, :], 1.0 / DV, EPS)
            for half in range(2):
                h = H2[:, :, half * 512:(half + 1) * 512].rearrange("p b (h d) -> p b h d", d=DV)
                tt(h, h, h_sq[:, :, 4 * half:4 * half + 4].unsqueeze(3).to_broadcast([P, TB, 4, DV]), ALU.mult).then_inc(dv.step("h2"), 1)
            split_output("wo_c", "h2T", H2_PAGES)
            ada(KT)
            split(unit_of["up", 0, 0, 0])
            post_norm(0, lambda half, tb: ("wo_c", half, tb))
            norm()
            mlp(0)
            post_norm(1, lambda half, tb: ("mlp", 0, tb, half))

            modulation(12, 22, (2, 3))
            gate_row(2)
            norm()
            sq = DIAGF
            dve.wait_ge(*evacuated(("cq", 1)))
            for tb in range(TB):
                dve.wait_ge(*dv.last)
                V.tensor_tensor_reduce(sq[:, 0:QL], CQ[:, tb, :], CQ[:, tb, :], 1.0, 0.0, ALU.mult,
                                              ALU.add, accum_out=ss[:, tb:tb + 1]).then_inc(dv.step(), 1)
            dve.wait_ge(*dv.last)
            rsqrt(ss, ss, 1.0 / QL, EPS)
            for tb in range(TB):
                ins = ts(CQ[:, tb, :], CQ[:, tb, :], ss[:, tb:tb + 1], None, ALU.mult)
                ins.then_inc(dv.step("cq_n" if tb else None), 1)
            dve.wait_ge(*evacuated(("ckv", 1)))
            for tb in range(TB):
                dve.wait_ge(*dv.last)
                V.tensor_tensor_reduce(sq[:, 0:KVL], CKVR[:, tb, 0:KVL], CKVR[:, tb, 0:KVL], 1.0, 0.0, ALU.mult,
                                              ALU.add, accum_out=ss[:, tb:tb + 1]).then_inc(dv.step(), 1)
            dve.wait_ge(*dv.last)
            rsqrt(ss, ss, 1.0 / KVL, EPS)
            for tb in range(TB):
                ts(CKV[:, tb, :], CKVR[:, tb, 0:KVL], ss[:, tb:tb + 1], None, ALU.mult).then_inc(dv.step(), 1)
            dve.wait_ge(sem("tables"), 2)
            cosb, sinb = rope2[:, 0], rope2[:, 1]
            t = [sq[:, 512 + a * 64:512 + (a + 1) * 64].rearrange("p (b f) -> p b f", b=TB) for a in range(4)]
            rope(CKVR[:, :, KVL:KVL + 32], CKVR[:, :, KVL + 32:KVL + 64], cosb, sinb, t, None, KR[:, :, 0:32], KR[:, :, 32:64])
            dve.wait_ge(*dv.last)
            V.tensor_copy(KR[:, :, 64:128], KR[:, :, 0:64]).then_inc(dv.step("ckv_n"), 1)
            dve.wait_ge(*evacuated(("qr", 1)))
            for tb in range(TB):
                b3 = QR[:, tb, :].rearrange("p (h d) -> p h d", d=RD)
                c32 = [rope2[:, a, tb:tb + 1, :].to_broadcast([P, MH, 32]) for a in range(2)]
                t = [sq[:, a * 256:(a + 1) * 256].rearrange("p (h f) -> p h f", h=MH) for a in range(4)]
                rope(b3[:, :, 0:32], b3[:, :, 32:64], c32[0], c32[1], t, "qr_rope" if tb else None)
                dve.wait_ge(*dv.last)
            ada(2 * KT)
            attention("at3", MH, DV, MLA_SCALE, O3, lambda: ada(2))
            modulation(22, 28, (4,))
            split_output("wo_d", "o3T", O3_PAGES)
            gate_row(3)
            split(unit_of["up", 1, 0, 0])
            post_norm(2, lambda half, tb: ("wo_d", half, tb))
            norm()
            mlp(1)
            post_norm(3, lambda half, tb: ("mlp", 1, tb, half), "final")
    return [name for name, _ in order]


def lay_out(order, w):
    def tiles(a, k=KT):
        n = a.shape[1]
        return a.reshape(k, P, n).transpose(1, 0, 2).reshape(P, k * n)

    wa, wi, wkv, wb = w["w_in_a"][0], w["a_w_in_2"][0], w["w_kv"], w["w_in_b"][0]
    ada = np.concatenate([w["ada_w_2"][0], w["kv_ada_w_2"], w["ada_w_2"][1]], 1)
    kvb = w["kv_w_b_2"].reshape(KVL, MH, 2 * DV)
    qb = w["b_w_q_b_2"][0].reshape(QL, MH, DV + RD)
    cut = {"k": wa[:, 1088:2112], "r": wa[:, 0:1024], "v": wa[:, 2112:3136], "g": wa[:, 3200:4224],
           "wo_a": w["w_out_a"][0], "k1": wkv[:, :D], "v1": wkv[:, D:], "q1": wb[:, :D], "g1": wb[:, D:],
           "wo_b": w["w_out_b"][0], "v2": wi[:, 1024:2048], "og": wi[:, 2064:3088], "wo_c": w["a_w_out_2"][0],
           "wo_d": w["b_w_out_2"][0], "ada": ada}
    out = np.zeros((len(order), P, SLOT), np.float32)
    for i, name in enumerate(order):
        if name == "lora":
            out[i, :, 0:512], out[i, :, 512:1024] = tiles(wa[:, 1024:1088]), tiles(wa[:, 3136:3200])
            out[i, 0:64, 1024:2048], out[i, 0:64, 2048:3072] = w["w2_a"][0], w["a2_a"][0]
        elif name in (("q2",), ("k2",)):
            out[i] = tiles(wi[:, 512 * (name == ("k2",)):][:, :512])
        elif name == "kv_a":
            out[i, :, 0:2560] = tiles(w["kv_w_a_2"])
            out[i, :, 2560:4096] = tiles(qb[:, :, DV:].reshape(QL, 512), 3)
        elif name == "q_a":
            out[i, :, 0:3072] = tiles(w["b_w_q_a_2"][0])
        elif name == "kv_b":
            for half in range(2):
                hs = slice(4 * half, 4 * half + 4)
                out[i, :, half * 1024:(half + 1) * 1024] = tiles(kvb[:, hs, :DV].reshape(KVL, 512), 2)
                out[i, :, 2048 + half * 1024:3072 + half * 1024] = tiles(kvb[:, hs, DV:].reshape(KVL, 512), 2)
        elif name == "q_b":
            for half in range(2):
                out[i, :, half * 1536:(half + 1) * 1536] = tiles(qb[:, 4 * half:4 * half + 4, :DV].reshape(QL, 512), 3)
        elif name[0] == "up":
            _, l, n = name
            out[i] = tiles(w["mlp_w1_2"][l][:, n * 512:(n + 1) * 512])
        elif name[0] == "w2":
            _, l, n = name
            out[i] = tiles(w["mlp_w2_2"][l][n * 512:(n + 1) * 512], 4)
        else:
            kind, n = name
            out[i] = tiles(cut[kind][:, n * 512:(n + 1) * 512])
    return out


def lay_out_parameters(w):
    out = np.zeros((P, NPARAM), np.float32)

    def put(name, a):
        at, n = PARAM[name]
        out[:a.shape[0], at:at + n] = a

    def col(a):
        return a.reshape(-1, P).T

    for name, key in (("norm_a", "norm_a"), ("mu", "mu_a"), ("w0", "w0_a"), ("a0", "a0_a"), ("kk", "kk_a"), ("ka", "ka_a"),
                      ("rk", "rk_a"), ("norm_kv", "norm_kv"), ("norm_b", "norm_b"), ("cond", "c_2"), ("norm2", "norm_g_2"),
                      ("kv_norm2", "kv_norm_g_2"), ("kv_latent", "kv_latent_g_2"), ("q_latent", "b_q_latent_g_2"),
                      ("head_g", "a_head_g_2")):
        put(name, col(w[key]))
    put("ada_b", col(np.concatenate([w["ada_b_2"][0], w["kv_ada_b_2"], w["ada_b_2"][1]])))
    put("gate_w", w["a_w_in_2"][0][:, 2048:2064].reshape(KT, P, 16).transpose(1, 0, 2).reshape(P, 128))
    put("gate_b", w["a_gate_b_2"][0].T)
    put("k_norm", np.broadcast_to(w["k_norm"], (P, HD)))
    put("q_norm", np.broadcast_to(w["q_norm_b"][0], (P, HD)))
    return out


PANELS = 95


def kernel(**inputs):
    import concourse.bacc as _bacc
    from concourse.bass_utils import run_bass_kernel_spmd as _run

    w = {k: np.asarray(v) for k, v in inputs.items()}
    nc = _bacc.Bacc("TRN2", target_bir_lowering=False, num_devices=1)
    arrays = {"x": w["x"], "consts": constants(), "params": lay_out_parameters(w),
              "positions": np.ascontiguousarray(w["positions_2"].reshape(TB, P).T),
              "gn": np.concatenate([w["gn_w_a"], w["gn_b_a"]]),
              "head_sel": np.ascontiguousarray(np.broadcast_to(np.eye(8, dtype=np.float32)[:, :, None], (8, 8, P)).reshape(8, 8 * P))}
    args = [nc.dram_tensor(f"in_{k}", a.shape, mybir.dt.from_np(a.dtype), kind="ExternalInput").ap()
            for k, a in arrays.items()]
    stream = nc.dram_tensor("in_stream", (PANELS, P, SLOT), F32, kind="ExternalInput").ap()
    out = nc.dram_tensor("out", (1, T, D), F32, kind="ExternalOutput").ap()
    order = build(nc, *args, stream, out)
    assert len(order) == PANELS
    feed = {f"in_{k}": a for k, a in arrays.items()}
    feed["in_stream"] = lay_out(order, w)
    r = _run(nc, [feed], core_ids=[0])
    return r.results[0]["out"]
```
